# Optimizing a Trainium2 kernel written in Bass

```python
import math
import jax
import jax.numpy as jnp
from jax import lax
import numpy as np

D_MODEL = 1024
BATCH = 1
SEQ = 256
DEPTH = 4

CHUNK = 64
N_MIXERS = 3
HEAD_DIM = 64
N_HEADS = D_MODEL // HEAD_DIM
D_FF = -(-8 * D_MODEL // (3 * 256)) * 256
RMS_EPS = 1e-6
ROPE_THETA = 10000.0
RW_DECAY_LORA = max(32, int(round(1.8 * D_MODEL ** 0.5 / 32)) * 32)
RW_AAA_LORA = max(32, int(round(1.8 * D_MODEL ** 0.5 / 32)) * 32)
RW_MV_LORA = max(32, int(round(1.3 * D_MODEL ** 0.5 / 32)) * 32)
RW_GATE_LORA = max(32, int(round(0.6 * D_MODEL ** 0.8 / 32)) * 32)
RW_GN_EPS = HEAD_DIM * 1e-5
SB_QBLOCK = 128
DS_TOPK_MAX = 256
DS_IDX_HEADS = 8
DS_IDX_DIM = 64
DS_QBLOCK = CHUNK
DS_IN_WIDTH = 3 * D_MODEL + DS_IDX_HEADS * DS_IDX_DIM + DS_IDX_DIM + DS_IDX_HEADS
N_RWKV = (DEPTH + 2) // 3
N_SB = (DEPTH + 1) // 3
N_DSA = DEPTH // 3


def rms_norm(x, g):
    xf = x.astype(jnp.float32)
    y = xf * lax.rsqrt(jnp.mean(xf * xf, axis=-1, keepdims=True) + RMS_EPS)
    return (y * g.astype(jnp.float32)).astype(x.dtype)

def rope(x, pos):
    half = x.shape[-1] // 2
    inv = 1.0 / (ROPE_THETA ** (jnp.arange(half, dtype=jnp.float32) / half))
    ang = pos.astype(jnp.float32)[:, None] * inv[None, :]
    cos = jnp.cos(ang)[None, :, None, :]
    sin = jnp.sin(ang)[None, :, None, :]
    xf = x.astype(jnp.float32)
    x1, x2 = xf[..., :half], xf[..., half:]
    return jnp.concatenate([x1 * cos - x2 * sin, x1 * sin + x2 * cos], axis=-1).astype(x.dtype)

def swiglu(h, w_gu, w_down):
    g, u = jnp.split(h @ w_gu, 2, axis=-1)
    return (jax.nn.silu(g) * u) @ w_down

def rwkv7_time_mix(h, v_first, mix, w_rkv, w0, w1, w2, a0, a1, a2, g1, g2, k_k, k_a, r_k, ln_w, ln_b, w_out, v_res):
    B, S, D = h.shape
    f32 = jnp.float32
    shifted = jnp.pad(h, ((0, 0), (1, 0), (0, 0)))[:, :-1]
    xm = h[:, :, None, :] + (shifted - h)[:, :, None, :] * mix
    rkv = jnp.einsum('bsjd,jde->bsje', xm[:, :, :3], w_rkv)
    r, k, v = rkv[:, :, 0], rkv[:, :, 1], rkv[:, :, 2]
    xv, xw, xa, xg = xm[:, :, 2], xm[:, :, 3], xm[:, :, 4], xm[:, :, 5]
    logw = -jax.nn.softplus(-(w0 + jnp.tanh(xw @ w1) @ w2).astype(f32)) - 0.5
    decay = jnp.exp(-jnp.exp(logw))
    a = jax.nn.sigmoid((a0 + (xa @ a1) @ a2).astype(f32))
    g = jax.nn.sigmoid(xg @ g1) @ g2
    v_layer = v
    if v_res is not None:
        v0, v1, v2 = v_res
        v = v + (v_first - v) * jax.nn.sigmoid(v0 + (xv @ v1) @ v2)

    def heads(t):
        return t.astype(f32).reshape(B, S, N_HEADS, HEAD_DIM)

    kk = heads(k * k_k)
    kk = kk * lax.rsqrt(jnp.maximum(jnp.sum(kk * kk, axis=-1, keepdims=True), 1e-24))
    k = k.astype(f32) * (1.0 + (a - 1.0) * k_a)
    rh, kh, vh, wh, ah = heads(r), heads(k), heads(v), heads(decay), heads(a)

    def step(state, inp):
        r_t, w_t, k_t, v_t, kk_t, a_t = inp
        sa = jnp.einsum('bhvk,bhk->bhv', state, kk_t)
        state = (state * w_t[:, :, None, :]
                 - sa[..., None] * (kk_t * a_t)[:, :, None, :]
                 + v_t[..., None] * k_t[:, :, None, :])
        return state, jnp.einsum('bhvk,bhk->bhv', state, r_t)

    def tmaj(t):
        return jnp.moveaxis(t, 1, 0)

    s0 = jnp.zeros((B, N_HEADS, HEAD_DIM, HEAD_DIM), f32)
    _, y = lax.scan(step, s0, (tmaj(rh), tmaj(wh), tmaj(kh), tmaj(vh), tmaj(kk), tmaj(ah)))
    y = jnp.moveaxis(y, 0, 1)
    mu = jnp.mean(y, axis=-1, keepdims=True)
    var = jnp.mean(jnp.square(y - mu), axis=-1, keepdims=True)
    y = ((y - mu) * lax.rsqrt(var + RW_GN_EPS)).reshape(B, S, D) * ln_w + ln_b
    y = y + (jnp.sum(rh * kh * r_k, axis=-1, keepdims=True) * vh).reshape(B, S, D)
    out = (y * g).astype(h.dtype) @ w_out
    return out, v_layer

def stick_breaking_attention(h, w_qkv, w_out):
    B, S, D = h.shape
    f32 = jnp.float32
    qkv = (h @ w_qkv).reshape(B, S, 3, N_HEADS, HEAD_DIM)
    q = qkv[:, :, 0].astype(f32) * HEAD_DIM ** -0.5
    k = qkv[:, :, 1].astype(f32)
    v = qkv[:, :, 2]
    nb = S // SB_QBLOCK
    q_blocks = jnp.moveaxis(q.reshape(B, nb, SB_QBLOCK, N_HEADS, HEAD_DIM), 1, 0)
    kpos = jnp.arange(S)

    def block(args):
        q_b, i = args
        qpos = i * SB_QBLOCK + jnp.arange(SB_QBLOCK)
        earlier = kpos[None, :] < qpos[:, None]
        z = jnp.einsum('bqhd,bshd->bhqs', q_b, k)
        log_1m = jnp.where(earlier, jax.nn.log_sigmoid(-z), 0.0)
        between = lax.cumsum(log_1m, axis=3, reverse=True) - log_1m
        att = jnp.where(earlier, jnp.exp(jax.nn.log_sigmoid(z) + between), 0.0)
        return jnp.einsum('bhqs,bshd->bqhd', att.astype(v.dtype), v)

    o = lax.map(block, (q_blocks, jnp.arange(nb)))
    o = jnp.moveaxis(o, 0, 1).reshape(B, S, D)
    return o @ w_out

def dsa_attention(h, w_in, q_norm, k_norm, w_out):
    B, S, D = h.shape
    f32 = jnp.float32
    pos = jnp.arange(S)
    c3 = 3 * D
    c4 = c3 + DS_IDX_HEADS * DS_IDX_DIM
    c5 = c4 + DS_IDX_DIM
    q, k, v, qi, ki, wi = jnp.split(h @ w_in, [D, 2 * D, c3, c4, c5], axis=-1)
    q = rope(rms_norm(q.reshape(B, S, N_HEADS, HEAD_DIM), q_norm), pos)
    k = rope(rms_norm(k.reshape(B, S, N_HEADS, HEAD_DIM), k_norm), pos)
    v = v.reshape(B, S, N_HEADS, HEAD_DIM)
    qi = rope(qi.reshape(B, S, DS_IDX_HEADS, DS_IDX_DIM), pos)
    ki = rope(ki.reshape(B, S, 1, DS_IDX_DIM), pos)[:, :, 0]
    wi = wi * (DS_IDX_HEADS ** -0.5 * DS_IDX_DIM ** -0.5)
    n_sel = min(DS_TOPK_MAX, S // 4)
    nb = S // DS_QBLOCK

    def blocks(t):
        return jnp.moveaxis(t.reshape(B, nb, DS_QBLOCK, *t.shape[2:]), 1, 0)

    kpos = jnp.arange(S)

    def block(args):
        q_b, qi_b, wi_b, i = args
        qpos = i * DS_QBLOCK + jnp.arange(DS_QBLOCK)
        visible = kpos[None, :] < ((qpos // CHUNK + 1) * CHUNK)[:, None]
        idx = jnp.einsum('bqhd,bsd->bqhs', qi_b, ki)
        score = jnp.einsum('bqh,bqhs->bqs', wi_b, jax.nn.relu(idx)).astype(f32)
        score = jnp.where(visible[None], score, -jnp.inf)
        top_val, top_idx = lax.top_k(score, n_sel)
        valid = top_val > -jnp.inf
        k_sel = jax.vmap(lambda kb, ib: kb[ib])(k, top_idx)
        v_sel = jax.vmap(lambda vb, ib: vb[ib])(v, top_idx)
        logits = jnp.einsum('bqhd,bqkhd->bhqk', q_b, k_sel).astype(f32) * HEAD_DIM ** -0.5
        logits = jnp.where(valid[:, None], logits, -jnp.inf)
        p = jax.nn.softmax(logits, axis=-1)
        return jnp.einsum('bhqk,bqkhd->bqhd', p.astype(v.dtype), v_sel)

    o = lax.map(block, (blocks(q), blocks(qi), blocks(wi), jnp.arange(nb)))
    o = jnp.moveaxis(o, 0, 1).reshape(B, S, D)
    return o @ w_out

def first_inputs(seed: int = 0) -> dict:
    key = jax.random.key(seed)
    ks = iter(jax.random.split(key, 64))
    D, F, H, dh = D_MODEL, D_FF, N_HEADS, HEAD_DIM
    nA, nB, nC = N_RWKV, N_SB, N_DSA
    out_scale = D ** -0.5 / math.sqrt(2 * DEPTH)

    def nrm(shape, scale):
        return jax.random.normal(next(ks), shape, jnp.float32) * scale

    def unif(shape, lo, hi):
        return jax.random.uniform(next(ks), shape, jnp.float32, lo, hi)

    return {
        'x': nrm((BATCH, SEQ, D), 1.0),
        'norm_mix': 1.0 + nrm((DEPTH, D), 0.02),
        'norm_ffn': 1.0 + nrm((DEPTH, D), 0.02),
        'ffn_w_gu': nrm((DEPTH, D, 2 * F), D ** -0.5),
        'ffn_w_down': nrm((DEPTH, F, D), F ** -0.5 / math.sqrt(2 * DEPTH)),
        'rw_mix': unif((nA, 6, D), 0.0, 1.0),
        'rw_w_rkv': nrm((nA, 3, D, D), D ** -0.5),
        'rw_w0': unif((nA, D), -5.0, 1.0),
        'rw_w1': nrm((nA, D, RW_DECAY_LORA), D ** -0.5),
        'rw_w2': nrm((nA, RW_DECAY_LORA, D), 0.1 * RW_DECAY_LORA ** -0.5),
        'rw_a0': nrm((nA, D), 0.1),
        'rw_a1': nrm((nA, D, RW_AAA_LORA), D ** -0.5),
        'rw_a2': nrm((nA, RW_AAA_LORA, D), 0.3 * RW_AAA_LORA ** -0.5),
        'rw_g1': nrm((nA, D, RW_GATE_LORA), D ** -0.5),
        'rw_g2': nrm((nA, RW_GATE_LORA, D), RW_GATE_LORA ** -0.5),
        'rw_v0': 1.0 + nrm((nA - 1, D), 0.1),
        'rw_v1': nrm((nA - 1, D, RW_MV_LORA), D ** -0.5),
        'rw_v2': nrm((nA - 1, RW_MV_LORA, D), 0.3 * RW_MV_LORA ** -0.5),
        'rw_k_k': 0.85 + nrm((nA, D), 0.05),
        'rw_k_a': 1.0 + nrm((nA, D), 0.05),
        'rw_r_k': nrm((nA, H, dh), 0.1),
        'rw_ln_w': 1.0 + nrm((nA, D), 0.02),
        'rw_ln_b': nrm((nA, D), 0.02),
        'rw_w_out': nrm((nA, D, D), out_scale),
        'sb_w_qkv': nrm((nB, D, 3 * D), D ** -0.5),
        'sb_w_out': nrm((nB, D, D), out_scale),
        'ds_w_in': nrm((nC, D, DS_IN_WIDTH), D ** -0.5),
        'ds_q_norm': 1.0 + nrm((nC, dh), 0.02),
        'ds_k_norm': 1.0 + nrm((nC, dh), 0.02),
        'ds_w_out': nrm((nC, D, D), out_scale),
    }

def first_block(x, norm_mix, norm_ffn, ffn_w_gu, ffn_w_down,
              rw_mix, rw_w_rkv, rw_w0, rw_w1, rw_w2, rw_a0, rw_a1, rw_a2, rw_g1, rw_g2,
              rw_v0, rw_v1, rw_v2, rw_k_k, rw_k_a, rw_r_k, rw_ln_w, rw_ln_b, rw_w_out,
              sb_w_qkv, sb_w_out,
              ds_w_in, ds_q_norm, ds_k_norm, ds_w_out):
    v_first = None
    for i in range(DEPTH):
        kind, j = i % N_MIXERS, i // N_MIXERS
        h = rms_norm(x, norm_mix[i])
        if kind == 0:
            v_res = None if j == 0 else (rw_v0[j - 1], rw_v1[j - 1], rw_v2[j - 1])
            y, v_layer = rwkv7_time_mix(h, v_first, rw_mix[j], rw_w_rkv[j], rw_w0[j], rw_w1[j], rw_w2[j],
                                        rw_a0[j], rw_a1[j], rw_a2[j], rw_g1[j], rw_g2[j],
                                        rw_k_k[j], rw_k_a[j], rw_r_k[j], rw_ln_w[j], rw_ln_b[j],
                                        rw_w_out[j], v_res)
            if j == 0:
                v_first = v_layer
        elif kind == 1:
            y = stick_breaking_attention(h, sb_w_qkv[j], sb_w_out[j])
        else:
            y = dsa_attention(h, ds_w_in[j], ds_q_norm[j], ds_k_norm[j], ds_w_out[j])
        x = x + y
        x = x + swiglu(rms_norm(x, norm_ffn[i]), ffn_w_gu[i], ffn_w_down[i])
    return x


DEPTH_2 = 2

GRID_W = 64
CTX_LEN = 256
EPS = 1e-6
N_MOD = 9
D_FF_2 = 2816

CONV_A_W = 256
CONV_A_K = 3
SGU_W = 256
SGU_GROUPS = 4
SGU_GROUP_W = SGU_W // SGU_GROUPS
CHUNK_2 = 128
DA_HEADS = 4
DA_HEAD_DIM = 64
DA_W = DA_HEADS * 2 * DA_HEAD_DIM
ROPE_BASE = 10000.0
ROPE_NF = DA_HEAD_DIM // 4
Q_BLOCK = 128
CONF_W = 256
CONF_K = 31
N_BRANCH = 4

A_OFF = 0
B_OFF = A_OFF + 3 * CONV_A_W
Q_OFF = B_OFF + 2 * SGU_W
K_OFF = Q_OFF + DA_W
V_OFF = K_OFF + DA_W
D_OFF = V_OFF + DA_W
G_OFF = D_OFF + 2 * CONF_W
IN_COLS = G_OFF + N_BRANCH * D_MODEL


def rmsnorm(x, g):
    xf = x.astype(jnp.float32)
    y = xf * lax.rsqrt(jnp.mean(xf * xf, axis=-1, keepdims=True) + EPS)
    return (y * g.astype(jnp.float32)).astype(x.dtype)

def layernorm_plain(x):
    xf = x.astype(jnp.float32)
    mu = jnp.mean(xf, axis=-1, keepdims=True)
    var = jnp.mean(jnp.square(xf - mu), axis=-1, keepdims=True)
    return ((xf - mu) * lax.rsqrt(var + EPS)).astype(x.dtype)

def layernorm_affine(x, g, b):
    return (layernorm_plain(x) * g + b).astype(x.dtype)

def modulated_norm(x, g, shift, scale):
    return rmsnorm(x, g) * (1 + scale) + shift

def swiglu_2(h, w1, w3, w2):
    return (jax.nn.silu(h @ w1) * (h @ w3)) @ w2

def dwconv_centred(x, w):
    k = w.shape[0]
    return lax.conv_general_dilated(
        x, w[:, None, :].astype(x.dtype), window_strides=(1,),
        padding=[(k // 2, k // 2)], dimension_numbers=("NWC", "WIO", "NWC"),
        feature_group_count=x.shape[-1])

def axial_rope_tables(n_tokens):
    n_rows = n_tokens // GRID_W
    row = jnp.repeat(jnp.arange(n_rows, dtype=jnp.float32), GRID_W)
    col = jnp.tile(jnp.arange(GRID_W, dtype=jnp.float32), n_rows)
    inv = ROPE_BASE ** (-jnp.arange(ROPE_NF, dtype=jnp.float32) / ROPE_NF)
    ang = jnp.stack([row[:, None] * inv, col[:, None] * inv], axis=1)
    ang = ang[:, None, None]
    return jnp.cos(ang), jnp.sin(ang)

def apply_rope(x, cos, sin):
    xs = x.reshape(x.shape[:-1] + (2, 2, ROPE_NF))
    x1, x2 = xs[..., 0, :], xs[..., 1, :]
    cos, sin = cos.astype(x.dtype), sin.astype(x.dtype)
    out = jnp.stack([x1 * cos - x2 * sin, x2 * cos + x1 * sin], axis=-2)
    return out.reshape(x.shape)

def heads_qk(p):
    return p.reshape(p.shape[:2] + (DA_HEADS, 2, DA_HEAD_DIM))

def heads_v(p):
    return p.reshape(p.shape[:2] + (DA_HEADS, 2 * DA_HEAD_DIM))

def diff_attend(q, k, v, lam):
    s = jnp.einsum("bqhmd,bkhmd->bmhqk", q, k).astype(jnp.float32) * (DA_HEAD_DIM ** -0.5)
    p = jax.nn.softmax(s, axis=-1)
    a = p[:, 0] - lam * p[:, 1]
    return jnp.einsum("bhqk,bkhe->bqhe", a.astype(v.dtype), v)

def diff_attn_out(o, subln_g, lam_init, w_c_out):
    o = rmsnorm(o, subln_g) * (1 - lam_init)
    return o.reshape(o.shape[:2] + (DA_W,)) @ w_c_out

def short_conv_branch(p, conv_w, w_out):
    bg, cg, xin = jnp.split(p[..., A_OFF:B_OFF], 3, axis=-1)
    return (bg * dwconv_centred(cg * xin, conv_w)) @ w_out

def sgu_branch(p, w_s, b_s, w_out):
    z = jax.nn.gelu(p[..., B_OFF:Q_OFF])
    u, v = jnp.split(z, 2, axis=-1)
    v = layernorm_plain(v)
    bsz, t = v.shape[:2]
    vc = v.reshape(bsz, t // CHUNK_2, CHUNK_2, SGU_GROUPS, SGU_GROUP_W)
    s = jnp.einsum("gpq,bnqgc->bnpgc", w_s, vc) + b_s.T[:, :, None]
    return (u * s.reshape(bsz, t, SGU_W)) @ w_out

def conformer_conv_branch(p, dw, db, ln_g, ln_b, w_out):
    z = p[..., D_OFF:G_OFF]
    h = z[..., :CONF_W] * jax.nn.sigmoid(z[..., CONF_W:])
    h = dwconv_centred(h, dw) + db
    h = jax.nn.silu(layernorm_affine(h, ln_g, ln_b))
    return h @ w_out

def mix_stream(p, yc, conv_a_w, w_a_out, sgu_w, sgu_b, w_b_out,
               conf_dw, conf_db, conf_ln_g, conf_ln_b, w_d_out, w_o):
    ya = short_conv_branch(p, conv_a_w, w_a_out)
    yb = sgu_branch(p, sgu_w, sgu_b, w_b_out)
    yd = conformer_conv_branch(p, conf_dw, conf_db, conf_ln_g, conf_ln_b, w_d_out)
    g = jax.nn.sigmoid(p[..., G_OFF:]).reshape(p.shape[:2] + (N_BRANCH, D_MODEL))
    merged = g[:, :, 0] * ya + g[:, :, 1] * yb + g[:, :, 2] * yc + g[:, :, 3] * yd
    return merged @ w_o

def second_inputs(seed: int = 0) -> dict:
    key = jax.random.key(seed)
    ks = iter(jax.random.split(key, 32))

    def nrm(shape, scale):
        return scale * jax.random.normal(next(ks), shape, jnp.float32)

    L, D = DEPTH_2, D_MODEL
    return {
        "x": nrm((BATCH, SEQ, D), 1.0),
        "c": nrm((BATCH, D), 1.0),
        "ctx": nrm((BATCH, CTX_LEN, D), 1.0),
        "c_ctx": nrm((D,), 1.0),
        "w_ada": nrm((L, D, N_MOD * D), 0.5 * D ** -0.5),
        "b_ada": nrm((L, N_MOD * D), 0.02),
        "norm_g": 1.0 + nrm((L, 3, D), 0.02),
        "ffn1_w1": nrm((L, D, D_FF_2), D ** -0.5),
        "ffn1_w3": nrm((L, D, D_FF_2), D ** -0.5),
        "ffn1_w2": nrm((L, D_FF_2, D), D_FF_2 ** -0.5),
        "ffn2_w1": nrm((L, D, D_FF_2), D ** -0.5),
        "ffn2_w3": nrm((L, D, D_FF_2), D ** -0.5),
        "ffn2_w2": nrm((L, D_FF_2, D), D_FF_2 ** -0.5),
        "w_in": nrm((L, D, IN_COLS), D ** -0.5),
        "conv_a_w": nrm((L, CONV_A_K, CONV_A_W), CONV_A_K ** -0.5),
        "w_a_out": nrm((L, CONV_A_W, D), CONV_A_W ** -0.5),
        "sgu_w": nrm((L, SGU_GROUPS, CHUNK_2, CHUNK_2), CHUNK_2 ** -0.5),
        "sgu_b": nrm((L, SGU_GROUPS, CHUNK_2), 0.02),
        "w_b_out": nrm((L, SGU_W, D), SGU_W ** -0.5),
        "lam_p": nrm((L, 4, DA_HEAD_DIM), 0.1),
        "subln_g": 1.0 + nrm((L, 2 * DA_HEAD_DIM), 0.02),
        "w_c_out": nrm((L, DA_W, D), DA_W ** -0.5),
        "conf_dw": nrm((L, CONF_K, CONF_W), CONF_K ** -0.5),
        "conf_db": nrm((L, CONF_W), 0.02),
        "conf_ln_g": 1.0 + nrm((L, CONF_W), 0.02),
        "conf_ln_b": nrm((L, CONF_W), 0.02),
        "w_d_out": nrm((L, CONF_W, D), CONF_W ** -0.5),
        "w_o": nrm((L, D, D), D ** -0.5),
        "final_g": 1.0 + nrm((D,), 0.02),
    }

def second_block(x, c, ctx, c_ctx, w_ada, b_ada, norm_g, ffn1_w1, ffn1_w3, ffn1_w2,
              ffn2_w1, ffn2_w3, ffn2_w2, w_in, conv_a_w, w_a_out, sgu_w, sgu_b,
              w_b_out, lam_p, subln_g, w_c_out, conf_dw, conf_db, conf_ln_g,
              conf_ln_b, w_d_out, w_o, final_g):
    bsz, n_tok = x.shape[:2]
    n_blk = n_tok // Q_BLOCK
    cos, sin = axial_rope_tables(n_tok)
    sc = jax.nn.silu(c)[:, None, :]
    scc = jax.nn.silu(c_ctx)[None, None, :]
    for l in range(DEPTH_2):
        last = l == DEPTH_2 - 1
        mx = jnp.split(sc @ w_ada[l] + b_ada[l], N_MOD, axis=-1)
        mc = jnp.split(scc @ w_ada[l] + b_ada[l], N_MOD, axis=-1)
        lam_init = 0.8 - 0.6 * float(np.exp(-0.3 * l))
        lp = lam_p[l].astype(jnp.float32)
        lam = jnp.exp(jnp.sum(lp[0] * lp[1])) - jnp.exp(jnp.sum(lp[2] * lp[3])) + lam_init
        ffn1 = (ffn1_w1[l], ffn1_w3[l], ffn1_w2[l])
        ffn2 = (ffn2_w1[l], ffn2_w3[l], ffn2_w2[l])
        lw = (conv_a_w[l], w_a_out[l], sgu_w[l], sgu_b[l], w_b_out[l],
              conf_dw[l], conf_db[l], conf_ln_g[l], conf_ln_b[l], w_d_out[l], w_o[l])

        x = x + 0.5 * mx[2] * swiglu_2(modulated_norm(x, norm_g[l, 0], mx[0], mx[1]), *ffn1)
        ctx = ctx + 0.5 * mc[2] * swiglu_2(modulated_norm(ctx, norm_g[l, 0], mc[0], mc[1]), *ffn1)

        hx = modulated_norm(x, norm_g[l, 1], mx[3], mx[4])
        hc = modulated_norm(ctx, norm_g[l, 1], mc[3], mc[4])
        px = hx @ w_in[l]
        if last:
            pc_kv = hc @ w_in[l][:, K_OFF:D_OFF]
            kc, vc = heads_qk(pc_kv[..., :DA_W]), heads_v(pc_kv[..., DA_W:])
        else:
            pc = hc @ w_in[l]
            qc = heads_qk(pc[..., Q_OFF:K_OFF])
            kc = heads_qk(pc[..., K_OFF:V_OFF])
            vc = heads_v(pc[..., V_OFF:D_OFF])
        qx = apply_rope(heads_qk(px[..., Q_OFF:K_OFF]), cos, sin)
        kx = apply_rope(heads_qk(px[..., K_OFF:V_OFF]), cos, sin)
        vx = heads_v(px[..., V_OFF:D_OFF])
        k_all = jnp.concatenate([kx, kc], axis=1)
        v_all = jnp.concatenate([vx, vc], axis=1)
        qb = jnp.moveaxis(qx.reshape((bsz, n_blk, Q_BLOCK) + qx.shape[2:]), 1, 0)
        ob = lax.map(lambda qi: diff_attend(qi, k_all, v_all, lam), qb)
        ox = jnp.moveaxis(ob, 0, 1).reshape((bsz, n_tok) + ob.shape[3:])
        yc_x = diff_attn_out(ox, subln_g[l], lam_init, w_c_out[l])
        x = x + mx[5] * mix_stream(px, yc_x, *lw)

        x = x + 0.5 * mx[8] * swiglu_2(modulated_norm(x, norm_g[l, 2], mx[6], mx[7]), *ffn2)

        if not last:
            oc = diff_attend(qc, kc, vc, lam)
            yc_c = diff_attn_out(oc, subln_g[l], lam_init, w_c_out[l])
            ctx = ctx + mc[5] * mix_stream(pc, yc_c, *lw)
            ctx = ctx + 0.5 * mc[8] * swiglu_2(modulated_norm(ctx, norm_g[l, 2], mc[6], mc[7]), *ffn2)

    return rmsnorm(x, final_g)


def setup_inputs(seed=0):
    out = dict(first_inputs(seed))
    for name, value in second_inputs(seed + 1).items():
        if name != "x":
            out[name + "_2"] = value
    return out


def reference(
    x, norm_mix, norm_ffn, ffn_w_gu, ffn_w_down, rw_mix, rw_w_rkv, rw_w0, rw_w1, rw_w2, rw_a0,
    rw_a1, rw_a2, rw_g1, rw_g2, rw_v0, rw_v1, rw_v2, rw_k_k, rw_k_a, rw_r_k, rw_ln_w, rw_ln_b,
    rw_w_out, sb_w_qkv, sb_w_out, ds_w_in, ds_q_norm, ds_k_norm, ds_w_out, c_2, ctx_2, c_ctx_2,
    w_ada_2, b_ada_2, norm_g_2, ffn1_w1_2, ffn1_w3_2, ffn1_w2_2, ffn2_w1_2, ffn2_w3_2,
    ffn2_w2_2, w_in_2, conv_a_w_2, w_a_out_2, sgu_w_2, sgu_b_2, w_b_out_2, lam_p_2, subln_g_2,
    w_c_out_2, conf_dw_2, conf_db_2, conf_ln_g_2, conf_ln_b_2, w_d_out_2, w_o_2, final_g_2,
):
    x = first_block(
        x, norm_mix, norm_ffn, ffn_w_gu, ffn_w_down, rw_mix, rw_w_rkv, rw_w0, rw_w1, rw_w2,
        rw_a0, rw_a1, rw_a2, rw_g1, rw_g2, rw_v0, rw_v1, rw_v2, rw_k_k, rw_k_a, rw_r_k, rw_ln_w,
        rw_ln_b, rw_w_out, sb_w_qkv, sb_w_out, ds_w_in, ds_q_norm, ds_k_norm, ds_w_out,
    )
    return second_block(
        x, c_2, ctx_2, c_ctx_2, w_ada_2, b_ada_2, norm_g_2, ffn1_w1_2, ffn1_w3_2, ffn1_w2_2,
        ffn2_w1_2, ffn2_w3_2, ffn2_w2_2, w_in_2, conv_a_w_2, w_a_out_2, sgu_w_2, sgu_b_2,
        w_b_out_2, lam_p_2, subln_g_2, w_c_out_2, conf_dw_2, conf_db_2, conf_ln_g_2,
        conf_ln_b_2, w_d_out_2, w_o_2, final_g_2,
    )


_drawn_inputs = setup_inputs


def setup_inputs(seed=0):
    import zlib

    import numpy as np

    out = dict(_drawn_inputs(seed))
    spreads = {}
    factors = {'norm_mix': 3.098,
     'norm_ffn': 3.861,
     'rw_w1': 8.0,
     'rw_w2': 8.0,
     'rw_a0': 3.478,
     'rw_v0': 8.0,
     'rw_v1': 3.573,
     'rw_v2': 3.525,
     'rw_k_k': 5.325,
     'rw_k_a': 3.224,
     'rw_ln_w': 7.197,
     'rw_ln_b': 7.513,
     'ds_q_norm': 8.0,
     'ds_k_norm': 8.0,
     'norm_g_2': 4.588,
     'sgu_b_2': 56.1,
     'lam_p_2': 3.077,
     'subln_g_2': 200.0,
     'conf_db_2': 64.0,
     'conf_ln_g_2': 200.0,
     'conf_ln_b_2': 200.0,
     'final_g_2': 23.686}
    for name, (base, spread) in spreads.items():
        noise = np.random.default_rng([zlib.crc32(name.encode()), seed]).standard_normal(out[name].shape)
        drawn = base * np.exp(spread * noise) if base else spread * noise
        out[name] = jnp.asarray(drawn.astype(out[name].dtype))
    for name, factor in factors.items():
        out[name] = (out[name] * factor).astype(out[name].dtype)
    return out
```

```python
from contextlib import ExitStack, contextmanager

import numpy as np

import concourse.bass as bass
import concourse.mybir as mybir

F32 = mybir.dt.float32
F32R = mybir.dt.float32r
ACT = mybir.ActivationFunctionType
ALU = mybir.AluOpType
AX_X = mybir.AxisListType.X

P = 128
S = 256
TT = S // P
D = 1024
C = D // P
H = 16
DH = 64
DEPTH = 4
F = 2816
FC = F // P
CHUNK = 64
NCH = S // CHUNK
L_W, L_A, L_G, L_V = 64, 64, 160, 32
IDX_H = 8
TOPK = S // 4
EPS = 1e-6
GN_EPS = DH * 1e-5
DECAY = float(np.exp(np.float64(-0.5)))
NEG = -3.0e38
TAKEN = -3.2e38
HIDE = -1.0e30

RING = 4
KPAN = 8

D2 = 2
N_MOD = 9
CA_W, CA_K = 256, 3
SG_W, SG_G = 256, 4
DA_H, DA_D = 4, 64
DA_W = DA_H * 2 * DA_D
CF_W, CF_K = 256, 31
N_BR = 4
A_OFF = 0
B_OFF = A_OFF + 3 * CA_W
Q_OFF = B_OFF + 2 * SG_W
K_OFF = Q_OFF + DA_W
V_OFF = K_OFF + DA_W
D_OFF = V_OFF + DA_W
G_OFF = D_OFF + 2 * CF_W


def name_of(eng):
    return str(eng.engine).split(".")[-1]


class Counts:

    def __init__(self):
        self.seen = {}
        self.turns = {}

    def at(self, eng, sem):
        return self.seen.get((sem, name_of(eng)), 0)

    def start(self, eng, sem, value):
        self.seen[sem, name_of(eng)] = value

    def after(self, eng, sem, n=1):
        have = self.at(eng, sem) + n
        self.start(eng, sem, have)
        if (sem, name_of(eng)) in self.turns:
            i, per = self.turns[sem, name_of(eng)]
            assert have > 0
            return i * per + have
        return have if have > 0 else None

    @contextmanager
    def repeat(self, eng, n, per):
        with eng.Fori(0, n) as i:
            at = {sem: self.at(eng, sem) for sem in per}
            for sem, k in per.items():
                self.turns[sem, name_of(eng)] = (i, k)
            yield i
        for sem, k in per.items():
            assert self.at(eng, sem) == at[sem] + k
            self.start(eng, sem, at[sem] + n * k)
            del self.turns[sem, name_of(eng)]


class Projection:

    def __init__(self, name, steps, panels, tokens_out=False):
        self.name, self.steps, self.panels = name, steps, panels
        self.tokens_out = tokens_out
        self.pps = len(panels)
        self.tiles = 1 + max(p[4] for p in panels)
        self.body = RING // self.tiles
        self.n_panels = steps * self.pps
        self.n_tiles = steps * self.tiles


def dense(name, w, col, n_out, operand, kc=C, tokens_out=False):
    groups = [(k0, min(KPAN, kc - k0)) for k0 in range(0, kc, KPAN)]
    return Projection(name, n_out // P, [(w, col, k0, nk, 0, operand) for k0, nk in groups], tokens_out)


def pair(name, w_a, col_a, kc_a, w_b, col_b, kc_b, n_out, operand_a, operand_b):
    return Projection(name, n_out // P, [(w_a, col_a, 0, kc_a, 0, operand_a), (w_b, col_b, 0, kc_b, 1, operand_b)])


def constants():
    p = np.arange(P)[:, None]
    f = np.arange(P)[None, :]
    t = np.arange(S)[None, :]
    parts = {}
    parts["ident"] = p == f
    parts["headones"] = p // DH == f // DH
    half = DH // 2
    rot = np.zeros((P, P))
    for m in range(P):
        if m % DH < half:
            rot[m + half, m] = -1.0
        else:
            rot[m - half, m] = 1.0
    parts["rot_head"] = rot
    nf = DA_D // 4
    rot = np.zeros((P, P))
    for m in range(P):
        if m % (2 * nf) < nf:
            rot[m + nf, m] = -1.0
        else:
            rot[m - nf, m] = 1.0
    parts["rot_axial"] = rot
    inv = (1.0 / (np.float32(10000.0) ** (np.arange(half, dtype=np.float32) / np.float32(half)))).astype(np.float32)
    ang = (np.arange(S, dtype=np.float32)[None, :] * inv[np.arange(P) % half][:, None]).astype(np.float32)
    parts["cos_head"], parts["sin_head"] = np.cos(ang), np.sin(ang)
    inv = (np.float32(10000.0) ** (-np.arange(nf, dtype=np.float32) / np.float32(nf))).astype(np.float32)
    grid = np.stack([np.arange(S) // 64, np.arange(S) % 64]).astype(np.float32)
    d = np.arange(P) % DA_D
    ang = (grid[d // (2 * nf)] * inv[d % nf][:, None]).astype(np.float32)
    parts["cos_axial"], parts["sin_axial"] = np.cos(ang), np.sin(ang)
    parts["earlier"] = np.concatenate([(st * P + p) < t for st in range(TT)], axis=1)
    parts["after"] = p > f
    j, i = np.arange(P)[:, None] % CHUNK, np.arange(CHUNK)[None, :]
    parts["before"] = j < i
    parts["upto"] = j <= i
    parts["below"] = j > i
    for lv in range(6):
        b = 2 ** lv
        parts[f"upper{lv}"] = ((j // b) % 2 == 0) & (i // b == j // b + 1)
        parts[f"lower{lv}"] = ((i // b) % 2 == 0) & (j // b == i // b + 1)
    parts["eye64"] = j == i
    parts["carry"] = np.broadcast_to(t % CHUNK != 0, (P, S))
    at, cols, n = {}, [], 0
    for name, a in parts.items():
        a = np.asarray(a, np.float32)
        at[name] = (n, a.shape[1])
        cols.append(a)
        n += a.shape[1]
    return np.ascontiguousarray(np.concatenate(cols, axis=1)), at


def vector_rows():
    rows, at, n = [], {}, 0
    for name, k in (("norm_mix", DEPTH), ("norm_ffn", DEPTH), ("rw_mix", 12), ("rw_w0", 2), ("rw_a0", 2),
                    ("rw_k_k", 2), ("rw_k_a", 2), ("rw_r_k", 2), ("rw_ln_w", 2), ("rw_ln_b", 2), ("rw_v0", 1),
                    ("norm_g_2", 3 * D2), ("b_ada_2", N_MOD * D2), ("c_2", 1), ("c_ctx_2", 1), ("final_g_2", 1)):
        at[name] = n
        rows.append((name, n, k))
        n += k
    return rows, at, n


def vector_rows_256():
    rows, at, n = [], {}, 0
    for name, k in (("conv_a_w_2", CA_K * D2), ("conf_dw_2", CF_K * D2), ("conf_db_2", D2),
                    ("conf_ln_g_2", D2), ("conf_ln_b_2", D2)):
        at[name] = n
        rows.append((name, n, k))
        n += k
    return rows, at, n


def build(nc, a, out, CONST_AT):
    VEC_ROWS, VAT, NV = vector_rows()
    VEC2_ROWS, V2AT, NV2 = vector_rows_256()
    with ExitStack() as ctx:
        place = [-(-nc.sbuf_base // 64) * 64]

        def sb(name, cols, dt=F32, at=None):
            off = place[0] if at is None else at
            t = nc.alloc_sbuf_tensor_at(name, [P, cols], dt, offset=off)
            if at is None:
                place[0] += -(-cols * 4 // 64) * 64
            return t

        def sem(name):
            return ctx.enter_context(nc.semaphore(name))

        def v3(t, n=S):
            return t[:, :].rearrange("p (c t) -> p c t", t=n)

        SLOT = KPAN * P
        raw = [sb(f"raw{i}", SLOT) for i in range(RING)]
        whi = [sb(f"whi{i}", SLOT, F32R) for i in range(RING)]
        wlo = [sb(f"wlo{i}", SLOT, F32R) for i in range(RING)]
        X = sb("X", C * S)
        CTX = sb("CTX", C * S)
        a_at = place[0]
        AH, AL = sb("AH", C * S, F32R), sb("AL", C * S, F32R)
        cst = sb("cst", sum(n for _, n in CONST_AT.values()))
        VEC = sb("VEC", C * NV)
        VEC2 = sb("VEC2", 2 * NV2)
        VEC3 = sb("VEC3", 12)
        ones = sb("ones", P)
        eps = sb("eps", 2)
        STD = sb("STD", S)
        RSTD = sb("RSTD", S)
        silu = [sb(f"silu{i}", S) for i in range(2)]
        hid = sb("hid", S)
        w_at = []
        W = []
        for i in range(9):
            w_at.append(place[0])
            W.append(sb(f"W{i}", C * S))
        HH = sb("HH", FC * S, F32R, at=w_at[0])
        HL = sb("HL", FC * S, F32R, at=w_at[0] + FC * S * 4)
        VF = sb("VF", C * S)
        l_at = place[0]
        lw1, la1, lg1, lv1 = sb("lw1", C * L_W), sb("la1", C * L_A), sb("lg1", C * L_G), sb("lv1", C * L_V)
        lwa2 = sb("lwa2", D)
        lg2 = sb("lg2", D)
        lgv2 = sb("lgv2", D)
        BRH, BRL = sb("BRH", 10 * S, F32R, at=l_at), sb("BRL", 10 * S, F32R, at=l_at + 10 * S * 4)
        COND_T = (sb("cond_hi", 2 * C, F32R), sb("cond_lo", 2 * C, F32R))
        assert place[0] <= nc.sbuf_usable_end, (place[0], nc.sbuf_usable_end)
        bank = [ctx.enter_context(nc.psum_tensor(f"bank{i}", [P, 512], F32)) for i in range(8)]

        def const(name):
            o, n = CONST_AT[name]
            return cst[:, o:o + n]

        VEC_v, VEC2_v = v3(VEC, NV), v3(VEC2, NV2)

        def vec(name, row, c):
            return VEC_v[:, c, VAT[name] + row:VAT[name] + row + 1]

        def vec_b(name, row):
            return VEC_v[:, :, VAT[name] + row:VAT[name] + row + 1].to_broadcast([P, C, S])

        counts = Counts()
        after, repeat = counts.after, counts.repeat

        const_landed = sem("const_landed")
        rows_landed = sem("rows_landed")
        x_rows_landed = sem("x_rows_landed")
        lora_landed = sem("lora_landed")
        raw_landed = [sem(f"raw_landed{i}") for i in range(RING)]
        hi_ready = sem("hi_ready")
        lo_ready = sem("lo_ready")
        panels_done = sem("panels_done")
        bank_free = sem("bank_free")
        operand_ready = sem("operand_ready")
        consts_set = sem("consts_set")
        vec_turned = sem("vec_turned")
        vec_ready = sem("vec_ready")
        x_turned = sem("x_turned")
        x_ready = sem("x_ready")
        squares_ready = sem("squares_ready")
        sums_ready = sem("sums_ready")
        std_ready = sem("std_ready")
        silu_ready = sem("silu_ready")
        hidden_ready = sem("hidden_ready")
        dve_step = sem("dve_step")
        act_step = sem("act_step")
        out_landed = sem("out_landed")
        head_in = sem("head_in")
        head_sums = sem("head_sums")
        head_taken = sem("head_taken")
        root_ready = sem("root_ready")
        lora_in = sem("lora_in")
        lora_mid = sem("lora_mid")
        lora_act = sem("lora_act")
        lora_out = sem("lora_out")
        lora_taken = sem("lora_taken")
        exp_ready = sem("exp_ready")
        decay_ready = sem("decay_ready")
        scan_in = sem("scan_in")
        gram_ready = sem("gram_ready")
        turned_ready = sem("turned_ready")
        turned_taken = sem("turned_taken")
        gram_taken = sem("gram_taken")
        inv_half = sem("inv_half")
        inv_half_taken = sem("inv_half_taken")
        inv_off = sem("inv_off")
        inv_taken = sem("inv_taken")
        rhs_ready = sem("rhs_ready")
        rhs_taken = sem("rhs_taken")
        sol_ready = sem("sol_ready")
        sol_taken = sem("sol_taken")
        chunk_out = sem("chunk_out")
        state_ready = sem("state_ready")
        z_ready = sem("z_ready")
        ds_z_ready = sem("ds_z_ready")
        att_raw = sem("att_raw")
        exps_ready = sem("exps_ready")
        later_in = sem("later_in")
        later_ready = sem("later_ready")
        logit_ready = sem("logit_ready")
        att_ready = sem("att_ready")
        heads_out = sem("heads_out")
        heads_taken = sem("heads_taken")
        idx_ready = sem("idx_ready")
        idx_act = sem("idx_act")
        idx_taken = sem("idx_taken")
        att_turned = sem("att_turned")
        att_turned_taken = sem("att_turned_taken")
        small_landed = sem("small_landed")
        small_ready = sem("small_ready")
        h_ready = sem("h_ready")
        turn_in = sem("turn_in")
        turned_out = sem("turned_out")
        out_ready = sem("out_ready")
        ctx_landed = sem("ctx_landed")
        cond_ready = sem("cond_ready")
        lam_in = sem("lam_in")
        lam_sums = sem("lam_sums")
        lam_exp = sem("lam_exp")
        sgu_free = sem("sgu_free")
        sgu_landed = sem("sgu_landed")
        sgu_turned = sem("sgu_turned")
        sgu_copied = sem("sgu_copied")
        sgu_out = sem("sgu_out")
        glu_ready = sem("glu_ready")
        conf_ready = sem("conf_ready")
        conf_act = sem("conf_act")
        merged_step = sem("merged_step")
        da_scores = sem("da_scores")
        da_max = sem("da_max")
        da_exp = sem("da_exp")
        da_mix = sem("da_mix")
        da_turned = sem("da_turned")
        da_copied = sem("da_copied")
        da_out = sem("da_out")
        da_stored = sem("da_stored")

        counts.start(nc.sync, lo_ready, -RING)
        counts.start(nc.tensor, bank_free, -RING)
        counts.start(nc.scalar, hidden_ready, -2)
        counts.start(nc.scalar, merged_step, -2)

        A = (v3(AH), v3(AL))
        HID = (v3(HH), v3(HL))
        COND = tuple(v3(t, 2) for t in COND_T)
        BR = (v3(BRH), v3(BRL))
        G = {}
        order = []

        def plan(g):
            g.p0 = sum(x.n_panels for x in order)
            g.t0 = sum(x.n_tiles for x in order)
            order.append(g)
            G[g.name] = g

        def plan_ffn(name, w_gate, gate_col, w_up, up_col, w_down):
            plan(pair(f"{name}.up", w_gate, gate_col, C, w_up, up_col, C, F, A, A))
            plan(dense(f"{name}.down", w_down, 0, D, HID, kc=FC))

        for layer in range(DEPTH):
            if layer % 3 == 0:
                for j, n in enumerate("rkv"):
                    plan(dense(f"rw{layer}.{n}", a["rw_w_rkv"][layer // 3, j], 0, D, A))
                plan(dense(f"rw{layer}.out", a["rw_w_out"][layer // 3], 0, D, A))
            elif layer % 3 == 1:
                for j, n in enumerate("qkv"):
                    plan(dense(f"sb.{n}", a["sb_w_qkv"][0], j * D, D, A, tokens_out=n == "v"))
                plan(dense("sb.out", a["sb_w_out"][0], 0, D, A))
            else:
                for j, n in enumerate("qkv"):
                    plan(dense(f"ds.{n}", a["ds_w_in"][0], j * D, D, A, tokens_out=n == "v"))
                plan(dense("ds.qi", a["ds_w_in"][0], 3 * D, IDX_H * DH, A))
                plan(dense("ds.out", a["ds_w_out"][0], 0, D, A))
            plan_ffn(f"ffn{layer}", a["ffn_w_gu"][layer], 0, a["ffn_w_gu"][layer], F, a["ffn_w_down"][layer])
        BRANCH = {"a": (0, CA_W), "b": (2, SG_W), "c": (4, DA_W), "d": (8, CF_W)}
        FULL = [(0, "c"), (0, "x"), (1, "x")]

        def plan_mix(l, s):
            w = a["w_in_2"][l]
            pre = f"mix{l}{s}"
            plan(dense(f"{pre}.k", w, K_OFF, DA_W, A))
            plan(dense(f"{pre}.v", w, V_OFF, DA_W, A, tokens_out=True))
            if (l, s) not in FULL:
                return
            plan(dense(f"{pre}.q", w, Q_OFF, DA_W, A))
            plan(dense(f"{pre}.ab", w, A_OFF, Q_OFF - A_OFF, A))
            plan(dense(f"{pre}.d", w, D_OFF, 2 * CF_W, A))
            for n, (b, (c0, width)) in enumerate(BRANCH.items()):
                opnd = tuple(t[:, c0:c0 + width // P] for t in BR)
                plan(pair(f"{pre}.{b}out", a[f"w_{b}_out_2"][l], 0, width // P, w, G_OFF + n * D, C, D, opnd, A))
            plan(dense(f"{pre}.o", a["w_o_2"][l], 0, D, A))

        for l in range(D2):
            plan(dense(f"ada{l}", a["w_ada_2"][l], 0, N_MOD * D, COND))
            for s in "xc":
                plan_ffn(f"f1{l}{s}", a["ffn1_w1_2"][l], 0, a["ffn1_w3_2"][l], 0, a["ffn1_w2_2"][l])
            for s in "cx":
                plan_mix(l, s)
                if (l, s) in FULL:
                    plan_ffn(f"f2{l}{s}", a["ffn2_w1_2"][l], 0, a["ffn2_w3_2"][l], 0, a["ffn2_w2_2"][l])

        def steps_of(eng, g, per, step, last_straight=False):
            full = g.steps // g.body
            first = 1 if any(counts.at(eng, x) < 0 for x in per) else 0
            last = full - (1 if last_straight else 0)
            for s in range(first * g.body):
                step(s, s % g.body)
            if last - first > 1:
                with repeat(eng, last - first, per) as i:
                    for j in range(g.body):
                        step((i + first) * g.body + j, j)
                begin = last * g.body
            else:
                begin = first * g.body
            for s in range(begin, g.steps):
                step(s, s % g.body)

        def sp_panels(sp, name):
            g = G[name]

            def step(s, j):
                for k, (w, col, k0, nk, _, _) in enumerate(g.panels):
                    slot = (g.p0 + j * g.pps + k) % RING
                    n = after(sp, lo_ready)
                    if n is not None:
                        sp.wait_ge(lo_ready, n)
                    src = w[k0 * P:(k0 + nk) * P, bass.ds(s * P + col, P)].rearrange("(c p) m -> p c m", p=P)
                    sp.dma_start(raw[slot][:, 0:nk * P].rearrange("p (c m) -> p c m", m=P), src).then_inc(raw_landed[slot], 16)

            steps_of(sp, g, {lo_ready: g.body * g.pps}, step)

        def pool_panels(pool, name):
            g = G[name]

            def step(s, j):
                for k, (_, _, _, nk, _, _) in enumerate(g.panels):
                    slot = (g.p0 + j * g.pps + k) % RING
                    n = nk * P
                    pool.wait_ge(hi_ready, after(pool, hi_ready))
                    pool.tensor_tensor(wlo[slot][:, 0:n], raw[slot][:, 0:n], whi[slot][:, 0:n],
                                                   ALU.subtract).then_inc(lo_ready, 1)

            steps_of(pool, g, {hi_ready: g.body * g.pps}, step)

        def act_round(act, g, q):
            slot, n = (g.p0 + q) % RING, g.panels[q % g.pps][3] * P
            act.wait_ge(raw_landed[slot], after(act, raw_landed[slot], 16))
            act.activation(whi[slot][:, 0:n], raw[slot][:, 0:n], ACT.Copy).then_inc(hi_ready, 1)

        def act_panels(act, name, work=None):
            g = G[name]
            at = order.index(g)
            following = order[at + 1] if at + 1 < len(order) else None

            def step(s, j):
                for k in range(g.pps):
                    act.wait_ge(panels_done, after(act, panels_done))
                    if work:
                        work(s, j, k)
                    q = j * g.pps + k + RING
                    if isinstance(s, int) and s * g.pps + k + RING >= g.n_panels:
                        if following:
                            act_round(act, following, s * g.pps + k + RING - g.n_panels)
                    else:
                        act_round(act, g, q)

            n = g.body * g.pps
            per = {panels_done: n, **{r: 16 * n // RING for r in raw_landed}}
            if work:
                per |= work.per
            steps_of(act, g, per, step, last_straight=True)

        def pe_panels(pe, name, fills=1):
            g = G[name]
            pe.wait_ge(operand_ready, after(pe, operand_ready, fills))

            def step(s, j):
                started = set()
                for k, (_, _, k0, nk, tile, (oh, ol)) in enumerate(g.panels):
                    slot = (g.p0 + j * g.pps + k) % RING
                    ps = bank[(g.t0 + j * g.tiles + tile) % RING]
                    if tile not in started:
                        n = after(pe, bank_free)
                        if n is not None:
                            pe.wait_ge(bank_free, n)
                    pe.wait_ge(lo_ready, after(pe, lo_ready))
                    last_panel = tile not in [x[4] for x in g.panels[k + 1:]]
                    for tt in range(TT if g.tokens_out else 1):
                        for c in range(nk):
                            wh, wl = (t[slot][:, c * P:(c + 1) * P] for t in (whi, wlo))
                            passes = ((wh, oh), (wh, ol), (wl, oh))
                            for n, (w, o) in enumerate(passes):
                                first = tile not in started and c == 0 and n == 0
                                last = last_panel and c == nk - 1 and n == 2
                                if g.tokens_out:
                                    mm = pe.matmul(ps[:, tt * P:(tt + 1) * P], o[:, k0 + c, tt * P:(tt + 1) * P], w,
                                                   start=first, stop=last)
                                else:
                                    mm = pe.matmul(ps[:, 0:o.shape[2]], w, o[:, k0 + c, :], start=first, stop=last)
                    started.add(tile)
                    mm.then_inc(panels_done, 1)

            n = g.body * g.pps
            steps_of(pe, g, {bank_free: RING, lo_ready: n}, step)

        def dve_tiles(dve, name, take, per=None):
            g = G[name]

            def step(s, j):
                dve.wait_ge(panels_done, after(dve, panels_done, g.pps))
                take(s, j, [bank[(g.t0 + j * g.tiles + t) % RING] for t in range(g.tiles)])

            steps_of(dve, g, {panels_done: g.body * g.pps, **{k: v * g.body for k, v in (per or {}).items()}}, step)
            dve.wait_ge(bank_free, tiles_of(name))

        def take_copy(dve, dst, scale=None):
            def take(s, j, banks):
                o = dst[:, bass.ds(s * S, S)]
                if scale is None:
                    dve.tensor_copy(o, banks[0][:, 0:S]).then_inc(bank_free, 1)
                else:
                    dve.tensor_scalar(o, banks[0][:, 0:S], scale, None, ALU.mult).then_inc(bank_free, 1)
            return take

        def take_tokens(dve, dst):
            def take(s, j, banks):
                dve.tensor_copy(dst[:, :, bass.ds(s * P, P)],
                                             banks[0][:, 0:S].rearrange("p (a m) -> p a m", m=P)).then_inc(bank_free, 1)
            return take

        def take_residual(dve, x, gate=None):
            def take(s, j, banks):
                o = x[:, bass.ds(s * S, S)]
                if gate is None:
                    dve.tensor_tensor(o, o, banks[0][:, 0:S], ALU.add).then_inc(bank_free, 1)
                else:
                    dve.scalar_tensor_tensor(o, banks[0][:, 0:S], gate[:, bass.ds(s, 1)], o,
                                                          ALU.mult, ALU.add).then_inc(bank_free, 1)
            return take

        def split(dve, src, dst=None):
            hi, lo = dst or (AH, AL)
            n = src.shape[1]
            dve.tensor_copy(hi[:, 0:n], src[:, :]).then_inc(dve_step, 1)
            dve.wait_ge(dve_step, after(dve, dve_step))
            dve.tensor_tensor(lo[:, 0:n], src[:, :], hi[:, 0:n], ALU.subtract).then_inc(operand_ready, 1)
            dve.wait_ge(operand_ready, after(dve, operand_ready))

        def act_norm(act, x, sq):
            act.activation(sq[:, :], x[:, :], ACT.Square).then_inc(squares_ready, 1)
            act.wait_ge(sums_ready, after(act, sums_ready))
            act.activation(STD[:, :], bank[4][:, 0:S], ACT.Sqrt, bias=eps[:, 0:1], scale=1.0 / D).then_inc(std_ready, 1)

        def pe_norm(pe, sq):
            pe.wait_ge(squares_ready, after(pe, squares_ready))
            for c in range(C):
                mm = pe.matmul(bank[4][:, 0:S], ones[:, :], sq[:, c * S:(c + 1) * S], start=c == 0, stop=c == C - 1)
            mm.then_inc(sums_ready, 1)

        def dve_norm(dve, x, gain, h, shift=None, to_operand=True):
            dve.wait_ge(std_ready, after(dve, std_ready))
            dve.reciprocal(RSTD[:, :], STD[:, :]).then_inc(dve_step, 1)
            dve.wait_ge(dve_step, after(dve, dve_step))
            for c in range(C):
                o = h[:, c * S:(c + 1) * S]
                op = dve.scalar_tensor_tensor(o, x[:, c * S:(c + 1) * S], gain(c), RSTD[:, :], ALU.mult, ALU.mult)
                if shift:
                    if c == C - 1:
                        op.then_inc(dve_step, 1)
                        dve.wait_ge(dve_step, after(dve, dve_step))
            if shift:
                for c in range(C):
                    o = h[:, c * S:(c + 1) * S]
                    op = dve.tensor_scalar(o, o, shift(c), None, ALU.add)
            op.then_inc(h_ready, 1)
            dve.wait_ge(h_ready, after(dve, h_ready))
            if to_operand:
                split(dve, h)

        def tiles_of(name):
            return G[name].t0 + G[name].n_tiles

        def act_ffn(act, name, x):
            act_norm(act, x, W[8])

            def gate(s, j, k):
                if k == 0:
                    n = after(act, hidden_ready)
                    if n is not None:
                        act.wait_ge(hidden_ready, n)
                    g = G[f"{name}.up"]
                    ps = bank[(g.t0 + j * g.tiles) % RING]
                    act.activation(silu[j % 2][:, :], ps[:, 0:S], ACT.Silu).then_inc(silu_ready, 1)
            gate.per = {hidden_ready: 2}
            act_panels(act, f"{name}.up", gate)
            act_panels(act, f"{name}.down")

        def pe_ffn(pe, name):
            pe_norm(pe, W[8])
            pe_panels(pe, f"{name}.up")
            pe.wait_ge(hidden_ready, after(pe, hidden_ready, FC))
            pe_panels(pe, f"{name}.down", fills=0)

        def dve_ffn(dve, name, x, gain, shift=None, out_gate=None):
            dve_norm(dve, x, gain, W[7], shift)

            def take(s, j, banks):
                dve.wait_ge(silu_ready, after(dve, silu_ready))
                o = bass.ds(s * S, S)
                dve.tensor_tensor(hid[:, :], silu[j % 2][:, :], banks[1][:, 0:S], ALU.mult).then_inc(bank_free, 2)
                dve.wait_ge(bank_free, after(dve, bank_free, 2))
                dve.tensor_copy(HH[:, o], hid[:, :]).then_inc(dve_step, 1)
                dve.wait_ge(dve_step, after(dve, dve_step))
                dve.tensor_tensor(HL[:, o], hid[:, :], HH[:, o], ALU.subtract).then_inc(hidden_ready, 1)
                dve.wait_ge(hidden_ready, after(dve, hidden_ready))
            counts.start(dve, bank_free, G[f"{name}.up"].t0)
            dve_tiles(dve, f"{name}.up", take, {silu_ready: 1, bank_free: 2, dve_step: 1, hidden_ready: 1})
            dve_tiles(dve, f"{name}.down", take_residual(dve, x, out_gate))

        def pe_heads(pe, mat, src, chunks=C):
            pe.wait_ge(head_in, after(pe, head_in))
            for c in range(chunks):
                mm = pe.matmul(bank[4 + c // 2][:, (c % 2) * S:(c % 2 + 1) * S], mat, src[:, c * S:(c + 1) * S],
                               start=True, stop=True)
                if c % 2 or c == chunks - 1:
                    mm.then_inc(head_sums, 1)

        def dve_heads(dve, take, chunks=C):
            for c in range(0, chunks, 2):
                dve.wait_ge(head_sums, after(dve, head_sums))
                n = min(2, chunks - c) * S
                op = take(slice(c * S, c * S + n), bank[4 + c // 2][:, 0:n])
            return op

        RW_H, RW_D, RW_XA, RW_XB, RW_R, RW_K, RW_A, RW_CUM, RW_G = W[0], W[1], W[2], CTX, W[3], W[4], W[6], W[7], W[8]
        RW_Q, RW_P, RW_B, RW_C, RW_Y, RW_BONUS = W[3], W[0], W[1], W[4], W[6], W[2]
        lora_wa, lora_g, lora_gv = silu[0], silu[1], hid
        WEND = sb("WEND", C * NCH)
        Q4 = 512
        N_, GBQ, GCP, GCQ = (CTX[:, k * Q4:(k + 1) * Q4] for k in range(4))
        L_, VT, BT, CT = (W[7][:, k * Q4:(k + 1) * Q4] for k in range(4))
        work = [sb(f"scan{k}", Q4, at=a_at + k * Q4 * 4) for k in range(7)]
        IY, IX, IT, LOFF, RHS, SOL, STATE = (t[:, :] for t in work)
        KK_MIN = 1e-24

        def rw_values(layer):
            return VF if layer == 0 else W[5]

        def lora_parts(layer):
            parts = [("w", RW_XB, lw1, L_W), ("a", RW_XB, la1, L_A)]
            if layer:
                parts.append(("v", RW_XA, lv1, L_V))
            return parts + [("g", RW_XB, lg1, L_G)]

        def sp_lora(sp, j):
            for t, w, n in ((lw1, "rw_w1", L_W), (la1, "rw_a1", L_A), (lg1, "rw_g1", L_G)):
                sp.dma_start(t[:, :].rearrange("p (c m) -> p c m", m=n),
                                            a[w][j].rearrange("(c p) m -> p c m", p=P)).then_inc(lora_landed, 16)
            sp.dma_start(lwa2[0:64, :], a["rw_w2"][j]).then_inc(lora_landed, 16)
            sp.dma_start(lwa2[64:128, :], a["rw_a2"][j]).then_inc(lora_landed, 16)
            sp.dma_start(lg2[:, :], a["rw_g2"][j][0:P, :]).then_inc(lora_landed, 16)
            sp.dma_start(lgv2[0:32, :], a["rw_g2"][j][P:L_G, :]).then_inc(lora_landed, 16)
            if j:
                sp.dma_start(lv1[:, :].rearrange("p (c m) -> p c m", m=L_V),
                                            a["rw_v1"][j - 1].rearrange("(c p) m -> p c m", p=P)).then_inc(lora_landed, 16)
                sp.dma_start(lgv2[32:64, :], a["rw_v2"][j - 1]).then_inc(lora_landed, 16)

        def pe_lora(pe, part, first=False):
            name, x, w1, n = part
            pe.wait_ge(lora_in, after(pe, lora_in))
            if not first:
                pe.wait_ge(lora_taken, after(pe, lora_taken, 4))
            base = {"w": 0, "a": 64, "v": 32, "g": 0}[name]
            m = min(n, P)
            w3 = w1[:, :].rearrange("p (c m) -> p c m", m=n)
            for c in range(C):
                mm = pe.matmul(bank[4][base:base + m, 0:S], w3[:, c, 0:m], x[:, c * S:(c + 1) * S],
                               start=c == 0, stop=c == C - 1)
            if n > P:
                for c in range(C):
                    mm = pe.matmul(bank[5][0:n - P, 0:S], w3[:, c, P:n], x[:, c * S:(c + 1) * S],
                                   start=c == 0, stop=c == C - 1)
            mm.then_inc(lora_mid, 1)
            pe.wait_ge(lora_act, after(pe, lora_act))
            for t in range(C):
                if t >= 4:
                    pe.wait_ge(lora_taken, after(pe, lora_taken))
                o, cols = bank[4 + t % 4][:, 0:S], slice(t * P, (t + 1) * P)
                if name == "w":
                    mm = pe.matmul(o, lwa2[0:64, cols], lora_wa[0:64, :], start=True, stop=True)
                elif name == "a":
                    mm = pe.matmul(o, lwa2[64:128, cols], lora_wa[64:128, :], start=True, stop=True)
                elif name == "v":
                    mm = pe.matmul(o, lgv2[32:64, cols], lora_gv[32:64, :], start=True, stop=True)
                else:
                    pe.matmul(o, lg2[:, cols], lora_g[:, :], start=True, stop=False)
                    mm = pe.matmul(o, lgv2[0:32, cols], lora_gv[0:32, :], start=False, stop=True)
                mm.then_inc(lora_out, 1)

        def act_lora(act, part, j):
            name = part[0]
            act.wait_ge(lora_mid, after(act, lora_mid))
            if name == "w":
                op = act.activation(lora_wa[0:64, :], bank[4][0:64, 0:S], ACT.Tanh)
            elif name == "a":
                op = act.activation(lora_wa[64:128, :], bank[4][64:128, 0:S], ACT.Copy)
            elif name == "v":
                op = act.activation(lora_gv[32:64, :], bank[4][32:64, 0:S], ACT.Copy)
            else:
                act.activation(lora_g[:, :], bank[4][:, 0:S], ACT.Sigmoid)
                op = act.activation(lora_gv[0:32, :], bank[5][0:32, 0:S], ACT.Sigmoid)
            op.then_inc(lora_act, 1)
            dst = {"w": RW_CUM, "a": RW_A, "v": RW_XA, "g": RW_G}[name]
            for t in range(C):
                act.wait_ge(lora_out, after(act, lora_out))
                o, i = dst[:, t * S:(t + 1) * S], bank[4 + t % 4][:, 0:S]
                if name == "g":
                    op = act.activation(o, i, ACT.Copy)
                else:
                    b = vec("rw_v0", 0, t) if name == "v" else vec(f"rw_{name}0", j, t)
                    op = act.activation(o, i, ACT.Sigmoid, bias=b)
                op.then_inc(lora_taken, 1)

        def act_rwkv(act, layer):
            j = layer // 3
            parts = lora_parts(layer)
            act_norm(act, X, W[8])
            act_panels(act, f"rw{layer}.r")
            act_lora(act, parts[0], j)
            act_panels(act, f"rw{layer}.k")
            act_lora(act, parts[1], j)
            act_panels(act, f"rw{layer}.v")
            for part in parts[2:]:
                act_lora(act, part, j)
            act.wait_ge(head_taken, after(act, head_taken))
            act.activation(RW_BONUS[:, :], RW_BONUS[:, :], ACT.Sqrt).then_inc(root_ready, 1)
            act.wait_ge(decay_ready, after(act, decay_ready))
            act.activation(RW_CUM[:, :], RW_XB[:, :], ACT.Exp, scale=-DECAY).then_inc(exp_ready, 1)
            act.activation(RW_XB[:, :], RW_XB[:, :], ACT.Exp, scale=DECAY).then_inc(exp_ready, 1)
            for ch in range(NCH):
                for k, t in enumerate((VT, BT, CT)):
                    act.wait_ge(turned_ready, after(act, turned_ready))
                    act.activation(t, bank[5 + k][:, :], ACT.Copy).then_inc(turned_taken, 1)
                act.wait_ge(rhs_ready, after(act, rhs_ready))
                act.activation(RHS, bank[3][:, :], ACT.Copy).then_inc(rhs_taken, 1)
                for lv in range(1, 6):
                    act.wait_ge(inv_half, after(act, inv_half))
                    act.activation(IT, bank[0][:, :], ACT.Copy).then_inc(inv_half_taken, 1)
                act.wait_ge(sol_ready, after(act, sol_ready))
                act.activation(SOL, bank[4][:, :], ACT.Copy, scale=-1.0).then_inc(sol_taken, 1)
            act.wait_ge(head_taken, after(act, head_taken))
            act.activation(RW_Y[:, :], RW_Y[:, :], ACT.Sqrt).then_inc(root_ready, 1)
            act_panels(act, f"rw{layer}.out")

        def pe_scan(pe, layer):
            V = rw_values(layer)
            heads = [(c, slice(DH * hh, DH * hh + DH)) for c in range(C) for hh in range(2)]
            pe.wait_ge(scan_in, after(pe, scan_in))
            for ch in range(NCH):
                def tok(t, c, r):
                    return t[r, c * S + ch * CHUNK:c * S + (ch + 1) * CHUNK]

                def sq(t, c, r):
                    return t[r, c * DH:(c + 1) * DH]

                if ch:
                    pe.wait_ge(state_ready, after(pe, state_ready))
                for k, (l, r_) in enumerate(((RW_B, RW_P), (RW_P, RW_B), (RW_C, RW_P), (RW_B, RW_Q), (RW_C, RW_Q))):
                    for c, r in heads:
                        mm = pe.matmul(sq(bank[k], c, r), tok(l, c, r), tok(r_, c, r), start=True, stop=True)
                    mm.then_inc(gram_ready, 1)
                for k, t in enumerate((V, RW_B, RW_C)):
                    for c, r in heads:
                        mm = pe.matmul(sq(bank[5 + k], c, r), tok(t, c, r), const("ident")[r, r], start=True, stop=True)
                    mm.then_inc(turned_ready, 1)
                pe.wait_ge(turned_taken, after(pe, turned_taken, 3))
                pe.wait_ge(gram_taken, after(pe, gram_taken, 5))
                for c, r in heads:
                    if ch:
                        pe.matmul(sq(bank[3], c, r), tok(RW_P, c, r), sq(STATE, c, r), start=True, stop=False)
                    mm = pe.matmul(sq(bank[3], c, r), sq(GCP, c, r), sq(VT, c, r), start=not ch, stop=True)
                mm.then_inc(rhs_ready, 1)
                for lv in range(1, 6):
                    pe.wait_ge(inv_taken, after(pe, inv_taken))
                    for c, r in heads:
                        mm = pe.matmul(sq(bank[0], c, r), sq(LOFF, c, r), sq(IY, c, r), start=True, stop=True)
                    mm.then_inc(inv_half, 1)
                    pe.wait_ge(inv_half_taken, after(pe, inv_half_taken))
                    for c, r in heads:
                        mm = pe.matmul(sq(bank[1], c, r), sq(IX, c, r), sq(IT, c, r), start=True, stop=True)
                        if lv < 5:
                            mm = pe.matmul(sq(bank[2], c, r), sq(IT, c, r), sq(IX, c, r), start=True, stop=True)
                    mm.then_inc(inv_off, 1)
                pe.wait_ge(inv_taken, after(pe, inv_taken))
                pe.wait_ge(rhs_taken, after(pe, rhs_taken))
                for c, r in heads:
                    mm = pe.matmul(sq(bank[4], c, r), sq(IY, c, r), sq(RHS, c, r), start=True, stop=True)
                mm.then_inc(sol_ready, 1)
                pe.wait_ge(sol_taken, after(pe, sol_taken))
                for c, r in heads:
                    if ch:
                        pe.matmul(sq(bank[5], c, r), sq(STATE, c, r), tok(RW_Q, c, r), start=True, stop=False)
                    pe.matmul(sq(bank[5], c, r), sq(VT, c, r), sq(GCQ, c, r), start=not ch, stop=False)
                    mm = pe.matmul(sq(bank[5], c, r), sq(SOL, c, r), sq(GBQ, c, r), start=False, stop=True)
                if ch < NCH - 1:
                    for c, r in heads:
                        pe.matmul(sq(bank[6], c, r), sq(CT, c, r), sq(VT, c, r), start=True, stop=False)
                        mm = pe.matmul(sq(bank[6], c, r), sq(BT, c, r), sq(SOL, c, r), start=False, stop=True)
                mm.then_inc(chunk_out, 1)

        def pe_rwkv(pe, layer):
            parts = lora_parts(layer)
            pe_norm(pe, W[8])
            pe_panels(pe, f"rw{layer}.r")
            pe.wait_ge(lora_landed, after(pe, lora_landed, 16 * (9 if layer else 7)))
            pe_lora(pe, parts[0], first=True)
            pe_panels(pe, f"rw{layer}.k")
            pe_lora(pe, parts[1])
            pe_panels(pe, f"rw{layer}.v")
            for part in parts[2:]:
                pe_lora(pe, part)
            pe.wait_ge(lora_taken, after(pe, lora_taken, 4))
            pe_heads(pe, const("headones"), RW_D)
            pe_heads(pe, const("headones"), RW_D)
            pe_scan(pe, layer)
            pe_heads(pe, const("headones"), RW_Y)
            pe_heads(pe, const("headones"), RW_D)
            pe_panels(pe, f"rw{layer}.out")

        def dve_scan(dve, layer):
            def masked(dst, src, mask):
                return dve.tensor_tensor(dst.rearrange("p (c t) -> p c t", t=DH), src.rearrange("p (c t) -> p c t", t=DH),
                                         const(mask).unsqueeze(1).to_broadcast([P, C, DH]), ALU.mult)

            def eye_minus(t):
                v = t.rearrange("p (c t) -> p c t", t=DH)
                return dve.scalar_tensor_tensor(v, v, -1.0, const("eye64").unsqueeze(1).to_broadcast([P, C, DH]),
                                                ALU.mult, ALU.add)

            wend = WEND[:, :].rearrange("p (c n) -> p c n", n=NCH)
            for ch in range(NCH):
                for k, (dst, mask) in enumerate(((N_, "before"), (L_, "below"), (GCP, "before"), (GBQ, "upto"), (GCQ, "upto"))):
                    dve.wait_ge(gram_ready, after(dve, gram_ready))
                    masked(dst, bank[k][:, :], mask).then_inc(gram_taken, 1)
                    dve.wait_ge(gram_taken, after(dve, gram_taken))
                masked(IY, N_, "upper0")
                masked(IX, L_, "lower0").then_inc(dve_step, 1)
                dve.wait_ge(dve_step, after(dve, dve_step))
                eye_minus(IY).then_inc(dve_step, 1)
                dve.wait_ge(dve_step, after(dve, dve_step))
                eye_minus(IX)
                masked(LOFF, L_, "lower1").then_inc(inv_taken, 1)
                dve.wait_ge(inv_taken, after(dve, inv_taken))
                for lv in range(1, 6):
                    dve.wait_ge(inv_off, after(dve, inv_off))
                    last = dve.tensor_tensor(IY, IY, bank[1][:, :], ALU.subtract)
                    if lv < 5:
                        dve.tensor_tensor(IX, IX, bank[2][:, :], ALU.subtract)
                        last = masked(LOFF, L_, f"lower{lv + 1}")
                    last.then_inc(inv_taken, 1)
                    dve.wait_ge(inv_taken, after(dve, inv_taken))
                dve.wait_ge(chunk_out, after(dve, chunk_out))
                y = dve.tensor_copy(v3(RW_Y)[:, :, ch * CHUNK:(ch + 1) * CHUNK],
                                    bank[5][:, :].rearrange("p (c t) -> p c t", t=CHUNK))
                if ch == NCH - 1:
                    y.then_inc(head_in, 1)
                    dve.wait_ge(head_in, after(dve, head_in))
                    continue
                if ch:
                    dve.tensor_tensor(STATE, STATE, bank[6][:, :], ALU.add).then_inc(dve_step, 1)
                    dve.wait_ge(dve_step, after(dve, dve_step))
                src = STATE if ch else bank[6][:, :]
                dve.tensor_tensor(STATE.rearrange("p (c t) -> p c t", t=DH),
                                                 src.rearrange("p (c t) -> p c t", t=DH),
                                                 wend[:, :, ch:ch + 1].to_broadcast([P, C, DH]), ALU.mult).then_inc(state_ready, 1)
                dve.wait_ge(state_ready, after(dve, state_ready))

        def dve_rwkv(dve, layer):
            j = layer // 3
            V = rw_values(layer)
            dve_norm(dve, X, lambda c: vec("norm_mix", layer, c), RW_H, to_operand=False)
            h, d = v3(RW_H), v3(RW_D)
            dve.tensor_scalar(d[:, :, 0:1], h[:, :, 0:1], -1.0, None, ALU.mult)
            dve.tensor_tensor(d[:, :, 1:S], h[:, :, 0:S - 1], h[:, :, 1:S], ALU.subtract).then_inc(dve_step, 1)
            dve.wait_ge(dve_step, after(dve, dve_step))

            def mixed(k, dst):
                for c in range(C):
                    cs = slice(c * S, (c + 1) * S)
                    op = dve.scalar_tensor_tensor(dst[:, cs], RW_D[:, cs], vec("rw_mix", 6 * j + k, c), RW_H[:, cs],
                                                  ALU.mult, ALU.add)
                return op

            mixed(0, RW_XA).then_inc(dve_step, 1)
            dve.wait_ge(dve_step, after(dve, dve_step))
            split(dve, RW_XA)
            mixed(3, RW_XB).then_inc(lora_in, 1)
            dve.wait_ge(lora_in, after(dve, lora_in))
            mixed(1, RW_XA).then_inc(dve_step, 1)
            dve.wait_ge(dve_step, after(dve, dve_step))
            dve_tiles(dve, f"rw{layer}.r", take_copy(dve, RW_R))
            split(dve, RW_XA)
            dve.wait_ge(lora_mid, after(dve, lora_mid))
            mixed(4, RW_XB).then_inc(lora_in, 1)
            dve.wait_ge(lora_in, after(dve, lora_in))
            op = mixed(2, RW_XA)
            if layer:
                op.then_inc(lora_in, 1)
                dve.wait_ge(lora_in, after(dve, lora_in))
            else:
                op.then_inc(dve_step, 1)
                dve.wait_ge(dve_step, after(dve, dve_step))
            dve_tiles(dve, f"rw{layer}.k", take_copy(dve, RW_K))
            split(dve, RW_XA)
            dve.wait_ge(lora_mid, after(dve, lora_mid))
            mixed(5, RW_XB).then_inc(lora_in, 1)
            dve.wait_ge(lora_in, after(dve, lora_in))
            dve_tiles(dve, f"rw{layer}.v", take_copy(dve, V))
            dve.wait_ge(lora_taken, after(dve, lora_taken, 16))
            if layer:
                dve.wait_ge(lora_mid, after(dve, lora_mid))
                dve.wait_ge(lora_taken, after(dve, lora_taken, 8))
                dve.tensor_tensor(RW_D[:, :], VF[:, :], V[:, :], ALU.subtract).then_inc(dve_step, 1)
                dve.wait_ge(dve_step, after(dve, dve_step))
                dve.tensor_tensor(RW_D[:, :], RW_D[:, :], RW_XA[:, :], ALU.mult).then_inc(dve_step, 1)
                dve.wait_ge(dve_step, after(dve, dve_step))
                dve.tensor_tensor(V[:, :], V[:, :], RW_D[:, :], ALU.add)
            kk, b = RW_P, RW_B
            dve.tensor_tensor(v3(kk), v3(RW_K), vec_b("rw_k_k", j), ALU.mult).then_inc(dve_step, 1)
            dve.wait_ge(dve_step, after(dve, dve_step))
            dve.tensor_tensor(b[:, :], kk[:, :], kk[:, :], ALU.mult).then_inc(head_in, 1)
            dve.wait_ge(head_in, after(dve, head_in))
            t = RW_BONUS
            dve.scalar_tensor_tensor(v3(t), v3(RW_A), -1.0, vec_b("rw_k_a", j), ALU.add, ALU.mult).then_inc(dve_step, 1)
            dve.wait_ge(dve_step, after(dve, dve_step))
            dve.scalar_tensor_tensor(RW_K[:, :], t[:, :], 1.0, RW_K[:, :], ALU.add, ALU.mult).then_inc(dve_step, 1)
            dve.wait_ge(dve_step, after(dve, dve_step))
            dve_heads(dve, lambda s, ps: dve.tensor_scalar(t[:, s], ps, KK_MIN, None, ALU.max)).then_inc(head_taken, 1)
            dve.wait_ge(head_taken, after(dve, head_taken))
            dve.wait_ge(lora_mid, after(dve, lora_mid))
            for c in range(C):
                cs = slice(c * S, (c + 1) * S)
                op = dve.tensor_tensor_scan(RW_XB[:, cs], const("carry"), RW_CUM[:, cs], 0.0, ALU.mult, ALU.add)
            op.then_inc(decay_ready, 1)
            dve.wait_ge(decay_ready, after(dve, decay_ready))
            dve.tensor_tensor(b[:, :], RW_R[:, :], RW_K[:, :], ALU.mult).then_inc(dve_step, 1)
            dve.wait_ge(dve_step, after(dve, dve_step))
            dve.tensor_tensor(v3(b), v3(b), vec_b("rw_r_k", j), ALU.mult).then_inc(head_in, 1)
            dve.wait_ge(head_in, after(dve, head_in))
            dve.wait_ge(root_ready, after(dve, root_ready))
            dve.reciprocal(t[:, :], t[:, :]).then_inc(dve_step, 1)
            dve.wait_ge(dve_step, after(dve, dve_step))
            dve.tensor_tensor(kk[:, :], kk[:, :], t[:, :], ALU.mult).then_inc(dve_step, 1)
            dve.wait_ge(dve_step, after(dve, dve_step))
            dve_heads(dve, lambda s, ps: dve.tensor_tensor(t[:, s], ps, V[:, s], ALU.mult))
            dve.tensor_tensor(b[:, :], kk[:, :], RW_A[:, :], ALU.mult).then_inc(dve_step, 1)
            dve.wait_ge(dve_step, after(dve, dve_step))
            dve.wait_ge(exp_ready, after(dve, exp_ready))
            g64 = [x[:, :].rearrange("p (g t) -> p g t", t=CHUNK) for x in (kk, RW_CUM)]
            dve.tensor_tensor(g64[0][:, :, 1:CHUNK], g64[0][:, :, 1:CHUNK], g64[1][:, :, 0:CHUNK - 1], ALU.mult)
            dve.tensor_copy(WEND[:, :].unsqueeze(2), g64[1][:, :, CHUNK - 1:CHUNK])
            dve.tensor_tensor(RW_Q[:, :], RW_R[:, :], RW_CUM[:, :], ALU.mult)
            dve.wait_ge(exp_ready, after(dve, exp_ready))
            dve.tensor_tensor(RW_C[:, :], RW_K[:, :], RW_XB[:, :], ALU.mult)
            dve.tensor_tensor(b[:, :], b[:, :], RW_XB[:, :], ALU.mult).then_inc(scan_in, 1)
            dve.wait_ge(scan_in, after(dve, scan_in))
            dve_scan(dve, layer)
            y, yc = RW_Y, RW_P
            dve_heads(dve, lambda s, ps: dve.scalar_tensor_tensor(
                yc[:, s], ps, -1.0 / DH, y[:, s], ALU.mult, ALU.add)).then_inc(dve_step, 1)
            dve.wait_ge(dve_step, after(dve, dve_step))
            dve.tensor_tensor(b[:, :], yc[:, :], yc[:, :], ALU.mult).then_inc(head_in, 1)
            dve.wait_ge(head_in, after(dve, head_in))
            dve_heads(dve, lambda s, ps: dve.tensor_scalar(y[:, s], ps, 1.0 / DH, GN_EPS, ALU.mult, ALU.add)).then_inc(head_taken, 1)
            dve.wait_ge(head_taken, after(dve, head_taken))
            dve.wait_ge(root_ready, after(dve, root_ready))
            dve.reciprocal(y[:, :], y[:, :]).then_inc(dve_step, 1)
            dve.wait_ge(dve_step, after(dve, dve_step))
            dve.tensor_tensor(yc[:, :], yc[:, :], y[:, :], ALU.mult).then_inc(dve_step, 1)
            dve.wait_ge(dve_step, after(dve, dve_step))
            dve.wait_ge(lora_taken, after(dve, lora_taken, 8))
            for c in range(C):
                cs = slice(c * S, (c + 1) * S)
                op = dve.scalar_tensor_tensor(yc[:, cs], yc[:, cs], vec("rw_ln_w", j, c), RW_BONUS[:, cs], ALU.mult, ALU.add)
            op.then_inc(dve_step, 1)
            dve.wait_ge(dve_step, after(dve, dve_step))
            for c in range(C):
                cs = slice(c * S, (c + 1) * S)
                op = dve.scalar_tensor_tensor(yc[:, cs], yc[:, cs], vec("rw_ln_b", j, c), RW_G[:, cs], ALU.add, ALU.mult)
            op.then_inc(dve_step, 1)
            dve.wait_ge(dve_step, after(dve, dve_step))
            split(dve, yc)
            dve_tiles(dve, f"rw{layer}.out", take_residual(dve, X))

        Q_, K_, VT_, O_ = W[3], W[4], W[5], W[6]
        HS = TT * S

        def slots(t, n=4):
            return [t[:, k * HS:(k + 1) * HS] for k in range(n)]

        SB_E, SB_ATT = slots(W[0])[0:2], slots(W[0])[2:4]
        SB_SP, SB_MASKED = slots(W[1])[0:2], slots(W[1])[2:4]
        SB_Z, SB_LOG = slots(W[2])[0:2], slots(W[2])[2:4]

        def head_rows(hd):
            return slice(DH * (hd % 2), DH * (hd % 2) + DH), hd // 2

        def pe_sb(pe):
            pe_norm(pe, W[8])
            for n in "qkv":
                pe_panels(pe, f"sb.{n}", fills=1 if n == "q" else 0)
            pe.wait_ge(bank_free, tiles_of("sb.v"))

            def scores(hd):
                r, c = head_rows(hd)
                if hd >= 2:
                    pe.wait_ge(logit_ready, after(pe, logit_ready))
                for st in range(TT):
                    mm = pe.matmul(bank[4 + hd % 2][:, st * S:(st + 1) * S], K_[r, c * S + st * P:c * S + (st + 1) * P],
                                   Q_[r, c * S:(c + 1) * S], start=True, stop=True)
                mm.then_inc(z_ready, 1)

            def output(hd):
                r, c = head_rows(hd)
                pe.wait_ge(att_ready, after(pe, att_ready))
                if hd % 2 == 0 and hd >= 4:
                    pe.wait_ge(heads_taken, after(pe, heads_taken))
                for st in range(TT):
                    mm = pe.matmul(bank[c % 2][r, 0:S], VT_[:, st * D + hd * DH:st * D + (hd + 1) * DH],
                                   SB_ATT[hd % 2][:, st * S:(st + 1) * S], start=st == 0, stop=st == TT - 1)
                if hd % 2:
                    mm.then_inc(heads_out, 1)

            scores(0)
            for hd in range(H):
                if hd + 1 < H:
                    scores(hd + 1)
                pe.wait_ge(later_in, after(pe, later_in))
                m, o = SB_MASKED[hd % 2], bank[6 + hd % 2]
                pe.matmul(o[:, 0:S], const("after"), m[:, 0:S], start=True, stop=False)
                pe.matmul(o[:, 0:S], ones[:, :], m[:, S:2 * S], start=False, stop=True)
                pe.matmul(o[:, S:2 * S], const("after"), m[:, S:2 * S], start=True, stop=True).then_inc(later_ready, 1)
                if hd:
                    output(hd - 1)
            output(H - 1)
            pe.wait_ge(logit_ready, after(pe, logit_ready, 2))
            pe.wait_ge(heads_taken, after(pe, heads_taken, 2))
            pe_panels(pe, "sb.out")

        def act_sb(act):
            act_norm(act, X, W[8])
            for n in "qkv":
                act_panels(act, f"sb.{n}")

            def softplus(hd):
                e = SB_E[hd % 2]
                act.wait_ge(z_ready, after(act, z_ready))
                if hd >= 2:
                    act.wait_ge(later_in, after(act, later_in))
                act.activation(e, bank[4 + hd % 2][:, :], ACT.Abs).then_inc(act_step, 1)
                act.wait_ge(act_step, after(act, act_step))
                act.activation(e, e, ACT.Exp, scale=-1.0).then_inc(act_step, 1)
                act.wait_ge(act_step, after(act, act_step))
                act.activation(e, e, ACT.Ln, bias=1.0).then_inc(exps_ready, 1)

            softplus(0)
            for hd in range(H):
                if hd + 1 < H:
                    softplus(hd + 1)
                act.wait_ge(logit_ready, after(act, logit_ready))
                if hd % 2 == 0 and hd:
                    act.wait_ge(heads_out, after(act, heads_out))
                act.activation(SB_ATT[hd % 2], SB_LOG[hd % 2], ACT.Exp).then_inc(att_raw, 1)
            act.wait_ge(later_in, after(act, later_in, 2))
            act.wait_ge(heads_out, after(act, heads_out))
            act_panels(act, "sb.out")

        def dve_sb(dve, layer):
            dve_norm(dve, X, lambda c: vec("norm_mix", layer, c), W[0])
            dve_tiles(dve, "sb.q", take_copy(dve, Q_, DH ** -0.5))
            dve_tiles(dve, "sb.k", take_copy(dve, K_))
            dve_tiles(dve, "sb.v", take_tokens(dve, VT_[:, :].rearrange("p (a m) -> p a m", m=D)))

            def masked(hd):
                b = hd % 2
                dve.wait_ge(exps_ready, after(dve, exps_ready))
                ps = bank[4 + b][:, :]
                dve.scalar_tensor_tensor(SB_SP[b], ps, 0.0, SB_E[b], ALU.max, ALU.add).then_inc(dve_step, 1)
                dve.wait_ge(dve_step, after(dve, dve_step))
                dve.tensor_tensor(SB_MASKED[b], SB_SP[b], const("earlier"), ALU.mult).then_inc(later_in, 1)
                dve.wait_ge(later_in, after(dve, later_in))
                dve.tensor_tensor(SB_Z[b], ps, SB_SP[b], ALU.subtract).then_inc(dve_step, 1)
                dve.wait_ge(dve_step, after(dve, dve_step))

            def logits(hd):
                b = hd % 2
                dve.wait_ge(later_ready, after(dve, later_ready))
                dve.tensor_tensor(SB_LOG[b], SB_Z[b], bank[6 + b][:, :], ALU.subtract).then_inc(logit_ready, 1)
                dve.wait_ge(logit_ready, after(dve, logit_ready))

            def weights(hd):
                dve.wait_ge(att_raw, after(dve, att_raw))
                dve.tensor_tensor(SB_ATT[hd % 2], SB_ATT[hd % 2], const("earlier"), ALU.mult).then_inc(att_ready, 1)
                dve.wait_ge(att_ready, after(dve, att_ready))
                if hd % 2:
                    dve.wait_ge(heads_out, after(dve, heads_out))
                    c = hd // 2
                    dve.tensor_copy(O_[:, c * S:(c + 1) * S], bank[c % 2][:, 0:S]).then_inc(heads_taken, 1)
                    dve.wait_ge(heads_taken, after(dve, heads_taken))

            masked(0)
            for hd in range(H):
                if hd + 1 < H:
                    masked(hd + 1)
                logits(hd)
                weights(hd)
            split(dve, O_)
            dve_tiles(dve, "sb.out", take_residual(dve, X))

        DS_QI, DS_T = W[5], W[6]
        DS_Q, DS_K, DS_V, DS_O = W[1], W[2], W[3], W[4]
        kiw = sb("kiw", C * P, at=l_at)
        wiw = sb("wiw", C * IDX_H, at=l_at + C * P * 4)
        WI = sb("WI", TT * IDX_H)
        SC, SC2, SEL = W[7][:, 0:HS], W[7][:, HS:2 * HS], W[7][:, 2 * HS:3 * HS]
        IDX = [W[8][:, k * HS:(k + 1) * HS] for k in range(2)]
        best = sb("best", TT * 8)
        DS_L = slots(W[0])[0:2]
        DS_PT = slots(W[0])[2:4]
        top = sb("top", 4 * TT)
        DS_COLS = 3 * D + IDX_H * DH

        def sp_ds_small(sp):
            w = a["ds_w_in"][0]
            for k in range(2):
                sp.dma_start(
                    kiw[:, :].rearrange("p (c m) -> p c m", m=P)[:, :, k * DH:(k + 1) * DH],
                    w[:, DS_COLS:DS_COLS + DH].rearrange("(c p) m -> p c m", p=P)).then_inc(small_landed, 16)
            sp.dma_start(wiw[:, :].rearrange("p (c m) -> p c m", m=IDX_H),
                                         w[:, DS_COLS + DH:DS_COLS + DH + IDX_H].rearrange("(c p) m -> p c m", p=P)).then_inc(small_landed, 16)

        def pe_ds(pe):
            pe_norm(pe, W[8])
            pe_panels(pe, "ds.q")
            pe.wait_ge(small_landed, after(pe, small_landed, 48))
            for c in range(C):
                mm = pe.matmul(bank[4][:, 0:S], kiw[:, c * P:(c + 1) * P], W[0][:, c * S:(c + 1) * S],
                               start=c == 0, stop=c == C - 1)
            mm.then_inc(small_ready, 1)
            for tt in range(TT):
                for c in range(C):
                    mm = pe.matmul(bank[5][:, tt * IDX_H:(tt + 1) * IDX_H], W[0][:, c * S + tt * P:c * S + (tt + 1) * P],
                                   wiw[:, c * IDX_H:(c + 1) * IDX_H], start=c == 0, stop=c == C - 1)
            mm.then_inc(small_ready, 1)
            for n in ("k", "v", "qi"):
                pe_panels(pe, f"ds.{n}", fills=0)
            for t in (DS_Q, DS_K):
                pe_heads(pe, const("headones"), DS_T)
                pe_heads(pe, const("rot_head"), t)
            pe_heads(pe, const("rot_head"), DS_QI, chunks=5)
            pe.wait_ge(head_in, after(pe, head_in))
            for hd in range(IDX_H):
                r, c = head_rows(hd)
                if hd >= 2:
                    pe.wait_ge(idx_act, after(pe, idx_act))
                for qt in range(TT):
                    mm = pe.matmul(bank[4 + hd % 2][:, qt * S:(qt + 1) * S],
                                   DS_QI[r, c * S + qt * P:c * S + (qt + 1) * P], DS_QI[r, 4 * S:5 * S],
                                   start=True, stop=True)
                mm.then_inc(idx_ready, 1)
            pe.wait_ge(idx_act, after(pe, idx_act, 2))
            pe.wait_ge(bank_free, tiles_of("ds.qi"))

            def scores(hd):
                r, c = head_rows(hd)
                if hd >= 2:
                    pe.wait_ge(logit_ready, after(pe, logit_ready))
                for qt in range(TT):
                    mm = pe.matmul(bank[4 + hd % 2][:, qt * S:(qt + 1) * S], DS_Q[r, c * S + qt * P:c * S + (qt + 1) * P],
                                   DS_K[r, c * S:(c + 1) * S], start=True, stop=True)
                mm.then_inc(ds_z_ready, 1)

            def turn(hd):
                pe.wait_ge(att_ready, after(pe, att_ready))
                for qt in range(TT):
                    for st in range(TT):
                        mm = pe.transpose(bank[6 + hd % 2][:, st * S + qt * P:st * S + (qt + 1) * P],
                                          DS_L[hd % 2][:, qt * S + st * P:qt * S + (st + 1) * P], const("ident"))
                mm.then_inc(att_turned, 1)

            def output(hd):
                r, c = head_rows(hd)
                pe.wait_ge(att_turned_taken, after(pe, att_turned_taken))
                if hd % 2 == 0 and hd >= 4:
                    pe.wait_ge(heads_taken, after(pe, heads_taken))
                for st in range(TT):
                    mm = pe.matmul(bank[c % 2][r, 0:S], DS_V[:, st * D + hd * DH:st * D + (hd + 1) * DH],
                                   DS_PT[hd % 2][:, st * S:(st + 1) * S], start=st == 0, stop=st == TT - 1)
                mm.then_inc(heads_out, 1)

            scores(0)
            scores(1)
            for hd in range(H):
                turn(hd)
                if hd + 2 < H:
                    scores(hd + 2)
                if hd:
                    output(hd - 1)
            output(H - 1)
            pe.wait_ge(logit_ready, after(pe, logit_ready, 2))
            pe.wait_ge(heads_taken, after(pe, heads_taken, 2))
            pe_panels(pe, "ds.out")

        def act_ds(act):
            act_norm(act, X, W[8])
            act_panels(act, "ds.q")
            for n in ("k", "v", "qi"):
                act_panels(act, f"ds.{n}")
            for _ in range(2):
                act.wait_ge(head_taken, after(act, head_taken))
                act.activation(DS_T[:, :], DS_T[:, :], ACT.Sqrt).then_inc(root_ready, 1)
            for n in range(IDX_H):
                act.wait_ge(idx_ready, after(act, idx_ready))
                if n >= 2:
                    act.wait_ge(idx_taken, after(act, idx_taken))
                act.activation(IDX[n % 2], bank[4 + n % 2][:, :], ACT.Relu).then_inc(idx_act, 1)
            act.wait_ge(idx_taken, after(act, idx_taken, 2))

            def powers(hd):
                b = hd % 2
                act.wait_ge(logit_ready, after(act, logit_ready))
                for qt in range(TT):
                    l = DS_L[b][:, qt * S:(qt + 1) * S]
                    op = act.activation(l, l, ACT.Exp, bias=top[:, 4 * b + qt:4 * b + qt + 1],
                                        accum_out=top[:, 4 * b + 2 + qt:4 * b + 3 + qt])
                op.then_inc(exps_ready, 1)

            def turned(hd):
                act.wait_ge(att_turned, after(act, att_turned))
                if hd >= 2:
                    act.wait_ge(heads_out, after(act, heads_out))
                act.activation(DS_PT[hd % 2], bank[6 + hd % 2][:, :], ACT.Copy).then_inc(att_turned_taken, 1)

            powers(0)
            for hd in range(H):
                if hd + 1 < H:
                    powers(hd + 1)
                turned(hd)
            act.wait_ge(heads_out, after(act, heads_out, 2))
            act_panels(act, "ds.out")

        def dve_ds(dve, layer):
            dve_norm(dve, X, lambda c: vec("norm_mix", layer, c), W[0])
            dve_tiles(dve, "ds.q", take_copy(dve, DS_Q))
            dve.wait_ge(small_ready, after(dve, small_ready))
            dve.tensor_copy(DS_QI[:, 4 * S:5 * S], bank[4][:, 0:S])
            dve.wait_ge(small_ready, after(dve, small_ready))
            dve.tensor_scalar(WI[:, :], bank[5][:, 0:TT * IDX_H], IDX_H ** -0.5 * DH ** -0.5, None, ALU.mult)
            dve_tiles(dve, "ds.k", take_copy(dve, DS_K))
            dve_tiles(dve, "ds.v", take_tokens(dve, DS_V[:, :].rearrange("p (a m) -> p a m", m=D)))
            dve_tiles(dve, "ds.qi", take_copy(dve, DS_QI))

            def rope(t, chunks=C):
                n = chunks * S

                def over(name, k):
                    return const(name).unsqueeze(1).to_broadcast([P, k, S])

                def times_sin(s, ps):
                    k = (s.stop - s.start) // S
                    return dve.tensor_tensor(DS_T[:, s].rearrange("p (c t) -> p c t", t=S),
                                             ps.rearrange("p (c t) -> p c t", t=S), over("sin_head", k), ALU.mult)
                dve_heads(dve, times_sin, chunks)
                v = v3(t)[:, 0:chunks]
                dve.tensor_tensor(v, v, over("cos_head", chunks), ALU.mult).then_inc(dve_step, 1)
                dve.wait_ge(dve_step, after(dve, dve_step))
                return dve.tensor_tensor(t[:, 0:n], t[:, 0:n], DS_T[:, 0:n], ALU.add)

            for k, t in enumerate((DS_Q, DS_K)):
                dve.tensor_tensor(DS_T[:, :], t[:, :], t[:, :], ALU.mult).then_inc(head_in, 1)
                dve.wait_ge(head_in, after(dve, head_in))
                dve_heads(dve, lambda s, ps: dve.tensor_scalar(DS_T[:, s], ps, 1.0 / DH, EPS, ALU.mult, ALU.add)).then_inc(head_taken, 1)
                dve.wait_ge(head_taken, after(dve, head_taken))
                dve.wait_ge(root_ready, after(dve, root_ready))
                dve.reciprocal(DS_T[:, :], DS_T[:, :]).then_inc(dve_step, 1)
                dve.wait_ge(dve_step, after(dve, dve_step))
                dve.scalar_tensor_tensor(t[:, :], t[:, :], VEC3[:, k:k + 1], DS_T[:, :], ALU.mult, ALU.mult).then_inc(head_in, 1)
                dve.wait_ge(head_in, after(dve, head_in))
                rope(t).then_inc(dve_step, 1)
                dve.wait_ge(dve_step, after(dve, dve_step))
            dve.memset(SC, 0.0).then_inc(dve_step, 1)
            dve.wait_ge(dve_step, after(dve, dve_step))
            dve.memset(SEL, 0.0).then_inc(head_in, 1)
            dve.wait_ge(head_in, after(dve, head_in))
            rope(DS_QI, 5).then_inc(head_in, 1)
            dve.wait_ge(head_in, after(dve, head_in))
            for hd in range(IDX_H):
                dve.wait_ge(idx_act, after(dve, idx_act))
                for qt in range(TT):
                    o = SC[:, qt * S:(qt + 1) * S]
                    op = dve.scalar_tensor_tensor(o, IDX[hd % 2][:, qt * S:(qt + 1) * S],
                                                  WI[:, qt * IDX_H + hd:qt * IDX_H + hd + 1], o, ALU.mult, ALU.add)
                op.then_inc(idx_taken, 1)
                dve.wait_ge(idx_taken, after(dve, idx_taken))
            for qt in range(TT):
                for hh in range(2):
                    seen = qt * P + (hh + 1) * CHUNK
                    if seen < S:
                        op = dve.memset(SC[hh * DH:(hh + 1) * DH, qt * S + seen:(qt + 1) * S], NEG)
            op.then_inc(dve_step, 1)
            dve.wait_ge(dve_step, after(dve, dve_step))
            dve.tensor_copy(SC2, SC).then_inc(dve_step, 1)
            dve.wait_ge(dve_step, after(dve, dve_step))
            for n in range(TOPK // 8):
                for qt in range(TT):
                    op = dve.max(best[:, qt * 8:(qt + 1) * 8], SC2[:, qt * S:(qt + 1) * S])
                op.then_inc(dve_step, 1)
                dve.wait_ge(dve_step, after(dve, dve_step))
                for qt in range(TT):
                    o = SC2[:, qt * S:(qt + 1) * S]
                    op = dve.match_replace(o, best[:, qt * 8:(qt + 1) * 8], o, TAKEN)
                op.then_inc(dve_step, 1)
                dve.wait_ge(dve_step, after(dve, dve_step))
            dve.tensor_tensor(SEL, SC2, SC, ALU.is_equal).then_inc(dve_step, 1)
            dve.wait_ge(dve_step, after(dve, dve_step))
            dve.tensor_scalar(SEL, SEL, HIDE, None, ALU.mult).then_inc(dve_step, 1)
            dve.wait_ge(dve_step, after(dve, dve_step))

            def logits(hd):
                b = hd % 2
                dve.wait_ge(ds_z_ready, after(dve, ds_z_ready))
                if hd >= 2:
                    dve.wait_ge(att_turned, after(dve, att_turned))
                l = DS_L[b]
                dve.scalar_tensor_tensor(l, bank[4 + b][:, :], DH ** -0.5, SEL, ALU.mult, ALU.add).then_inc(dve_step, 1)
                dve.wait_ge(dve_step, after(dve, dve_step))
                t = top[:, 4 * b:4 * b + 2]
                dve.tensor_reduce(t, l.rearrange("p (a s) -> p a s", s=S), AX_X, ALU.max).then_inc(dve_step, 1)
                dve.wait_ge(dve_step, after(dve, dve_step))
                dve.tensor_scalar(t, t, -1.0, None, ALU.mult).then_inc(logit_ready, 1)
                dve.wait_ge(logit_ready, after(dve, logit_ready))

            def weights(hd):
                b = hd % 2
                dve.wait_ge(exps_ready, after(dve, exps_ready))
                t = top[:, 4 * b + 2:4 * b + 4]
                dve.reciprocal(t, t).then_inc(dve_step, 1)
                dve.wait_ge(dve_step, after(dve, dve_step))
                for qt in range(TT):
                    l = DS_L[b][:, qt * S:(qt + 1) * S]
                    op = dve.tensor_scalar(l, l, t[:, qt:qt + 1], None, ALU.mult)
                op.then_inc(att_ready, 1)
                dve.wait_ge(att_ready, after(dve, att_ready))

            def store(hd):
                dve.wait_ge(heads_out, after(dve, heads_out, 2))
                c = hd // 2
                dve.tensor_copy(DS_O[:, c * S:(c + 1) * S], bank[c % 2][:, 0:S]).then_inc(heads_taken, 1)
                dve.wait_ge(heads_taken, after(dve, heads_taken))

            logits(0)
            for hd in range(H):
                if hd + 1 < H:
                    logits(hd + 1)
                weights(hd)
                if hd % 2 == 0 and hd:
                    store(hd - 1)
            store(H - 1)
            dve.wait_ge(att_turned, after(dve, att_turned, 2))
            split(dve, DS_O)
            dve_tiles(dve, "ds.out", take_residual(dve, X))

        ROWS, ROWS2, ROWS3, XROWS = W[0], W[1][:, 0:CF_W], W[1][:, CF_W:CF_W + P], W[2]
        OUTROWS = W[2]

        def table_view(name):
            t = a[name]
            if name == "rw_mix":
                return t.rearrange("a b d -> (a b) d")
            if name == "rw_r_k":
                return t.rearrange("a h d -> a (h d)")
            if name == "b_ada_2":
                return t.rearrange("l (n d) -> (l n) d", d=D)
            if name in ("norm_g_2", "conv_a_w_2", "conf_dw_2"):
                return t.rearrange("l k d -> (l k) d")
            if name in ("c_ctx_2", "final_g_2"):
                return t.rearrange("(a d) -> a d", a=1)
            return t

        def sp_setup(sp):
            sp.dma_start(cst[:, :], a["const"]).then_inc(const_landed, 16)
            sp.dma_start(XROWS[:, :].rearrange("p (a d) -> p a d", d=D),
                                          a["x"][0].rearrange("(a p) d -> p a d", p=P)).then_inc(x_rows_landed, 16)
            for name, at, k in VEC_ROWS:
                sp.dma_start(ROWS[at:at + k, 0:D], table_view(name)).then_inc(rows_landed, 16)
            for name, at, k in VEC2_ROWS:
                sp.dma_start(ROWS2[at:at + k, :], table_view(name)).then_inc(rows_landed, 16)
            for half in range(2):
                o = slice(half * DH, half * DH + DH)
                sp.dma_start(ROWS3[0:1, o], a["ds_q_norm"]).then_inc(rows_landed, 16)
                sp.dma_start(ROWS3[1:2, o], a["ds_k_norm"]).then_inc(rows_landed, 16)
                sp.dma_start(ROWS3[2:10, o], a["lam_p_2"].rearrange("l k d -> (l k) d")).then_inc(rows_landed, 16)
            sp.dma_start(ROWS3[10:12, :], a["subln_g_2"]).then_inc(rows_landed, 16)

        N_TABLES = len(VEC_ROWS) + len(VEC2_ROWS) + 7

        def pe_turn_in(pe, src):
            for k in range(4):
                for c in (2 * k, 2 * k + 1):
                    for tt in range(TT):
                        o = (c % 2) * S + tt * P
                        mm = pe.transpose(bank[k][:, o:o + P], src[:, tt * D + c * P:tt * D + (c + 1) * P], const("ident"))
                mm.then_inc(x_turned, 1)

        def pe_setup(pe):
            pe.wait_ge(const_landed, after(pe, const_landed, 16))
            pe.wait_ge(x_rows_landed, after(pe, x_rows_landed, 16))
            pe_turn_in(pe, XROWS)
            pe.wait_ge(rows_landed, after(pe, rows_landed, 16 * N_TABLES))
            for c in range(C):
                mm = pe.transpose(bank[4][:, c * NV:(c + 1) * NV], ROWS[0:NV, c * P:(c + 1) * P], const("ident")[0:NV, 0:NV])
            mm.then_inc(vec_turned, 1)
            for c in range(2):
                pe.transpose(bank[5][:, c * NV2:(c + 1) * NV2], ROWS2[0:NV2, c * P:(c + 1) * P], const("ident")[0:NV2, 0:NV2])
            pe.transpose(bank[5][:, 2 * NV2:2 * NV2 + 12], ROWS3[0:12, :], const("ident")[0:12, 0:12]).then_inc(vec_turned, 1)
            pe.wait_ge(consts_set, after(pe, consts_set))

        def dve_turn_in(dve, dst):
            for k in range(4):
                dve.wait_ge(x_turned, after(dve, x_turned))
                dve.tensor_copy(dst[:, k * 2 * S:(k + 1) * 2 * S], bank[k][:, :]).then_inc(x_ready, 1)
                dve.wait_ge(x_ready, after(dve, x_ready))

        def dve_setup(dve):
            dve.memset(eps[:, 0:1], EPS)
            dve.memset(ones[:, :], 1.0).then_inc(consts_set, 1)
            dve.wait_ge(consts_set, after(dve, consts_set))
            dve_turn_in(dve, X)
            dve.wait_ge(vec_turned, after(dve, vec_turned))
            dve.tensor_copy(VEC[:, :], bank[4][:, 0:C * NV]).then_inc(vec_ready, 1)
            dve.wait_ge(vec_ready, after(dve, vec_ready))
            dve.wait_ge(vec_turned, after(dve, vec_turned))
            dve.tensor_copy(VEC2[:, :], bank[5][:, 0:2 * NV2])
            dve.tensor_copy(VEC3[:, :], bank[5][:, 2 * NV2:2 * NV2 + 12]).then_inc(vec_ready, 1)
            dve.wait_ge(vec_ready, after(dve, vec_ready))

        def act_input(act):
            act.wait_ge(consts_set, after(act, consts_set))
            act.wait_ge(vec_ready, after(act, vec_ready, 2))
            act.wait_ge(x_ready, after(act, x_ready, 4))

        def pe_turn_out(pe, src):
            pe.wait_ge(turn_in, after(pe, turn_in))
            for k in range(4):
                tt, half = k // 2, k % 2
                for q in range(4):
                    c = half * 4 + q
                    mm = pe.transpose(bank[k][:, q * P:(q + 1) * P], src[:, c * S + tt * P:c * S + (tt + 1) * P], const("ident"))
                mm.then_inc(turned_out, 1)

        def dve_turn_out(dve):
            for k in range(4):
                dve.wait_ge(turned_out, after(dve, turned_out))
                dve.tensor_copy(OUTROWS[:, k * 512:(k + 1) * 512], bank[k][:, :]).then_inc(out_ready, 1)
                dve.wait_ge(out_ready, after(dve, out_ready))

        def sp_out(sp):
            for tt in range(TT):
                sp.wait_ge(out_ready, after(sp, out_ready, 2))
                sp.dma_start(out[0, tt * P:(tt + 1) * P, :], OUTROWS[:, tt * D:(tt + 1) * D]).then_inc(out_landed, 16)
            sp.wait_ge(out_landed, after(sp, out_landed, 16 * TT))

        STREAM = {"x": X, "c": CTX}
        MOD = {s: sb(f"mod_{s}", N_MOD * C) for s in "xc"}
        GAIN = {s: sb(f"gain_{s}", 3 * C) for s in "xc"}
        both = sb("both", N_MOD * C * 2)
        LAM = sb("LAM", 8)
        cond = sb("cond", C * 2)
        lam_init = [0.8 - 0.6 * float(np.exp(-0.3 * l)) for l in range(D2)]

        def act_cond(act):
            for n, name in enumerate(("c_2", "c_ctx_2")):
                op = act.activation(cond[:, :].rearrange("p (c n) -> p c n", n=2)[:, :, n:n + 1],
                                    VEC_v[:, :, VAT[name]:VAT[name] + 1], ACT.Silu)
            op.then_inc(cond_ready, 1)

        def act_ada(act, l):
            act_panels(act, f"ada{l}")
            act.wait_ge(lam_sums, after(act, lam_sums))
            act.activation(LAM[:, 0:2], bank[5][:, 0:2], ACT.Exp).then_inc(lam_exp, 1)

        def pe_ada(pe, l):
            pe_panels(pe, f"ada{l}", fills=0 if l else 1)
            pe.wait_ge(lam_in, after(pe, lam_in))
            pe.matmul(bank[5][:, 0:2], const("headones"), LAM[:, 2:4], start=True, stop=True).then_inc(lam_sums, 1)

        def dve_ada(dve, l):
            if l == 0:
                dve.wait_ge(cond_ready, after(dve, cond_ready))
                split(dve, cond, COND_T)

            def take(s, j, banks):
                dve.tensor_copy(both[:, bass.ds(s * 2, 2)], banks[0][:, 0:2]).then_inc(bank_free, 1)

            dve_tiles(dve, f"ada{l}", take)
            b4 = both[:, :].rearrange("p (n c s) -> p n c s", c=C, s=2)
            row = VAT["b_ada_2"] + l * N_MOD
            bias = VEC_v[:, :, row:row + N_MOD].rearrange("p c n -> p n c")
            for k, s in enumerate("xc"):
                m = MOD[s][:, :]
                dve.tensor_tensor(m.rearrange("p (n c) -> p n c", c=C), b4[:, :, :, k], bias, ALU.add).then_inc(dve_step, 1)
                dve.wait_ge(dve_step, after(dve, dve_step))
                for n in range(3):
                    g = VAT["norm_g_2"] + 3 * l + n
                    dve.scalar_tensor_tensor(
                        GAIN[s][:, n * C:(n + 1) * C], m[:, (3 * n + 1) * C:(3 * n + 2) * C], 1.0,
                        VEC_v[:, :, g], ALU.add, ALU.mult).then_inc(dve_step, 1)
                    dve.wait_ge(dve_step, after(dve, dve_step))
                for n in (0, 2):
                    o = m[:, (3 * n + 2) * C:(3 * n + 3) * C]
                    dve.tensor_scalar(o, o, 0.5, None, ALU.mult).then_inc(dve_step, 1)
                    dve.wait_ge(dve_step, after(dve, dve_step))
            v = VEC3[:, 2 + 4 * l:6 + 4 * l].rearrange("p (a b) -> p a b", b=2)
            dve.tensor_tensor(LAM[:, 2:4], v[:, :, 0], v[:, :, 1], ALU.mult).then_inc(lam_in, 1)
            dve.wait_ge(lam_in, after(dve, lam_in))
            dve.wait_ge(lam_exp, after(dve, lam_exp))
            dve.tensor_tensor(LAM[:, 4:5], LAM[:, 1:2], LAM[:, 0:1], ALU.subtract).then_inc(dve_step, 1)
            dve.wait_ge(dve_step, after(dve, dve_step))
            dve.tensor_scalar(LAM[:, 5:6], LAM[:, 4:5], -lam_init[l], None, ALU.add).then_inc(dve_step, 1)
            dve.wait_ge(dve_step, after(dve, dve_step))

        def mod(s, n):
            return lambda c: MOD[s][:, n * C + c:n * C + c + 1]

        def mod_gate(s, n):
            return MOD[s][:, n * C:(n + 1) * C]

        def gain(s, n):
            return lambda c: GAIN[s][:, n * C + c:n * C + c + 1]

        def dve_ffn2(dve, name, s, n):
            dve_ffn(dve, name, STREAM[s], gain(s, n), mod(s, 3 * n), mod_gate(s, 3 * n + 2))

        AB = sb("AB", 10 * S, at=w_at[0])
        D_ = W[2][:, 0:4 * S]
        LN_SQ = W[2][:, 4 * S:6 * S]
        LN_STD = W[2][:, 6 * S:7 * S]
        MERGED = W[3]
        DQ, DK = W[4][:, 0:4 * S], W[4][:, 4 * S:8 * S]
        KC, VC = VF[:, 0:4 * S], VF[:, 4 * S:8 * S]
        DV, DO = W[5][:, 0:4 * S], W[5][:, 4 * S:8 * S]
        DP = [[W[6][:, (2 * b + m) * HS:(2 * b + m + 1) * HS] for m in range(2)] for b in range(2)]
        DAT = [W[7][:, b * HS:(b + 1) * HS] for b in range(2)]
        da_top = sb("da_top", 8)
        T2 = W[7][:, 2 * HS:4 * HS]
        V_TOK = W[8][:, 0:HS]
        SGW, SGWT = W[8][:, HS:2 * HS], W[8][:, 2 * HS:3 * HS]
        SGB = W[8][:, 3 * HS:3 * HS + 2 * P]
        PADW = S + CF_K - 1
        PAD = AB[:, 0:2 * PADW]

        def v2vec(name, row, c):
            o = V2AT[name] + row
            return VEC2_v[:, c, o:o + 1]

        def sp_gated_unit(sp, l):
            sp.wait_ge(sgu_free, after(sp, sgu_free))
            sp.dma_start(SGW.rearrange("p (g q) -> p g q", q=P),
                                       a["sgu_w_2"][l].rearrange("g p q -> p g q")).then_inc(sgu_landed, 16)
            for g in range(SG_G):
                sp.dma_start(SGB[DH * (g % 2):DH * (g % 2) + DH, (g // 2) * P:(g // 2 + 1) * P],
                                           a["sgu_b_2"][l, g].partition_broadcast(DH)).then_inc(sgu_landed, 16)

        def keys_of(s):
            return [(DK, DV), (KC, VC)] if s == "x" else [(KC, VC)]

        def pe_total(pe, src, chunks=2):
            pe.wait_ge(head_in, after(pe, head_in))
            for c in range(chunks):
                mm = pe.matmul(bank[4][:, 0:S], ones[:, :], src[:, c * S:(c + 1) * S], start=c == 0, stop=c == chunks - 1)
            mm.then_inc(head_sums, 1)

        def dve_layer_norm(dve, t):
            dve.wait_ge(head_sums, after(dve, head_sums))
            for c in range(2):
                o = t[:, c * S:(c + 1) * S]
                op = dve.scalar_tensor_tensor(o, bank[4][:, 0:S], -1.0 / CF_W, o, ALU.mult, ALU.add)
            op.then_inc(dve_step, 1)
            dve.wait_ge(dve_step, after(dve, dve_step))
            dve.tensor_tensor(LN_SQ, t, t, ALU.mult).then_inc(head_in, 1)
            dve.wait_ge(head_in, after(dve, head_in))
            dve.wait_ge(head_sums, after(dve, head_sums))
            dve.tensor_scalar(LN_STD, bank[4][:, 0:S], 1.0 / CF_W, EPS, ALU.mult, ALU.add).then_inc(head_taken, 1)
            dve.wait_ge(head_taken, after(dve, head_taken))
            dve.wait_ge(root_ready, after(dve, root_ready))
            dve.reciprocal(LN_STD, LN_STD).then_inc(dve_step, 1)
            dve.wait_ge(dve_step, after(dve, dve_step))
            v = t.rearrange("p (c t) -> p c t", t=S)
            return dve.tensor_tensor(v, v, LN_STD.unsqueeze(1).to_broadcast([P, 2, S]), ALU.mult)

        def act_root(act, t):
            act.wait_ge(head_taken, after(act, head_taken))
            act.activation(t, t, ACT.Sqrt).then_inc(root_ready, 1)

        UNITS = [(h, qt) for h in range(DA_H) for qt in range(TT)]

        def pe_diff(pe, s):
            parts = keys_of(s)
            nkt = TT * len(parts)

            def scores(u):
                h, qt = UNITS[u]
                if u >= 2:
                    pe.wait_ge(da_exp, after(pe, da_exp))
                for m in range(2):
                    r = slice(DA_D * m, DA_D * m + DA_D)
                    for k, (keys, _) in enumerate(parts):
                        mm = pe.matmul(bank[(u % 2) * 2 + m][:, k * S:(k + 1) * S], DQ[r, h * S + qt * P:h * S + (qt + 1) * P],
                                       keys[r, h * S:(h + 1) * S], start=True, stop=True)
                mm.then_inc(da_scores, 1)

            def turn(u):
                pe.wait_ge(da_mix, after(pe, da_mix))
                for kt in range(nkt):
                    mm = pe.transpose(bank[4 + u % 2][:, kt * P:(kt + 1) * P], DP[u % 2][0][:, kt * P:(kt + 1) * P], const("ident"))
                mm.then_inc(da_turned, 1)

            def output(u):
                h, qt = UNITS[u]
                pe.wait_ge(da_copied, after(pe, da_copied))
                if u >= 2:
                    pe.wait_ge(da_stored, after(pe, da_stored))
                for kt in range(nkt):
                    v = parts[kt // TT][1]
                    o = (kt % TT) * DA_W + h * P
                    mm = pe.matmul(bank[6 + u % 2][:, 0:P], v[:, o:o + P], DAT[u % 2][:, kt * P:(kt + 1) * P],
                                   start=kt == 0, stop=kt == nkt - 1)
                mm.then_inc(da_out, 1)

            scores(0)
            scores(1)
            for u in range(len(UNITS)):
                turn(u)
                if u + 2 < len(UNITS):
                    scores(u + 2)
                if u:
                    output(u - 1)
            output(len(UNITS) - 1)
            pe.wait_ge(da_exp, after(pe, da_exp, 2))
            pe.wait_ge(da_stored, after(pe, da_stored, 2))
            pe_heads(pe, ones[:, :], W[6], chunks=4)

        def act_diff(act, s):
            nk = S * len(keys_of(s))

            def powers(u):
                b = u % 2
                act.wait_ge(da_max, after(act, da_max))
                for m in range(2):
                    op = act.activation(DP[b][m][:, 0:nk], bank[2 * b + m][:, 0:nk], ACT.Exp, scale=DA_D ** -0.5,
                                        bias=da_top[:, 4 * b + m:4 * b + m + 1],
                                        accum_out=da_top[:, 4 * b + 2 + m:4 * b + 3 + m])
                op.then_inc(da_exp, 1)

            def copied(u):
                act.wait_ge(da_turned, after(act, da_turned))
                if u >= 2:
                    act.wait_ge(da_out, after(act, da_out))
                act.activation(DAT[u % 2][:, 0:nk], bank[4 + u % 2][:, 0:nk], ACT.Copy).then_inc(da_copied, 1)

            powers(0)
            for u in range(len(UNITS)):
                if u + 1 < len(UNITS):
                    powers(u + 1)
                copied(u)
            act.wait_ge(da_out, after(act, da_out, 2))
            act_root(act, W[6][:, 0:4 * S])

        def dve_diff(dve, s, l):
            nk = S * len(keys_of(s))

            def maxima(u):
                b = u % 2
                dve.wait_ge(da_scores, after(dve, da_scores))
                t = da_top[:, 4 * b:4 * b + 2]
                for m in range(2):
                    op = dve.tensor_reduce(t[:, m:m + 1], bank[2 * b + m][:, 0:nk], AX_X, ALU.max)
                op.then_inc(dve_step, 1)
                dve.wait_ge(dve_step, after(dve, dve_step))
                dve.tensor_scalar(t, t, -(DA_D ** -0.5), None, ALU.mult).then_inc(da_max, 1)
                dve.wait_ge(da_max, after(dve, da_max))

            def mix(u):
                b = u % 2
                dve.wait_ge(da_exp, after(dve, da_exp))
                t = da_top[:, 4 * b + 2:4 * b + 4]
                dve.reciprocal(t, t).then_inc(dve_step, 1)
                dve.wait_ge(dve_step, after(dve, dve_step))
                dve.tensor_scalar(t[:, 1:2], t[:, 1:2], LAM[:, 5:6], None, ALU.mult).then_inc(dve_step, 1)
                dve.wait_ge(dve_step, after(dve, dve_step))
                p0, p1 = (x[:, 0:nk] for x in DP[b])
                dve.tensor_scalar(p0, p0, t[:, 0:1], None, ALU.mult).then_inc(dve_step, 1)
                dve.wait_ge(dve_step, after(dve, dve_step))
                dve.scalar_tensor_tensor(p0, p1, t[:, 1:2], p0, ALU.mult, ALU.add).then_inc(da_mix, 1)
                dve.wait_ge(da_mix, after(dve, da_mix))

            def store(u):
                h, qt = UNITS[u]
                dve.wait_ge(da_out, after(dve, da_out))
                dve.tensor_copy(DO[:, h * S + qt * P:h * S + (qt + 1) * P], bank[6 + u % 2][:, 0:P]).then_inc(da_stored, 1)
                dve.wait_ge(da_stored, after(dve, da_stored))

            maxima(0)
            for u in range(len(UNITS)):
                if u + 1 < len(UNITS):
                    maxima(u + 1)
                mix(u)
                if u:
                    store(u - 1)
            store(len(UNITS) - 1)
            t = W[6][:, 0:4 * S]
            dve.tensor_tensor(t, DO, DO, ALU.mult).then_inc(head_in, 1)
            dve.wait_ge(head_in, after(dve, head_in))
            dve_heads(dve, lambda c, ps: dve.tensor_scalar(t[:, c], ps, 1.0 / P, EPS, ALU.mult, ALU.add), 4).then_inc(head_taken, 1)
            dve.wait_ge(head_taken, after(dve, head_taken))
            dve.wait_ge(root_ready, after(dve, root_ready))
            dve.reciprocal(t, t).then_inc(dve_step, 1)
            dve.wait_ge(dve_step, after(dve, dve_step))
            dve.tensor_scalar(t, t, 1.0 - lam_init[l], None, ALU.mult).then_inc(dve_step, 1)
            dve.wait_ge(dve_step, after(dve, dve_step))
            dve.scalar_tensor_tensor(DO, DO, VEC3[:, 10 + l:11 + l], t, ALU.mult, ALU.mult).then_inc(dve_step, 1)
            dve.wait_ge(dve_step, after(dve, dve_step))

        def branch_parts(b):
            c0, width = BRANCH[b]
            return tuple(t[:, c0 * S:c0 * S + width // P * S] for t in (BRH, BRL))

        def pe_mix(pe, l, s):
            pre = f"mix{l}{s}"
            pe_norm(pe, W[8])
            pe_panels(pe, f"{pre}.k")
            pe_panels(pe, f"{pre}.v", fills=0)
            if (l, s) not in FULL:
                return
            for n in ("q", "ab", "d"):
                pe_panels(pe, f"{pre}.{n}", fills=0)
            if s == "x":
                pe_heads(pe, const("rot_axial"), DQ, chunks=4)
                pe_heads(pe, const("rot_axial"), DK, chunks=4)
            pe_total(pe, AB[:, 8 * S:10 * S])
            pe_total(pe, LN_SQ)
            pe.wait_ge(sgu_landed, after(pe, sgu_landed, 16 * (1 + SG_G)))
            for g in range(SG_G):
                mm = pe.transpose(bank[5][:, g * P:(g + 1) * P], SGW[:, g * P:(g + 1) * P], const("ident"))
            mm.then_inc(sgu_turned, 1)
            pe.wait_ge(head_in, after(pe, head_in))
            for tt in range(TT):
                for c in range(2):
                    mm = pe.transpose(bank[6][:, tt * S + c * P:tt * S + (c + 1) * P],
                                      AB[:, (8 + c) * S + tt * P:(8 + c) * S + (tt + 1) * P], const("ident"))
            mm.then_inc(sgu_turned, 1)
            pe.wait_ge(sgu_copied, after(pe, sgu_copied, 2))
            for g in range(SG_G):
                for tt in range(TT):
                    mm = pe.matmul(bank[4 + 3 * (g // 2)][DH * (g % 2):DH * (g % 2) + DH, tt * P:(tt + 1) * P],
                                   V_TOK[:, tt * SG_W + g * DH:tt * SG_W + (g + 1) * DH], SGWT[:, g * P:(g + 1) * P],
                                   start=True, stop=True)
            mm.then_inc(sgu_out, 1)
            pe.wait_ge(bank_free, tiles_of(f"{pre}.d"))
            pe_diff(pe, s)
            pe_total(pe, D_)
            pe_total(pe, LN_SQ)
            pe.wait_ge(operand_ready, after(pe, operand_ready, 4))
            for b in BRANCH:
                pe_panels(pe, f"{pre}.{b}out", fills=0)
            pe_panels(pe, f"{pre}.o")

        def act_mix(act, l, s):
            pre = f"mix{l}{s}"
            act_norm(act, STREAM[s], W[8])
            sgu_free_by_pe = (l, s) in FULL
            act_panels(act, f"{pre}.k")
            act_panels(act, f"{pre}.v")
            if not sgu_free_by_pe:
                return
            for n in ("q", "ab", "d"):
                act_panels(act, f"{pre}.{n}")
            act.wait_ge(bank_free, tiles_of(f"{pre}.d"))
            t = AB[:, 6 * S:10 * S]
            act.activation(t, t, ACT.Gelu_apprx_tanh).then_inc(glu_ready, 1)
            t = D_[:, 2 * S:4 * S]
            act.activation(t, t, ACT.Sigmoid).then_inc(glu_ready, 1)
            act_root(act, LN_STD)
            act.wait_ge(sgu_turned, after(act, sgu_turned))
            act.activation(SGWT, bank[5][:, :], ACT.Copy).then_inc(sgu_copied, 1)
            act.wait_ge(sgu_turned, after(act, sgu_turned))
            act.activation(V_TOK, bank[6][:, :], ACT.Copy).then_inc(sgu_copied, 1)
            act_diff(act, s)
            act_root(act, LN_STD)
            act.wait_ge(conf_ready, after(act, conf_ready))
            for c in range(2):
                o = D_[:, c * S:(c + 1) * S]
                op = act.activation(o, o, ACT.Silu, scale=v2vec("conf_ln_g_2", l, c), bias=v2vec("conf_ln_b_2", l, c))
            op.then_inc(conf_act, 1)
            for b in BRANCH:
                def gate(st, j, k, g=G[f"{pre}.{b}out"]):
                    if k == 1:
                        n = after(act, merged_step)
                        if n is not None:
                            act.wait_ge(merged_step, n)
                        act.activation(silu[j % 2][:, :], bank[(g.t0 + j * g.tiles + 1) % RING][:, 0:S], ACT.Sigmoid).then_inc(silu_ready, 1)
                gate.per = {merged_step: 2}
                act_panels(act, f"{pre}.{b}out", gate)
            act_panels(act, f"{pre}.o")

        def dve_mix(dve, l, s):
            pre = f"mix{l}{s}"
            k_dst, v_dst = (KC, VC) if s == "c" else (DK, DV)
            dve_norm(dve, STREAM[s], gain(s, 1), W[7], mod(s, 3))
            if (l, s) in FULL:
                dve.memset(LAM[:, 6:7], 0.0).then_inc(dve_step, 1)
                dve.wait_ge(dve_step, after(dve, dve_step))
                dve.memset(LAM[:, 7:8], 0.0).then_inc(sgu_free, 1)
                dve.wait_ge(sgu_free, after(dve, sgu_free))
            dve_tiles(dve, f"{pre}.k", take_copy(dve, k_dst))
            dve_tiles(dve, f"{pre}.v", take_tokens(dve, v_dst.rearrange("p (a m) -> p a m", m=DA_W)))
            if (l, s) not in FULL:
                return
            dve_tiles(dve, f"{pre}.q", take_copy(dve, DQ))
            dve_tiles(dve, f"{pre}.ab", take_copy(dve, AB))
            dve_tiles(dve, f"{pre}.d", take_copy(dve, D_))
            if s == "x":
                def over(name, k):
                    return const(name).unsqueeze(1).to_broadcast([P, k, S])

                for t in (DQ, DK):
                    rot = W[6][:, 0:4 * S]

                    def times_sin(c, ps):
                        return dve.tensor_tensor(rot[:, c].rearrange("p (c t) -> p c t", t=S),
                                                 ps.rearrange("p (c t) -> p c t", t=S), over("sin_axial", 2), ALU.mult)
                    dve.memset(da_top[:, 0:1], 0.0).then_inc(head_in, 1)
                    dve.wait_ge(head_in, after(dve, head_in))
                    dve_heads(dve, times_sin, 4)
                    v = t.rearrange("p (c t) -> p c t", t=S)
                    dve.tensor_tensor(v, v, over("cos_axial", 4), ALU.mult).then_inc(dve_step, 1)
                    dve.wait_ge(dve_step, after(dve, dve_step))
                    dve.tensor_tensor(t, t, rot, ALU.add).then_inc(dve_step, 1)
                    dve.wait_ge(dve_step, after(dve, dve_step))
            bg, cg, xin = (AB[:, 2 * k * S:2 * (k + 1) * S] for k in range(3))
            y = T2[:, 0:2 * S]
            dve.tensor_tensor(xin, cg, xin, ALU.mult).then_inc(dve_step, 1)
            dve.wait_ge(dve_step, after(dve, dve_step))
            for c in range(2):
                i, o = xin[:, c * S:(c + 1) * S], y[:, c * S:(c + 1) * S]
                w = [v2vec("conv_a_w_2", CA_K * l + k, c) for k in range(CA_K)]
                dve.tensor_scalar(o, i, w[1], None, ALU.mult).then_inc(dve_step, 1)
                dve.wait_ge(dve_step, after(dve, dve_step))
                dve.scalar_tensor_tensor(o[:, 1:S], i[:, 0:S - 1], w[0], o[:, 1:S], ALU.mult, ALU.add).then_inc(dve_step, 1)
                dve.wait_ge(dve_step, after(dve, dve_step))
                dve.scalar_tensor_tensor(o[:, 0:S - 1], i[:, 1:S], w[2], o[:, 0:S - 1], ALU.mult, ALU.add).then_inc(dve_step, 1)
                dve.wait_ge(dve_step, after(dve, dve_step))
            dve.tensor_tensor(y, y, bg, ALU.mult).then_inc(dve_step, 1)
            dve.wait_ge(dve_step, after(dve, dve_step))
            split(dve, y, branch_parts("a"))
            dve.wait_ge(glu_ready, after(dve, glu_ready))
            u, v = AB[:, 6 * S:8 * S], AB[:, 8 * S:10 * S]
            dve.memset(da_top[:, 0:1], 0.0).then_inc(head_in, 1)
            dve.wait_ge(head_in, after(dve, head_in))
            dve_layer_norm(dve, v).then_inc(head_in, 1)
            dve.wait_ge(head_in, after(dve, head_in))
            dve.wait_ge(sgu_out, after(dve, sgu_out))
            for k in range(2):
                o = y[:, k * S:(k + 1) * S].rearrange("p (n t) -> p n t", t=P)
                dve.tensor_tensor(
                    o, bank[4 + 3 * k][:, 0:S].rearrange("p (n t) -> p n t", t=P),
                    SGB[:, k * P:(k + 1) * P].unsqueeze(1).to_broadcast([P, TT, P]), ALU.add).then_inc(dve_step, 1)
                dve.wait_ge(dve_step, after(dve, dve_step))
            dve.tensor_tensor(y, y, u, ALU.mult).then_inc(dve_step, 1)
            dve.wait_ge(dve_step, after(dve, dve_step))
            split(dve, y, branch_parts("b"))
            dve_diff(dve, s, l)
            split(dve, DO, branch_parts("c"))
            dve.wait_ge(glu_ready, after(dve, glu_ready))
            pad = PAD.rearrange("p (c t) -> p c t", t=PADW)
            edge = CF_K // 2
            dve.memset(pad[:, :, 0:edge], 0.0)
            dve.memset(pad[:, :, edge + S:PADW], 0.0)
            z = D_.rearrange("p (c t) -> p c t", t=S)
            dve.tensor_tensor(pad[:, :, edge:edge + S], z[:, 0:2], z[:, 2:4], ALU.mult).then_inc(dve_step, 1)
            dve.wait_ge(dve_step, after(dve, dve_step))
            acc = D_[:, 0:2 * S]
            for k in range(CF_K):
                for c in range(2):
                    i, o, w = pad[:, c, k:k + S], acc[:, c * S:(c + 1) * S], v2vec("conf_dw_2", CF_K * l + k, c)
                    if k == 0:
                        op = dve.tensor_scalar(o, i, w, v2vec("conf_db_2", l, c), ALU.mult, ALU.add)
                    else:
                        op = dve.scalar_tensor_tensor(o, i, w, o, ALU.mult, ALU.add)
                if k < CF_K - 1:
                    op.then_inc(dve_step, 1)
                    dve.wait_ge(dve_step, after(dve, dve_step))
            op.then_inc(head_in, 1)
            dve.wait_ge(head_in, after(dve, head_in))
            dve_layer_norm(dve, acc).then_inc(conf_ready, 1)
            dve.wait_ge(conf_ready, after(dve, conf_ready))
            dve.wait_ge(conf_act, after(dve, conf_act))
            split(dve, acc, branch_parts("d"))
            for b in BRANCH:
                def take(st, j, banks, first=b == "a"):
                    dve.wait_ge(silu_ready, after(dve, silu_ready))
                    o = MERGED[:, bass.ds(st * S, S)]
                    if first:
                        dve.tensor_tensor(o, silu[j % 2][:, :], banks[0][:, 0:S], ALU.mult).then_inc(bank_free, 2)
                        dve.wait_ge(bank_free, after(dve, bank_free, 2))
                        dve.memset(hid[:, 0:2], 0.0).then_inc(merged_step, 1)
                        dve.wait_ge(merged_step, after(dve, merged_step))
                    else:
                        dve.tensor_tensor(hid[:, :], silu[j % 2][:, :], banks[0][:, 0:S], ALU.mult).then_inc(bank_free, 2)
                        dve.wait_ge(bank_free, after(dve, bank_free, 2))
                        dve.tensor_tensor(o, o, hid[:, :], ALU.add).then_inc(merged_step, 1)
                        dve.wait_ge(merged_step, after(dve, merged_step))
                name = f"{pre}.{b}out"
                counts.start(dve, bank_free, G[name].t0)
                dve_tiles(dve, name, take, {silu_ready: 1, bank_free: 2, merged_step: 1})
            split(dve, MERGED)
            dve_tiles(dve, f"{pre}.o", take_residual(dve, STREAM[s], mod_gate(s, 5)))

        CROWS = W[6]

        def sp_ctx(sp):
            sp.dma_start(CROWS[:, :].rearrange("p (a d) -> p a d", d=D),
                                       a["ctx_2"][0].rearrange("(a p) d -> p a d", p=P)).then_inc(ctx_landed, 16)

        def act_second(act):
            act_cond(act)
            act_ada(act, 0)
            act_ffn(act, "f10x", X)
            act.wait_ge(x_ready, after(act, x_ready, 4))
            act_ffn(act, "f10c", CTX)
            act.wait_ge(bank_free, tiles_of("f10c.down"))
            act_mix(act, 0, "c")
            act.wait_ge(bank_free, tiles_of("mix0c.o"))
            act_ffn(act, "f20c", CTX)
            act.wait_ge(bank_free, tiles_of("f20c.down"))
            act_mix(act, 0, "x")
            act.wait_ge(bank_free, tiles_of("mix0x.o"))
            act_ffn(act, "f20x", X)
            act_ada(act, 1)
            act_ffn(act, "f11x", X)
            act.wait_ge(bank_free, tiles_of("f11x.down"))
            act_ffn(act, "f11c", CTX)
            act.wait_ge(bank_free, tiles_of("f11c.down"))
            act_mix(act, 1, "c")
            act_mix(act, 1, "x")
            act.wait_ge(bank_free, tiles_of("mix1x.o"))
            act_ffn(act, "f21x", X)
            act.wait_ge(bank_free, tiles_of("f21x.down"))
            act_norm(act, X, W[8])

        def pe_second(pe):
            pe.wait_ge(bank_free, tiles_of("ffn3.down"))
            pe.wait_ge(ctx_landed, after(pe, ctx_landed, 16))
            pe_turn_in(pe, CROWS)
            pe.wait_ge(x_ready, after(pe, x_ready, 4))
            pe_ada(pe, 0)
            pe_ffn(pe, "f10x")
            pe_ffn(pe, "f10c")
            pe_mix(pe, 0, "c")
            pe_ffn(pe, "f20c")
            pe_mix(pe, 0, "x")
            pe_ffn(pe, "f20x")
            pe_ada(pe, 1)
            pe_ffn(pe, "f11x")
            pe_ffn(pe, "f11c")
            pe_mix(pe, 1, "c")
            pe_mix(pe, 1, "x")
            pe_ffn(pe, "f21x")
            pe_norm(pe, W[8])
            pe.wait_ge(bank_free, tiles_of("f21x.down"))
            pe_turn_out(pe, W[7])

        def dve_second(dve):
            dve_turn_in(dve, CTX)
            dve_ada(dve, 0)
            dve_ffn2(dve, "f10x", "x", 0)
            dve_ffn2(dve, "f10c", "c", 0)
            dve_mix(dve, 0, "c")
            dve_ffn2(dve, "f20c", "c", 2)
            dve_mix(dve, 0, "x")
            dve_ffn2(dve, "f20x", "x", 2)
            dve_ada(dve, 1)
            dve_ffn2(dve, "f11x", "x", 0)
            dve_ffn2(dve, "f11c", "c", 0)
            dve_mix(dve, 1, "c")
            dve_mix(dve, 1, "x")
            dve_ffn2(dve, "f21x", "x", 2)
            dve_norm(dve, X, lambda c: vec("final_g_2", 0, c), W[7], to_operand=False)
            dve.memset(eps[:, 1:2], 0.0).then_inc(turn_in, 1)
            dve.wait_ge(turn_in, after(dve, turn_in))
            dve_turn_out(dve)

        block = ctx.enter_context(nc.Block())
        FIRST = [f"rw{0}", "sb", "ds", f"rw{3}"]

        @block.sync
        def _(sp):
            sp_setup(sp)
            sp_lora(sp, 0)
            for g in order:
                if g.name == "ds.q":
                    sp_ds_small(sp)
                if g.name == "rw3.r":
                    sp_lora(sp, 1)
                if g.name == "ada0":
                    sp_ctx(sp)
                if g.name.endswith(".q") and g.name[:5] in [f"mix{l}{s}" for l, s in FULL]:
                    sp_gated_unit(sp, int(g.name[3]))
                sp_panels(sp, g.name)
            sp_out(sp)

        @block.gpsimd
        def _(pool):
            for g in order:
                pool_panels(pool, g.name)

        @block.scalar
        def _(act):
            for q in range(RING):
                act_round(act, order[0], q)
            act_input(act)
            act_rwkv(act, 0)
            act.wait_ge(bank_free, tiles_of("rw0.out"))
            act_ffn(act, "ffn0", X)
            act.wait_ge(bank_free, tiles_of("ffn0.down"))
            act_sb(act)
            act.wait_ge(bank_free, tiles_of("sb.out"))
            act_ffn(act, "ffn1", X)
            act.wait_ge(bank_free, tiles_of("ffn1.down"))
            act_ds(act)
            act.wait_ge(bank_free, tiles_of("ds.out"))
            act_ffn(act, "ffn2", X)
            act.wait_ge(bank_free, tiles_of("ffn2.down"))
            act_rwkv(act, 3)
            act.wait_ge(bank_free, tiles_of("rw3.out"))
            act_ffn(act, "ffn3", X)
            act_second(act)

        @block.tensor
        def _(pe):
            pe_setup(pe)
            pe_rwkv(pe, 0)
            pe_ffn(pe, "ffn0")
            pe_sb(pe)
            pe_ffn(pe, "ffn1")
            pe_ds(pe)
            pe_ffn(pe, "ffn2")
            pe_rwkv(pe, 3)
            pe_ffn(pe, "ffn3")
            pe_second(pe)

        @block.vector
        def _(dve):
            dve_setup(dve)
            dve_rwkv(dve, 0)
            dve_ffn(dve, "ffn0", X, lambda c: vec("norm_ffn", 0, c))
            dve_sb(dve, 1)
            dve_ffn(dve, "ffn1", X, lambda c: vec("norm_ffn", 1, c))
            dve_ds(dve, 2)
            dve_ffn(dve, "ffn2", X, lambda c: vec("norm_ffn", 2, c))
            dve_rwkv(dve, 3)
            dve_ffn(dve, "ffn3", X, lambda c: vec("norm_ffn", 3, c))
            dve_second(dve)


def kernel(**inputs):
    import concourse.bacc as bacc
    from concourse.bass_utils import run_bass_kernel_spmd

    nc = bacc.Bacc("TRN2", target_bir_lowering=False, num_devices=1)
    table, at = constants()
    arrays, views = {}, {}
    for name, value in [*inputs.items(), ("const", table)]:
        array = np.ascontiguousarray(value)
        arrays[f"in_{name}"] = array
        views[name] = nc.dram_tensor(f"in_{name}", array.shape, F32, kind="ExternalInput").ap()
    out = nc.dram_tensor("out", (1, S, D), F32, kind="ExternalOutput").ap()
    build(nc, views, out, at)
    return run_bass_kernel_spmd(nc, [arrays], core_ids=[0]).results[0]["out"]
```

```python
from contextlib import ExitStack, contextmanager

import numpy as np

import concourse.bass as bass
import concourse.mybir as mybir

F32 = mybir.dt.float32
F32R = mybir.dt.float32r
ACT = mybir.ActivationFunctionType
ALU = mybir.AluOpType
AX_X = mybir.AxisListType.X

P = 128
S = 256
TT = S // P
D = 1024
C = D // P
H = 16
DH = 64
DEPTH = 4
F = 2816
FC = F // P
CHUNK = 64
NCH = S // CHUNK
L_W, L_A, L_G, L_V = 64, 64, 160, 32
IDX_H = 8
TOPK = S // 4
EPS = 1e-6
GN_EPS = DH * 1e-5
DECAY = float(np.exp(np.float64(-0.5)))
NEG = -3.0e38
TAKEN = -3.2e38
HIDE = -1.0e30

RING = 4
KPAN = 8

D2 = 2
N_MOD = 9
CA_W, CA_K = 256, 3
SG_W, SG_G = 256, 4
DA_H, DA_D = 4, 64
DA_W = DA_H * 2 * DA_D
CF_W, CF_K = 256, 31
N_BR = 4
A_OFF = 0
B_OFF = A_OFF + 3 * CA_W
Q_OFF = B_OFF + 2 * SG_W
K_OFF = Q_OFF + DA_W
V_OFF = K_OFF + DA_W
D_OFF = V_OFF + DA_W
G_OFF = D_OFF + 2 * CF_W


def name_of(eng):
    return str(eng.engine).split(".")[-1]


class Counts:

    def __init__(self):
        self.seen = {}
        self.turns = {}

    def at(self, eng, sem):
        return self.seen.get((sem, name_of(eng)), 0)

    def start(self, eng, sem, value):
        self.seen[sem, name_of(eng)] = value

    def after(self, eng, sem, n=1):
        have = self.at(eng, sem) + n
        self.start(eng, sem, have)
        if (sem, name_of(eng)) in self.turns:
            i, per = self.turns[sem, name_of(eng)]
            assert have > 0
            return i * per + have
        return have if have > 0 else None

    @contextmanager
    def repeat(self, eng, n, per):
        with eng.Fori(0, n) as i:
            at = {sem: self.at(eng, sem) for sem in per}
            for sem, k in per.items():
                self.turns[sem, name_of(eng)] = (i, k)
            yield i
        for sem, k in per.items():
            assert self.at(eng, sem) == at[sem] + k
            self.start(eng, sem, at[sem] + n * k)
            del self.turns[sem, name_of(eng)]


class Projection:

    def __init__(self, name, steps, panels, tokens_out=False, direct=False):
        self.name, self.steps, self.panels = name, steps, panels
        self.tokens_out = tokens_out
        self.direct = direct
        self.pps = len(panels)
        self.tiles = 1 + max(p[4] for p in panels)
        self.body = RING // self.tiles
        self.n_panels = steps * self.pps
        self.n_tiles = 0 if direct else steps * self.tiles


def dense(name, w, col, n_out, operand, kc=C, tokens_out=False):
    groups = [(k0, min(KPAN, kc - k0)) for k0 in range(0, kc, KPAN)]
    return Projection(name, n_out // P, [(w, col, k0, nk, 0, operand) for k0, nk in groups], tokens_out)


def pair(name, w_a, col_a, kc_a, w_b, col_b, kc_b, n_out, operand_a, operand_b):
    return Projection(name, n_out // P, [(w_a, col_a, 0, kc_a, 0, operand_a), (w_b, col_b, 0, kc_b, 1, operand_b)])


def constants():
    p = np.arange(P)[:, None]
    f = np.arange(P)[None, :]
    t = np.arange(S)[None, :]
    parts = {}
    parts["ident"] = p == f
    parts["headones"] = p // DH == f // DH
    half = DH // 2
    rot = np.zeros((P, P))
    for m in range(P):
        if m % DH < half:
            rot[m + half, m] = -1.0
        else:
            rot[m - half, m] = 1.0
    parts["rot_head"] = rot
    nf = DA_D // 4
    rot = np.zeros((P, P))
    for m in range(P):
        if m % (2 * nf) < nf:
            rot[m + nf, m] = -1.0
        else:
            rot[m - nf, m] = 1.0
    parts["rot_axial"] = rot
    inv = (1.0 / (np.float32(10000.0) ** (np.arange(half, dtype=np.float32) / np.float32(half)))).astype(np.float32)
    ang = (np.arange(S, dtype=np.float32)[None, :] * inv[np.arange(P) % half][:, None]).astype(np.float32)
    parts["cos_head"], parts["sin_head"] = np.cos(ang), np.sin(ang)
    inv = (np.float32(10000.0) ** (-np.arange(nf, dtype=np.float32) / np.float32(nf))).astype(np.float32)
    grid = np.stack([np.arange(S) // 64, np.arange(S) % 64]).astype(np.float32)
    d = np.arange(P) % DA_D
    ang = (grid[d // (2 * nf)] * inv[d % nf][:, None]).astype(np.float32)
    parts["cos_axial"], parts["sin_axial"] = np.cos(ang), np.sin(ang)
    parts["earlier"] = np.concatenate([(st * P + p) < t for st in range(TT)], axis=1)
    parts["after"] = p > f
    j, i = np.arange(P)[:, None] % CHUNK, np.arange(CHUNK)[None, :]
    parts["before"] = j < i
    parts["upto"] = j <= i
    parts["below"] = j > i
    for lv in range(6):
        b = 2 ** lv
        parts[f"upper{lv}"] = ((j // b) % 2 == 0) & (i // b == j // b + 1)
        parts[f"lower{lv}"] = ((i // b) % 2 == 0) & (j // b == i // b + 1)
    parts["eye64"] = j == i
    parts["carry"] = np.broadcast_to(t % CHUNK != 0, (P, S))
    at, cols, n = {}, [], 0
    for name, a in parts.items():
        a = np.asarray(a, np.float32)
        at[name] = (n, a.shape[1])
        cols.append(a)
        n += a.shape[1]
    return np.ascontiguousarray(np.concatenate(cols, axis=1)), at


def vector_rows():
    rows, at, n = [], {}, 0
    for name, k in (("norm_mix", DEPTH), ("norm_ffn", DEPTH), ("rw_mix", 12), ("rw_w0", 2), ("rw_a0", 2),
                    ("rw_k_k", 2), ("rw_k_a", 2), ("rw_r_k", 2), ("rw_ln_w", 2), ("rw_ln_b", 2), ("rw_v0", 1),
                    ("norm_g_2", 3 * D2), ("b_ada_2", N_MOD * D2), ("c_2", 1), ("c_ctx_2", 1), ("final_g_2", 1)):
        at[name] = n
        rows.append((name, n, k))
        n += k
    return rows, at, n


def vector_rows_256():
    rows, at, n = [], {}, 0
    for name, k in (("conv_a_w_2", CA_K * D2), ("conf_dw_2", CF_K * D2), ("conf_db_2", D2),
                    ("conf_ln_g_2", D2), ("conf_ln_b_2", D2)):
        at[name] = n
        rows.append((name, n, k))
        n += k
    return rows, at, n


def build(nc, a, out, CONST_AT):
    VEC_ROWS, VAT, NV = vector_rows()
    VEC2_ROWS, V2AT, NV2 = vector_rows_256()
    with ExitStack() as ctx:
        place = [-(-nc.sbuf_base // 64) * 64]

        def sb(name, cols, dt=F32, at=None):
            off = place[0] if at is None else at
            t = nc.alloc_sbuf_tensor_at(name, [P, cols], dt, offset=off)
            if at is None:
                place[0] += -(-cols * 4 // 64) * 64
            return t

        def sem(name):
            return ctx.enter_context(nc.semaphore(name))

        def v3(t, n=S):
            return t[:, :].rearrange("p (c t) -> p c t", t=n)

        SLOT = KPAN * P
        raw = [sb(f"raw{i}", SLOT) for i in range(RING)]
        whi = [sb(f"whi{i}", SLOT, F32R) for i in range(RING)]
        wlo = [sb(f"wlo{i}", SLOT, F32R) for i in range(RING)]
        X = sb("X", C * S)
        CTX = sb("CTX", C * S)
        a_at = place[0]
        AH, AL = sb("AH", C * S, F32R), sb("AL", C * S, F32R)
        cst = sb("cst", sum(n for _, n in CONST_AT.values()))
        VEC = sb("VEC", C * NV)
        VEC2 = sb("VEC2", 2 * NV2)
        VEC3 = sb("VEC3", 12)
        ones = sb("ones", P)
        eps = sb("eps", 2)
        STD = sb("STD", S)
        RSTD = sb("RSTD", S)
        silu = [sb(f"silu{i}", S) for i in range(2)]
        hid = sb("hid", S)
        w_at = []
        W = []
        for i in range(9):
            w_at.append(place[0])
            W.append(sb(f"W{i}", C * S))
        HH = sb("HH", FC * S, F32R, at=w_at[0])
        HL = sb("HL", FC * S, F32R, at=w_at[0] + FC * S * 4)
        VF = sb("VF", C * S)
        l_at = place[0]
        lw1, la1, lg1, lv1 = sb("lw1", C * L_W), sb("la1", C * L_A), sb("lg1", C * L_G), sb("lv1", C * L_V)
        lwa2 = sb("lwa2", D)
        lg2 = sb("lg2", D)
        lgv2 = sb("lgv2", D)
        BRH, BRL = sb("BRH", 10 * S, F32R, at=l_at), sb("BRL", 10 * S, F32R, at=l_at + 10 * S * 4)
        assert place[0] <= nc.sbuf_usable_end, (place[0], nc.sbuf_usable_end)
        bank = [ctx.enter_context(nc.psum_tensor(f"bank{i}", [P, 512], F32)) for i in range(8)]

        def const(name):
            o, n = CONST_AT[name]
            return cst[:, o:o + n]

        VEC_v, VEC2_v = v3(VEC, NV), v3(VEC2, NV2)

        def vec(name, row, c):
            return VEC_v[:, c, VAT[name] + row:VAT[name] + row + 1]

        def vec_b(name, row):
            return VEC_v[:, :, VAT[name] + row:VAT[name] + row + 1].to_broadcast([P, C, S])

        counts = Counts()
        after, repeat = counts.after, counts.repeat

        const_landed = sem("const_landed")
        rows_landed = sem("rows_landed")
        x_rows_landed = sem("x_rows_landed")
        lora_landed = sem("lora_landed")
        raw_landed = [sem(f"raw_landed{i}") for i in range(RING)]
        hi_ready = sem("hi_ready")
        lo_ready = sem("lo_ready")
        panels_done = sem("panels_done")
        bank_free = sem("bank_free")
        operand_ready = sem("operand_ready")
        consts_set = sem("consts_set")
        vec_turned = sem("vec_turned")
        vec_ready = sem("vec_ready")
        x_turned = sem("x_turned")
        x_ready = sem("x_ready")
        squares_ready = sem("squares_ready")
        sums_ready = sem("sums_ready")
        std_ready = sem("std_ready")
        silu_ready = sem("silu_ready")
        hidden_ready = sem("hidden_ready")
        dve_step = sem("dve_step")
        act_step = sem("act_step")
        out_landed = sem("out_landed")
        head_in = sem("head_in")
        head_sums = sem("head_sums")
        head_taken = sem("head_taken")
        root_ready = sem("root_ready")
        lora_in = sem("lora_in")
        lora_mid = sem("lora_mid")
        lora_act = sem("lora_act")
        lora_out = sem("lora_out")
        lora_taken = sem("lora_taken")
        ada_rows = sem("ada_rows")
        ada_turned = sem("ada_turned")
        ada_ready = sem("ada_ready")
        direct_used = sem("direct_used")
        exp_ready = sem("exp_ready")
        decay_ready = sem("decay_ready")
        scan_in = sem("scan_in")
        gram_ready = sem("gram_ready")
        turned_ready = sem("turned_ready")
        turned_taken = sem("turned_taken")
        gram_taken = sem("gram_taken")
        inv_half = sem("inv_half")
        inv_half_taken = sem("inv_half_taken")
        inv_off = sem("inv_off")
        inv_taken = sem("inv_taken")
        rhs_ready = sem("rhs_ready")
        rhs_taken = sem("rhs_taken")
        sol_ready = sem("sol_ready")
        sol_taken = sem("sol_taken")
        chunk_out = sem("chunk_out")
        state_ready = sem("state_ready")
        z_ready = sem("z_ready")
        ds_z_ready = sem("ds_z_ready")
        att_raw = sem("att_raw")
        exps_ready = sem("exps_ready")
        later_in = sem("later_in")
        later_ready = sem("later_ready")
        logit_ready = sem("logit_ready")
        att_ready = sem("att_ready")
        heads_out = sem("heads_out")
        heads_taken = sem("heads_taken")
        idx_ready = sem("idx_ready")
        idx_act = sem("idx_act")
        idx_taken = sem("idx_taken")
        att_turned = sem("att_turned")
        att_turned_taken = sem("att_turned_taken")
        small_landed = sem("small_landed")
        small_ready = sem("small_ready")
        h_ready = sem("h_ready")
        turn_in = sem("turn_in")
        turned_out = sem("turned_out")
        out_ready = sem("out_ready")
        ctx_landed = sem("ctx_landed")
        cond_ready = sem("cond_ready")
        lam_in = sem("lam_in")
        lam_sums = sem("lam_sums")
        lam_exp = sem("lam_exp")
        sgu_free = sem("sgu_free")
        sgu_landed = sem("sgu_landed")
        sgu_turned = sem("sgu_turned")
        sgu_copied = sem("sgu_copied")
        sgu_out = sem("sgu_out")
        glu_ready = sem("glu_ready")
        conf_ready = sem("conf_ready")
        conf_act = sem("conf_act")
        merged_step = sem("merged_step")
        da_scores = sem("da_scores")
        da_max = sem("da_max")
        da_exp = sem("da_exp")
        da_mix = sem("da_mix")
        da_turned = sem("da_turned")
        da_copied = sem("da_copied")
        da_out = sem("da_out")
        da_stored = sem("da_stored")

        counts.start(nc.sync, lo_ready, -RING)
        counts.start(nc.tensor, bank_free, -RING)
        counts.start(nc.scalar, hidden_ready, -2)
        counts.start(nc.scalar, merged_step, -2)

        A = (v3(AH), v3(AL))
        HID = (v3(HH), v3(HL))
        BR = (v3(BRH), v3(BRL))
        G = {}
        order = []

        def plan(g):
            g.p0 = sum(x.n_panels for x in order)
            g.t0 = sum(x.n_tiles for x in order)
            order.append(g)
            G[g.name] = g

        def plan_ffn(name, w_gate, gate_col, w_up, up_col, w_down):
            plan(pair(f"{name}.up", w_gate, gate_col, C, w_up, up_col, C, F, A, A))
            plan(dense(f"{name}.down", w_down, 0, D, HID, kc=FC))

        ADA_N = 512
        ADA_ROWS = D // RING
        ADA_PANELS = N_MOD * D // ADA_N * RING
        for layer in range(DEPTH):
            if layer % 3 == 0:
                for j, n in enumerate("rkv"):
                    plan(dense(f"rw{layer}.{n}", a["rw_w_rkv"][layer // 3, j], 0, D, A))
                plan(Projection(f"ada{layer // 3}", ADA_PANELS, [(a["w_ada_2"][layer // 3], 0, 0, C, 0, None)], direct=True))
                plan(dense(f"rw{layer}.out", a["rw_w_out"][layer // 3], 0, D, A))
            elif layer % 3 == 1:
                for j, n in enumerate("qkv"):
                    plan(dense(f"sb.{n}", a["sb_w_qkv"][0], j * D, D, A, tokens_out=n == "v"))
                plan(dense("sb.out", a["sb_w_out"][0], 0, D, A))
            else:
                for j, n in enumerate("qkv"):
                    plan(dense(f"ds.{n}", a["ds_w_in"][0], j * D, D, A, tokens_out=n == "v"))
                plan(dense("ds.qi", a["ds_w_in"][0], 3 * D, IDX_H * DH, A))
                plan(dense("ds.out", a["ds_w_out"][0], 0, D, A))
            plan_ffn(f"ffn{layer}", a["ffn_w_gu"][layer], 0, a["ffn_w_gu"][layer], F, a["ffn_w_down"][layer])
        BRANCH = {"a": (0, CA_W), "b": (2, SG_W), "c": (4, DA_W), "d": (8, CF_W)}
        MERGE_ORDER = "abdc"
        FULL = [(0, "c"), (0, "x"), (1, "x")]

        def plan_mix(l, s):
            w = a["w_in_2"][l]
            pre = f"mix{l}{s}"
            plan(dense(f"{pre}.k", w, K_OFF, DA_W, A))
            if (l, s) in FULL:
                plan(dense(f"{pre}.q", w, Q_OFF, DA_W, A))
            plan(dense(f"{pre}.v", w, V_OFF, DA_W, A, tokens_out=True))
            if (l, s) not in FULL:
                return
            plan(dense(f"{pre}.ab", w, A_OFF, Q_OFF - A_OFF, A))
            plan(dense(f"{pre}.d", w, D_OFF, 2 * CF_W, A))
            for b in MERGE_ORDER:
                n, (c0, width) = "abcd".index(b), BRANCH[b]
                opnd = tuple(t[:, c0:c0 + width // P] for t in BR)
                plan(pair(f"{pre}.{b}out", a[f"w_{b}_out_2"][l], 0, width // P, w, G_OFF + n * D, C, D, opnd, A))
            plan(dense(f"{pre}.o", a["w_o_2"][l], 0, D, A))

        for l in range(D2):
            for s in "xc":
                plan_ffn(f"f1{l}{s}", a["ffn1_w1_2"][l], 0, a["ffn1_w3_2"][l], 0, a["ffn1_w2_2"][l])
            for s in "cx":
                plan_mix(l, s)
                if (l, s) in FULL:
                    plan_ffn(f"f2{l}{s}", a["ffn2_w1_2"][l], 0, a["ffn2_w3_2"][l], 0, a["ffn2_w2_2"][l])

        def steps_of(eng, g, per, step, peel=False, last_straight=False):
            full = g.steps // g.body
            first = 1 if peel or any(counts.at(eng, x) < 0 for x in per) else 0
            last = full - (1 if last_straight else 0)
            for s in range(first * g.body):
                step(s, s % g.body)
            if last - first > 1:
                with repeat(eng, last - first, per) as i:
                    for j in range(g.body):
                        step((i + first) * g.body + j, j)
                begin = last * g.body
            else:
                begin = first * g.body
            for s in range(begin, g.steps):
                step(s, s % g.body)

        def load_panel(sp, g, s, slot, k=0):
            w, col, k0, nk, _, _ = g.panels[k]
            src = w[k0 * P:(k0 + nk) * P, bass.ds(s * P + col, P)].rearrange("(c p) m -> p c m", p=P)
            sp.dma_start(raw[slot][:, 0:nk * P].rearrange("p (c m) -> p c m", m=P), src).then_inc(raw_landed[slot], 16)

        def sp_direct(sp, name):
            g = G[name]

            def load(group, j):
                src = g.panels[0][0][j * ADA_ROWS:(j + 1) * ADA_ROWS, bass.ds(group * ADA_N, ADA_N)]
                sp.dma_start(raw[j][:, :].rearrange("p (c m) -> p c m", m=ADA_N),
                             src.rearrange("(c p) m -> p c m", p=P)).then_inc(raw_landed[j], 16)

            for j in range(RING):
                sp.wait_ge(lo_ready, after(sp, lo_ready))
                load(0, j)
            with repeat(sp, g.steps // RING - 1, {direct_used: RING}) as i:
                for j in range(RING):
                    sp.wait_ge(direct_used, after(sp, direct_used))
                    load(i + 1, j)

        def sp_panels(sp, name):
            g = G[name]
            at = order.index(g)
            behind_direct = at > 0 and order[at - 1].direct

            def step(s, j):
                for k in range(g.pps):
                    slot = (g.p0 + j * g.pps + k) % RING
                    if behind_direct and isinstance(s, int) and s * g.pps + k < RING:
                        sp.wait_ge(direct_used, after(sp, direct_used))
                    else:
                        n = after(sp, lo_ready)
                        if n is not None:
                            sp.wait_ge(lo_ready, n)
                    load_panel(sp, g, s, slot, k)

            steps_of(sp, g, {lo_ready: g.body * g.pps}, step, peel=behind_direct)

        def pool_panels(pool, name):
            g = G[name]

            def step(s, j):
                for k, (_, _, _, nk, _, _) in enumerate(g.panels):
                    slot = (g.p0 + j * g.pps + k) % RING
                    n = nk * P
                    pool.wait_ge(hi_ready, after(pool, hi_ready))
                    pool.tensor_tensor(wlo[slot][:, 0:n], raw[slot][:, 0:n], whi[slot][:, 0:n],
                                                   ALU.subtract).then_inc(lo_ready, 1)

            steps_of(pool, g, {hi_ready: g.body * g.pps}, step)

        def act_round(act, g, q):
            slot, n = (g.p0 + q) % RING, g.panels[q % g.pps][3] * P
            act.wait_ge(raw_landed[slot], after(act, raw_landed[slot], 16))
            act.activation(whi[slot][:, 0:n], raw[slot][:, 0:n], ACT.Copy).then_inc(hi_ready, 1)

        def act_panels(act, name, work=None, by_hand=False):
            g = G[name]
            at = order.index(g)
            following = order[at + 1] if at + 1 < len(order) else None

            def step(s, j):
                for k in range(g.pps):
                    act.wait_ge(panels_done, after(act, panels_done))
                    if work:
                        work(s, j, k)
                    q = j * g.pps + k + RING
                    if isinstance(s, int) and s * g.pps + k + RING >= g.n_panels:
                        if following and not following.direct:
                            act_round(act, following, s * g.pps + k + RING - g.n_panels)
                    else:
                        act_round(act, g, q)

            if by_hand:
                return lambda s: step(s, s % g.body)
            n = g.body * g.pps
            per = {panels_done: n, **{r: 16 * n // RING for r in raw_landed}}
            if work:
                per |= work.per
            steps_of(act, g, per, step, last_straight=True)

        def pe_panels(pe, name, fills=1, by_hand=False):
            g = G[name]
            pe.wait_ge(operand_ready, after(pe, operand_ready, fills))

            def step(s, j):
                started = set()
                for k, (_, _, k0, nk, tile, (oh, ol)) in enumerate(g.panels):
                    slot = (g.p0 + j * g.pps + k) % RING
                    ps = bank[(g.t0 + j * g.tiles + tile) % RING]
                    if tile not in started:
                        n = after(pe, bank_free)
                        if n is not None:
                            pe.wait_ge(bank_free, n)
                    pe.wait_ge(lo_ready, after(pe, lo_ready))
                    last_panel = tile not in [x[4] for x in g.panels[k + 1:]]
                    for tt in range(TT if g.tokens_out else 1):
                        for c in range(nk):
                            wh, wl = (t[slot][:, c * P:(c + 1) * P] for t in (whi, wlo))
                            passes = ((wh, oh), (wh, ol), (wl, oh))
                            for n, (w, o) in enumerate(passes):
                                first = tile not in started and c == 0 and n == 0
                                last = last_panel and c == nk - 1 and n == 2
                                if g.tokens_out:
                                    mm = pe.matmul(ps[:, tt * P:(tt + 1) * P], o[:, k0 + c, tt * P:(tt + 1) * P], w,
                                                   start=first, stop=last)
                                else:
                                    mm = pe.matmul(ps[:, 0:o.shape[2]], w, o[:, k0 + c, :], start=first, stop=last)
                    started.add(tile)
                    mm.then_inc(panels_done, 1)

            if by_hand:
                return lambda s: step(s, s % g.body)
            n = g.body * g.pps
            steps_of(pe, g, {bank_free: RING, lo_ready: n}, step)

        def dve_tiles(dve, name, take, per=None, by_hand=False):
            g = G[name]

            def step(s, j):
                dve.wait_ge(panels_done, after(dve, panels_done, g.pps))
                take(s, j, [bank[(g.t0 + j * g.tiles + t) % RING] for t in range(g.tiles)])

            if by_hand:
                return lambda s: step(s, s % g.body)
            steps_of(dve, g, {panels_done: g.body * g.pps, **{k: v * g.body for k, v in (per or {}).items()}}, step)
            dve.wait_ge(bank_free, tiles_of(name))

        def take_copy(dve, dst, scale=None):
            def take(s, j, banks):
                o = dst[:, bass.ds(s * S, S)]
                if scale is None:
                    dve.tensor_copy(o, banks[0][:, 0:S]).then_inc(bank_free, 1)
                else:
                    dve.tensor_scalar(o, banks[0][:, 0:S], scale, None, ALU.mult).then_inc(bank_free, 1)
            return take

        def take_tokens(dve, dst):
            def take(s, j, banks):
                dve.tensor_copy(dst[:, :, bass.ds(s * P, P)],
                                             banks[0][:, 0:S].rearrange("p (a m) -> p a m", m=P)).then_inc(bank_free, 1)
            return take

        def take_residual(dve, x, gate=None):
            def take(s, j, banks):
                o = x[:, bass.ds(s * S, S)]
                if gate is None:
                    dve.tensor_tensor(o, o, banks[0][:, 0:S], ALU.add).then_inc(bank_free, 1)
                else:
                    dve.scalar_tensor_tensor(o, banks[0][:, 0:S], gate[:, bass.ds(s, 1)], o,
                                                          ALU.mult, ALU.add).then_inc(bank_free, 1)
            return take

        def split(dve, src, dst=None):
            hi, lo = dst or (AH, AL)
            n = src.shape[1]
            dve.tensor_copy(hi[:, 0:n], src[:, :]).then_inc(dve_step, 1)
            dve.wait_ge(dve_step, after(dve, dve_step))
            dve.tensor_tensor(lo[:, 0:n], src[:, :], hi[:, 0:n], ALU.subtract).then_inc(operand_ready, 1)
            dve.wait_ge(operand_ready, after(dve, operand_ready))

        def act_norm(act, x, sq):
            act.activation(sq[:, :], x[:, :], ACT.Square).then_inc(squares_ready, 1)
            act.wait_ge(sums_ready, after(act, sums_ready))
            act.activation(STD[:, :], bank[4][:, 0:S], ACT.Sqrt, bias=eps[:, 0:1], scale=1.0 / D).then_inc(std_ready, 1)

        def pe_norm(pe, sq):
            pe.wait_ge(squares_ready, after(pe, squares_ready))
            for c in range(C):
                mm = pe.matmul(bank[4][:, 0:S], ones[:, :], sq[:, c * S:(c + 1) * S], start=c == 0, stop=c == C - 1)
            mm.then_inc(sums_ready, 1)

        def dve_norm(dve, x, gain, h, shift=None, to_operand=True):
            dve.wait_ge(std_ready, after(dve, std_ready))
            dve.reciprocal(RSTD[:, :], STD[:, :]).then_inc(dve_step, 1)
            dve.wait_ge(dve_step, after(dve, dve_step))
            for c in range(C):
                o = h[:, c * S:(c + 1) * S]
                op = dve.scalar_tensor_tensor(o, x[:, c * S:(c + 1) * S], gain(c), RSTD[:, :], ALU.mult, ALU.mult)
                if shift:
                    if c == C - 1:
                        op.then_inc(dve_step, 1)
                        dve.wait_ge(dve_step, after(dve, dve_step))
            if shift:
                for c in range(C):
                    o = h[:, c * S:(c + 1) * S]
                    op = dve.tensor_scalar(o, o, shift(c), None, ALU.add)
            op.then_inc(h_ready, 1)
            dve.wait_ge(h_ready, after(dve, h_ready))
            if to_operand:
                split(dve, h)

        def tiles_of(name):
            return G[name].t0 + G[name].n_tiles

        def act_ffn(act, name, x):
            act_norm(act, x, W[8])

            def gate(s, j, k):
                if k == 0:
                    n = after(act, hidden_ready)
                    if n is not None:
                        act.wait_ge(hidden_ready, n)
                    g = G[f"{name}.up"]
                    ps = bank[(g.t0 + j * g.tiles) % RING]
                    act.activation(silu[j % 2][:, :], ps[:, 0:S], ACT.Silu).then_inc(silu_ready, 1)
            gate.per = {hidden_ready: 2}
            act_panels(act, f"{name}.up", gate)
            act_panels(act, f"{name}.down")

        def pe_ffn(pe, name):
            pe_norm(pe, W[8])
            pe_panels(pe, f"{name}.up")
            pe.wait_ge(hidden_ready, after(pe, hidden_ready, FC))
            pe_panels(pe, f"{name}.down", fills=0)

        def dve_ffn(dve, name, x, gain, shift=None, out_gate=None):
            dve_norm(dve, x, gain, W[7], shift)

            def take(s, j, banks):
                dve.wait_ge(silu_ready, after(dve, silu_ready))
                o = bass.ds(s * S, S)
                dve.tensor_tensor(hid[:, :], silu[j % 2][:, :], banks[1][:, 0:S], ALU.mult).then_inc(bank_free, 2)
                dve.wait_ge(bank_free, after(dve, bank_free, 2))
                dve.tensor_copy(HH[:, o], hid[:, :]).then_inc(dve_step, 1)
                dve.wait_ge(dve_step, after(dve, dve_step))
                dve.tensor_tensor(HL[:, o], hid[:, :], HH[:, o], ALU.subtract).then_inc(hidden_ready, 1)
                dve.wait_ge(hidden_ready, after(dve, hidden_ready))
            counts.start(dve, bank_free, G[f"{name}.up"].t0)
            dve_tiles(dve, f"{name}.up", take, {silu_ready: 1, bank_free: 2, dve_step: 1, hidden_ready: 1})
            dve_tiles(dve, f"{name}.down", take_residual(dve, x, out_gate))

        def pe_heads(pe, mat, src, chunks=C, first=4):
            pe.wait_ge(head_in, after(pe, head_in))
            for c in range(chunks):
                mm = pe.matmul(bank[first + c // 2][:, (c % 2) * S:(c % 2 + 1) * S], mat, src[:, c * S:(c + 1) * S],
                               start=True, stop=True)
                if c % 2 or c == chunks - 1:
                    mm.then_inc(head_sums, 1)

        def dve_heads(dve, take, chunks=C, first=4):
            for c in range(0, chunks, 2):
                dve.wait_ge(head_sums, after(dve, head_sums))
                n = min(2, chunks - c) * S
                op = take(slice(c * S, c * S + n), bank[first + c // 2][:, 0:n])
            return op

        RW_H, RW_D, RW_XA, RW_XB, RW_R, RW_K, RW_A, RW_CUM, RW_G = W[0], W[1], W[2], CTX, W[3], W[4], W[6], W[7], W[8]
        RW_Q, RW_P, RW_B, RW_C, RW_Y, RW_BONUS = W[3], W[0], W[1], W[4], W[6], W[2]
        lora_wa, lora_g, lora_gv = silu[0], silu[1], hid
        WEND = sb("WEND", C * NCH)
        Q4 = 512
        N_, GBQ, GCP, GCQ = (CTX[:, k * Q4:(k + 1) * Q4] for k in range(4))
        L_, VT, BT, CT = (W[7][:, k * Q4:(k + 1) * Q4] for k in range(4))
        work = [sb(f"scan{k}", Q4, at=a_at + k * Q4 * 4) for k in range(7)]
        IY, IX, IT, LOFF, RHS, SOL, STATE = (t[:, :] for t in work)
        KK_MIN = 1e-24
        HALF = [slice(h * Q4 // 2, (h + 1) * Q4 // 2) for h in range(2)]
        INV_BANKS = [(bank[0], bank[1], bank[2]), (bank[3], bank[4], bank[6])]
        OUT_BANKS, STATE_BANKS = (bank[5], bank[4]), (bank[2], bank[6])
        ADA_BANK = bank[7]
        VISITS = 1 + 5 * 4 + 4
        ADA_FIRST = N_MOD * D // ADA_N - 4 * NCH
        cond = sb("cond", C * 32)
        ada_tok = sb("ada_tok", ADA_N, at=a_at + 7 * Q4 * 4)
        both = [sb(f"both{l}", N_MOD * C * 2) for l in range(D2)]

        def rw_values(layer):
            return VF if layer == 0 else W[5]

        def lora_parts(layer):
            parts = [("w", RW_XB, lw1, L_W), ("a", RW_XB, la1, L_A)]
            if layer:
                parts.append(("v", RW_XA, lv1, L_V))
            return parts + [("g", RW_XB, lg1, L_G)]

        def sp_lora(sp, j):
            for t, w, n in ((lw1, "rw_w1", L_W), (la1, "rw_a1", L_A), (lg1, "rw_g1", L_G)):
                sp.dma_start(t[:, :].rearrange("p (c m) -> p c m", m=n),
                                            a[w][j].rearrange("(c p) m -> p c m", p=P)).then_inc(lora_landed, 16)
            sp.dma_start(lwa2[0:64, :], a["rw_w2"][j]).then_inc(lora_landed, 16)
            sp.dma_start(lwa2[64:128, :], a["rw_a2"][j]).then_inc(lora_landed, 16)
            sp.dma_start(lg2[:, :], a["rw_g2"][j][0:P, :]).then_inc(lora_landed, 16)
            sp.dma_start(lgv2[0:32, :], a["rw_g2"][j][P:L_G, :]).then_inc(lora_landed, 16)
            if j:
                sp.dma_start(lv1[:, :].rearrange("p (c m) -> p c m", m=L_V),
                                            a["rw_v1"][j - 1].rearrange("(c p) m -> p c m", p=P)).then_inc(lora_landed, 16)
                sp.dma_start(lgv2[32:64, :], a["rw_v2"][j - 1]).then_inc(lora_landed, 16)

        def pe_lora(pe, part, first=False):
            name, x, w1, n = part
            pe.wait_ge(lora_in, after(pe, lora_in))
            if not first:
                pe.wait_ge(lora_taken, after(pe, lora_taken, 4))
            base = {"w": 0, "a": 64, "v": 32, "g": 0}[name]
            m = min(n, P)
            w3 = w1[:, :].rearrange("p (c m) -> p c m", m=n)
            for c in range(C):
                mm = pe.matmul(bank[4][base:base + m, 0:S], w3[:, c, 0:m], x[:, c * S:(c + 1) * S],
                               start=c == 0, stop=c == C - 1)
            if n > P:
                for c in range(C):
                    mm = pe.matmul(bank[5][0:n - P, 0:S], w3[:, c, P:n], x[:, c * S:(c + 1) * S],
                                   start=c == 0, stop=c == C - 1)
            mm.then_inc(lora_mid, 1)
            pe.wait_ge(lora_act, after(pe, lora_act))
            for t in range(C):
                if t >= 4:
                    pe.wait_ge(lora_taken, after(pe, lora_taken))
                o, cols = bank[4 + t % 4][:, 0:S], slice(t * P, (t + 1) * P)
                if name == "w":
                    mm = pe.matmul(o, lwa2[0:64, cols], lora_wa[0:64, :], start=True, stop=True)
                elif name == "a":
                    mm = pe.matmul(o, lwa2[64:128, cols], lora_wa[64:128, :], start=True, stop=True)
                elif name == "v":
                    mm = pe.matmul(o, lgv2[32:64, cols], lora_gv[32:64, :], start=True, stop=True)
                else:
                    pe.matmul(o, lg2[:, cols], lora_g[:, :], start=True, stop=False)
                    mm = pe.matmul(o, lgv2[0:32, cols], lora_gv[0:32, :], start=False, stop=True)
                mm.then_inc(lora_out, 1)

        def act_lora(act, part, j):
            name = part[0]
            act.wait_ge(lora_mid, after(act, lora_mid))
            if name == "w":
                op = act.activation(lora_wa[0:64, :], bank[4][0:64, 0:S], ACT.Tanh)
            elif name == "a":
                op = act.activation(lora_wa[64:128, :], bank[4][64:128, 0:S], ACT.Copy)
            elif name == "v":
                op = act.activation(lora_gv[32:64, :], bank[4][32:64, 0:S], ACT.Copy)
            else:
                act.activation(lora_g[:, :], bank[4][:, 0:S], ACT.Sigmoid)
                op = act.activation(lora_gv[0:32, :], bank[5][0:32, 0:S], ACT.Sigmoid)
            op.then_inc(lora_act, 1)
            dst = {"w": RW_CUM, "a": RW_A, "v": RW_XA, "g": RW_G}[name]
            for t in range(C):
                act.wait_ge(lora_out, after(act, lora_out))
                o, i = dst[:, t * S:(t + 1) * S], bank[4 + t % 4][:, 0:S]
                if name == "g":
                    op = act.activation(o, i, ACT.Copy)
                else:
                    b = vec("rw_v0", 0, t) if name == "v" else vec(f"rw_{name}0", j, t)
                    op = act.activation(o, i, ACT.Sigmoid, bias=b)
                op.then_inc(lora_taken, 1)

        def act_rwkv(act, layer):
            j = layer // 3
            parts = lora_parts(layer)
            act_norm(act, X, W[8])
            act_panels(act, f"rw{layer}.r")
            act_lora(act, parts[0], j)
            act_panels(act, f"rw{layer}.k")
            act_lora(act, parts[1], j)
            act_panels(act, f"rw{layer}.v")
            for part in parts[2:]:
                act_lora(act, part, j)
            act.wait_ge(head_taken, after(act, head_taken))
            act.activation(RW_BONUS[:, :], RW_BONUS[:, :], ACT.Sqrt).then_inc(root_ready, 1)
            act.wait_ge(decay_ready, after(act, decay_ready))
            act.activation(RW_CUM[:, :], RW_XB[:, :], ACT.Exp, scale=-DECAY).then_inc(exp_ready, 1)
            act.activation(RW_XB[:, :], RW_XB[:, :], ACT.Exp, scale=DECAY).then_inc(exp_ready, 1)
            act_ada_rows(act, bank[0], ADA_FIRST)
            act_ada_place(act, layer // 3, bank[0], 0, ADA_FIRST)
            for ch in range(NCH):
                for k, t in enumerate((VT, BT, CT)):
                    act.wait_ge(turned_ready, after(act, turned_ready))
                    act.activation(t, bank[5 + k % 2][:, :], ACT.Copy).then_inc(turned_taken, 1)
                act.wait_ge(rhs_ready, after(act, rhs_ready))
                act.activation(RHS, bank[3][:, :], ACT.Copy).then_inc(rhs_taken, 1)
                for lv in range(1, 6):
                    for h, banks in zip(HALF, INV_BANKS):
                        act.wait_ge(inv_half, after(act, inv_half))
                        act.activation(IT[:, h], banks[0][:, h], ACT.Copy).then_inc(inv_half_taken, 1)
                act_ada_rows(act, ADA_BANK, 4)
                for h, banks in zip(HALF, INV_BANKS):
                    act.wait_ge(sol_ready, after(act, sol_ready))
                    act.activation(SOL[:, h], banks[0][:, h], ACT.Copy, scale=-1.0).then_inc(sol_taken, 1)
                act_ada_place(act, layer // 3, ADA_BANK, ADA_FIRST + 4 * ch, 4)
            out_panels = G[f"rw{layer}.out"]
            for slot in range(RING):
                counts.start(act, raw_landed[slot], 16 * out_panels.p0 // RING)
                act_round(act, out_panels, slot)
            act.wait_ge(head_taken, after(act, head_taken))
            act.activation(RW_Y[:, :], RW_Y[:, :], ACT.Sqrt).then_inc(root_ready, 1)
            act_panels(act, f"rw{layer}.out")

        def pe_ada_panel(pe, group, j, ps, row):
            pe.wait_ge(raw_landed[j], after(pe, raw_landed[j], 16))
            for k in range(ADA_ROWS // P):
                c = j * (ADA_ROWS // P) + k
                mm = pe.matmul(ps[32 * row:32 * row + 32, :], cond[:, 32 * c:32 * c + 32], raw[j][:, k * ADA_N:(k + 1) * ADA_N],
                               start=c == 0, stop=c == C - 1)
            mm.then_inc(direct_used, 1)

        def pe_ada_turn(pe, ps, groups):
            n = 32 * groups
            pe.wait_ge(ada_rows, after(pe, ada_rows))
            for k in range(ADA_N // P):
                mm = pe.transpose(ps[:, k * P:k * P + n], ada_tok[0:n, k * P:(k + 1) * P], const("ident")[0:n, 0:n])
            mm.then_inc(ada_turned, 1)

        def act_ada_rows(act, ps, groups):
            act.wait_ge(direct_used, after(act, direct_used, RING * groups))
            act.activation(ada_tok[0:32 * groups, :], ps[0:32 * groups, :], ACT.Copy).then_inc(ada_rows, 1)

        def act_ada_place(act, l, ps, first, groups):
            act.wait_ge(ada_turned, after(act, ada_turned))
            k = ADA_N // P
            o = both[l][:, first * k * 2:(first + groups) * k * 2].rearrange("p (g k s) -> p g k s", k=k, s=2)
            for g in range(groups):
                op = act.activation(o[:, g], ps[:, :].rearrange("p (k m) -> p k m", k=k)[:, :, 32 * g:32 * g + 2], ACT.Copy)
            op.then_inc(ada_ready, 1)

        def pe_ada_start(pe, layer):
            for slot in range(RING):
                counts.start(pe, raw_landed[slot], 16 * G[f"ada{layer // 3}"].p0 // RING)
            pe.wait_ge(bank_free, tiles_of(f"rw{layer}.v"))
            for group in range(ADA_FIRST):
                for j in range(RING):
                    pe_ada_panel(pe, group, j, bank[0], group)
            pe_ada_turn(pe, bank[0], ADA_FIRST)

        def pe_scan(pe, layer):
            V = rw_values(layer)
            halves = [[(c, slice(DH * hh, DH * hh + DH)) for c in range(C // 2 * h, C // 2 * (h + 1)) for hh in range(2)]
                      for h in range(2)]
            heads = halves[0] + halves[1]
            visits = [0]

            def fill():
                ch, v = visits[0] // VISITS, visits[0] % VISITS
                visits[0] += 1
                if v < 4 * RING:
                    if ch and v == 0:
                        pe.wait_ge(ada_ready, after(pe, ada_ready))
                    pe_ada_panel(pe, ADA_FIRST + 4 * ch + v // RING, v % RING, ADA_BANK, v // RING)
                elif v == 4 * RING + 5:
                    pe_ada_turn(pe, ADA_BANK, 4)

            pe.wait_ge(scan_in, after(pe, scan_in))
            pe.wait_ge(ada_ready, after(pe, ada_ready))
            for ch in range(NCH):
                def tok(t, c, r):
                    return t[r, c * S + ch * CHUNK:c * S + (ch + 1) * CHUNK]

                def sq(t, c, r):
                    return t[r, c * DH:(c + 1) * DH]

                for k, (l, r_) in enumerate(((RW_B, RW_P), (RW_P, RW_B), (RW_C, RW_P), (RW_B, RW_Q), (RW_C, RW_Q))):
                    if ch and k == 2:
                        pe.wait_ge(state_ready, after(pe, state_ready, 2))
                    for c, r in heads:
                        mm = pe.matmul(sq(bank[k], c, r), tok(l, c, r), tok(r_, c, r), start=True, stop=True)
                    mm.then_inc(gram_ready, 1)
                for k, t in enumerate((V, RW_B, RW_C)):
                    if k == 2:
                        pe.wait_ge(turned_taken, after(pe, turned_taken))
                    for c, r in heads:
                        mm = pe.matmul(sq(bank[5 + k % 2], c, r), tok(t, c, r), const("ident")[r, r], start=True, stop=True)
                    mm.then_inc(turned_ready, 1)
                fill()
                pe.wait_ge(turned_taken, after(pe, turned_taken, 2))
                pe.wait_ge(gram_taken, after(pe, gram_taken, 5))
                for c, r in heads:
                    if ch:
                        pe.matmul(sq(bank[3], c, r), tok(RW_P, c, r), sq(STATE, c, r), start=True, stop=False)
                    mm = pe.matmul(sq(bank[3], c, r), sq(GCP, c, r), sq(VT, c, r), start=not ch, stop=True)
                mm.then_inc(rhs_ready, 1)
                for lv in range(1, 6):
                    for h in range(2):
                        fill()
                        pe.wait_ge(inv_taken, after(pe, inv_taken))
                        if lv == 1 and h == 1:
                            pe.wait_ge(rhs_taken, after(pe, rhs_taken))
                        for c, r in halves[h]:
                            mm = pe.matmul(sq(INV_BANKS[h][0], c, r), sq(LOFF, c, r), sq(IY, c, r), start=True, stop=True)
                        mm.then_inc(inv_half, 1)
                    for h in range(2):
                        fill()
                        pe.wait_ge(inv_half_taken, after(pe, inv_half_taken))
                        for c, r in halves[h]:
                            mm = pe.matmul(sq(INV_BANKS[h][1], c, r), sq(IX, c, r), sq(IT, c, r), start=True, stop=True)
                            if lv < 5:
                                mm = pe.matmul(sq(INV_BANKS[h][2], c, r), sq(IT, c, r), sq(IX, c, r), start=True, stop=True)
                        mm.then_inc(inv_off, 1)
                for h in range(2):
                    fill()
                    pe.wait_ge(inv_taken, after(pe, inv_taken))
                    for c, r in halves[h]:
                        mm = pe.matmul(sq(INV_BANKS[h][0], c, r), sq(IY, c, r), sq(RHS, c, r), start=True, stop=True)
                    mm.then_inc(sol_ready, 1)
                for h in range(2):
                    fill()
                    pe.wait_ge(sol_taken, after(pe, sol_taken))
                    for c, r in halves[h]:
                        o = sq(OUT_BANKS[h], c, r)
                        if ch:
                            pe.matmul(o, sq(STATE, c, r), tok(RW_Q, c, r), start=True, stop=False)
                        pe.matmul(o, sq(VT, c, r), sq(GCQ, c, r), start=not ch, stop=False)
                        mm = pe.matmul(o, sq(SOL, c, r), sq(GBQ, c, r), start=False, stop=True)
                    if ch < NCH - 1:
                        for c, r in halves[h]:
                            o = sq(STATE_BANKS[h], c, r)
                            pe.matmul(o, sq(CT, c, r), sq(VT, c, r), start=True, stop=False)
                            mm = pe.matmul(o, sq(BT, c, r), sq(SOL, c, r), start=False, stop=True)
                    mm.then_inc(chunk_out, 1)
            assert visits[0] == NCH * VISITS
            pe.wait_ge(ada_ready, after(pe, ada_ready))

        def pe_rwkv(pe, layer):
            parts = lora_parts(layer)
            pe_norm(pe, W[8])
            pe_panels(pe, f"rw{layer}.r")
            pe.wait_ge(lora_landed, after(pe, lora_landed, 16 * (9 if layer else 7)))
            pe_lora(pe, parts[0], first=True)
            pe_panels(pe, f"rw{layer}.k")
            pe_lora(pe, parts[1])
            pe_panels(pe, f"rw{layer}.v")
            for part in parts[2:]:
                pe_lora(pe, part)
            pe.wait_ge(lora_taken, after(pe, lora_taken, 4))
            pe_heads(pe, const("headones"), RW_D)
            pe_heads(pe, const("headones"), RW_D)
            pe_ada_start(pe, layer)
            pe_scan(pe, layer)
            pe_heads(pe, const("headones"), RW_Y)
            pe_heads(pe, const("headones"), RW_D)
            pe_panels(pe, f"rw{layer}.out")

        def dve_scan(dve, layer):
            def masked(dst, src, mask):
                return dve.tensor_tensor(dst.rearrange("p (c t) -> p c t", t=DH), src.rearrange("p (c t) -> p c t", t=DH),
                                         const(mask).unsqueeze(1).to_broadcast([P, dst.shape[1] // DH, DH]), ALU.mult)

            def eye_minus(t):
                v = t.rearrange("p (c t) -> p c t", t=DH)
                return dve.scalar_tensor_tensor(v, v, -1.0, const("eye64").unsqueeze(1).to_broadcast([P, C, DH]),
                                                ALU.mult, ALU.add)

            wend = WEND[:, :].rearrange("p (c n) -> p c n", n=NCH)
            for ch in range(NCH):
                for k, (dst, mask) in enumerate(((N_, "before"), (L_, "below"), (GCP, "before"), (GBQ, "upto"), (GCQ, "upto"))):
                    dve.wait_ge(gram_ready, after(dve, gram_ready))
                    masked(dst, bank[k][:, :], mask).then_inc(gram_taken, 1)
                    dve.wait_ge(gram_taken, after(dve, gram_taken))
                masked(IY, N_, "upper0")
                masked(IX, L_, "lower0").then_inc(dve_step, 1)
                dve.wait_ge(dve_step, after(dve, dve_step))
                eye_minus(IY).then_inc(dve_step, 1)
                dve.wait_ge(dve_step, after(dve, dve_step))
                eye_minus(IX)
                for h in HALF:
                    masked(LOFF[:, h], L_[:, h], "lower1").then_inc(inv_taken, 1)
                dve.wait_ge(inv_taken, after(dve, inv_taken, 2))
                for lv in range(1, 6):
                    for h, banks in zip(HALF, INV_BANKS):
                        dve.wait_ge(inv_off, after(dve, inv_off))
                        last = dve.tensor_tensor(IY[:, h], IY[:, h], banks[1][:, h], ALU.subtract)
                        if lv < 5:
                            dve.tensor_tensor(IX[:, h], IX[:, h], banks[2][:, h], ALU.subtract)
                            last = masked(LOFF[:, h], L_[:, h], f"lower{lv + 1}")
                        last.then_inc(inv_taken, 1)
                        dve.wait_ge(inv_taken, after(dve, inv_taken))
                for k, h in enumerate(HALF):
                    dve.wait_ge(chunk_out, after(dve, chunk_out))
                    cs = slice(k * C // 2, (k + 1) * C // 2)
                    y = dve.tensor_copy(v3(RW_Y)[:, cs, ch * CHUNK:(ch + 1) * CHUNK],
                                        OUT_BANKS[k][:, h].rearrange("p (c t) -> p c t", t=CHUNK))
                    if ch == NCH - 1:
                        continue
                    src = STATE_BANKS[k][:, h]
                    if ch:
                        dve.tensor_tensor(STATE[:, h], STATE[:, h], src, ALU.add).then_inc(dve_step, 1)
                        dve.wait_ge(dve_step, after(dve, dve_step))
                        src = STATE[:, h]
                    dve.tensor_tensor(STATE[:, h].rearrange("p (c t) -> p c t", t=DH), src.rearrange("p (c t) -> p c t", t=DH),
                                      wend[:, cs, ch:ch + 1].to_broadcast([P, C // 2, DH]), ALU.mult).then_inc(state_ready, 1)
                    dve.wait_ge(state_ready, after(dve, state_ready))
            y.then_inc(head_in, 1)
            dve.wait_ge(head_in, after(dve, head_in))

        def dve_rwkv(dve, layer):
            j = layer // 3
            V = rw_values(layer)
            dve_norm(dve, X, lambda c: vec("norm_mix", layer, c), RW_H, to_operand=False)
            h, d = v3(RW_H), v3(RW_D)
            dve.tensor_scalar(d[:, :, 0:1], h[:, :, 0:1], -1.0, None, ALU.mult)
            dve.tensor_tensor(d[:, :, 1:S], h[:, :, 0:S - 1], h[:, :, 1:S], ALU.subtract).then_inc(dve_step, 1)
            dve.wait_ge(dve_step, after(dve, dve_step))

            def mixed(k, dst):
                for c in range(C):
                    cs = slice(c * S, (c + 1) * S)
                    op = dve.scalar_tensor_tensor(dst[:, cs], RW_D[:, cs], vec("rw_mix", 6 * j + k, c), RW_H[:, cs],
                                                  ALU.mult, ALU.add)
                return op

            mixed(0, RW_XA).then_inc(dve_step, 1)
            dve.wait_ge(dve_step, after(dve, dve_step))
            split(dve, RW_XA)
            mixed(3, RW_XB).then_inc(lora_in, 1)
            dve.wait_ge(lora_in, after(dve, lora_in))
            mixed(1, RW_XA).then_inc(dve_step, 1)
            dve.wait_ge(dve_step, after(dve, dve_step))
            dve_tiles(dve, f"rw{layer}.r", take_copy(dve, RW_R))
            split(dve, RW_XA)
            dve.wait_ge(lora_mid, after(dve, lora_mid))
            mixed(4, RW_XB).then_inc(lora_in, 1)
            dve.wait_ge(lora_in, after(dve, lora_in))
            op = mixed(2, RW_XA)
            if layer:
                op.then_inc(lora_in, 1)
                dve.wait_ge(lora_in, after(dve, lora_in))
            else:
                op.then_inc(dve_step, 1)
                dve.wait_ge(dve_step, after(dve, dve_step))
            dve_tiles(dve, f"rw{layer}.k", take_copy(dve, RW_K))
            split(dve, RW_XA)
            dve.wait_ge(lora_mid, after(dve, lora_mid))
            mixed(5, RW_XB).then_inc(lora_in, 1)
            dve.wait_ge(lora_in, after(dve, lora_in))
            dve_tiles(dve, f"rw{layer}.v", take_copy(dve, V))
            dve.wait_ge(lora_taken, after(dve, lora_taken, 16))
            if layer:
                dve.wait_ge(lora_mid, after(dve, lora_mid))
                dve.wait_ge(lora_taken, after(dve, lora_taken, 8))
                dve.tensor_tensor(RW_D[:, :], VF[:, :], V[:, :], ALU.subtract).then_inc(dve_step, 1)
                dve.wait_ge(dve_step, after(dve, dve_step))
                dve.tensor_tensor(RW_D[:, :], RW_D[:, :], RW_XA[:, :], ALU.mult).then_inc(dve_step, 1)
                dve.wait_ge(dve_step, after(dve, dve_step))
                dve.tensor_tensor(V[:, :], V[:, :], RW_D[:, :], ALU.add)
            kk, b = RW_P, RW_B
            dve.tensor_tensor(v3(kk), v3(RW_K), vec_b("rw_k_k", j), ALU.mult).then_inc(dve_step, 1)
            dve.wait_ge(dve_step, after(dve, dve_step))
            dve.tensor_tensor(b[:, :], kk[:, :], kk[:, :], ALU.mult).then_inc(head_in, 1)
            dve.wait_ge(head_in, after(dve, head_in))
            t = RW_BONUS
            dve.scalar_tensor_tensor(v3(t), v3(RW_A), -1.0, vec_b("rw_k_a", j), ALU.add, ALU.mult).then_inc(dve_step, 1)
            dve.wait_ge(dve_step, after(dve, dve_step))
            dve.scalar_tensor_tensor(RW_K[:, :], t[:, :], 1.0, RW_K[:, :], ALU.add, ALU.mult).then_inc(dve_step, 1)
            dve.wait_ge(dve_step, after(dve, dve_step))
            dve_heads(dve, lambda s, ps: dve.tensor_scalar(t[:, s], ps, KK_MIN, None, ALU.max)).then_inc(head_taken, 1)
            dve.wait_ge(head_taken, after(dve, head_taken))
            dve.wait_ge(lora_mid, after(dve, lora_mid))
            for c in range(C):
                cs = slice(c * S, (c + 1) * S)
                op = dve.tensor_tensor_scan(RW_XB[:, cs], const("carry"), RW_CUM[:, cs], 0.0, ALU.mult, ALU.add)
            op.then_inc(decay_ready, 1)
            dve.wait_ge(decay_ready, after(dve, decay_ready))
            dve.tensor_tensor(b[:, :], RW_R[:, :], RW_K[:, :], ALU.mult).then_inc(dve_step, 1)
            dve.wait_ge(dve_step, after(dve, dve_step))
            dve.tensor_tensor(v3(b), v3(b), vec_b("rw_r_k", j), ALU.mult).then_inc(head_in, 1)
            dve.wait_ge(head_in, after(dve, head_in))
            dve.wait_ge(root_ready, after(dve, root_ready))
            dve.reciprocal(t[:, :], t[:, :]).then_inc(dve_step, 1)
            dve.wait_ge(dve_step, after(dve, dve_step))
            dve.tensor_tensor(kk[:, :], kk[:, :], t[:, :], ALU.mult).then_inc(dve_step, 1)
            dve.wait_ge(dve_step, after(dve, dve_step))
            dve_heads(dve, lambda s, ps: dve.tensor_tensor(t[:, s], ps, V[:, s], ALU.mult))
            dve.tensor_tensor(b[:, :], kk[:, :], RW_A[:, :], ALU.mult).then_inc(dve_step, 1)
            dve.wait_ge(dve_step, after(dve, dve_step))
            dve.wait_ge(exp_ready, after(dve, exp_ready))
            g64 = [x[:, :].rearrange("p (g t) -> p g t", t=CHUNK) for x in (kk, RW_CUM)]
            dve.tensor_tensor(g64[0][:, :, 1:CHUNK], g64[0][:, :, 1:CHUNK], g64[1][:, :, 0:CHUNK - 1], ALU.mult)
            dve.tensor_copy(WEND[:, :].unsqueeze(2), g64[1][:, :, CHUNK - 1:CHUNK])
            dve.tensor_tensor(RW_Q[:, :], RW_R[:, :], RW_CUM[:, :], ALU.mult)
            dve.wait_ge(exp_ready, after(dve, exp_ready))
            dve.tensor_tensor(RW_C[:, :], RW_K[:, :], RW_XB[:, :], ALU.mult)
            dve.tensor_tensor(b[:, :], b[:, :], RW_XB[:, :], ALU.mult).then_inc(scan_in, 1)
            dve.wait_ge(scan_in, after(dve, scan_in))
            dve_scan(dve, layer)
            y, yc = RW_Y, RW_P
            dve_heads(dve, lambda s, ps: dve.scalar_tensor_tensor(
                yc[:, s], ps, -1.0 / DH, y[:, s], ALU.mult, ALU.add)).then_inc(dve_step, 1)
            dve.wait_ge(dve_step, after(dve, dve_step))
            dve.tensor_tensor(b[:, :], yc[:, :], yc[:, :], ALU.mult).then_inc(head_in, 1)
            dve.wait_ge(head_in, after(dve, head_in))
            dve_heads(dve, lambda s, ps: dve.tensor_scalar(y[:, s], ps, 1.0 / DH, GN_EPS, ALU.mult, ALU.add)).then_inc(head_taken, 1)
            dve.wait_ge(head_taken, after(dve, head_taken))
            dve.wait_ge(root_ready, after(dve, root_ready))
            dve.reciprocal(y[:, :], y[:, :]).then_inc(dve_step, 1)
            dve.wait_ge(dve_step, after(dve, dve_step))
            dve.tensor_tensor(yc[:, :], yc[:, :], y[:, :], ALU.mult).then_inc(dve_step, 1)
            dve.wait_ge(dve_step, after(dve, dve_step))
            dve.wait_ge(lora_taken, after(dve, lora_taken, 8))
            for c in range(C):
                cs = slice(c * S, (c + 1) * S)
                op = dve.scalar_tensor_tensor(yc[:, cs], yc[:, cs], vec("rw_ln_w", j, c), RW_BONUS[:, cs], ALU.mult, ALU.add)
            op.then_inc(dve_step, 1)
            dve.wait_ge(dve_step, after(dve, dve_step))
            for c in range(C):
                cs = slice(c * S, (c + 1) * S)
                op = dve.scalar_tensor_tensor(yc[:, cs], yc[:, cs], vec("rw_ln_b", j, c), RW_G[:, cs], ALU.add, ALU.mult)
            op.then_inc(dve_step, 1)
            dve.wait_ge(dve_step, after(dve, dve_step))
            split(dve, yc)
            dve_tiles(dve, f"rw{layer}.out", take_residual(dve, X))

        Q_, K_, VT_, O_ = W[3], W[4], W[5], W[6]
        HS = TT * S

        def slots(t, n=4):
            return [t[:, k * HS:(k + 1) * HS] for k in range(n)]

        SB_E, SB_ATT = slots(W[0])[0:2], slots(W[0])[2:4]
        SB_SP, SB_MASKED = slots(W[1])[0:2], slots(W[1])[2:4]
        SB_Z, SB_LOG = slots(W[2])[0:2], slots(W[2])[2:4]

        def head_rows(hd):
            return slice(DH * (hd % 2), DH * (hd % 2) + DH), hd // 2

        def pe_sb(pe):
            pe_norm(pe, W[8])
            for n in "qkv":
                pe_panels(pe, f"sb.{n}", fills=1 if n == "q" else 0)
            pe.wait_ge(bank_free, tiles_of("sb.v"))

            def scores(hd):
                r, c = head_rows(hd)
                if hd >= 2:
                    pe.wait_ge(logit_ready, after(pe, logit_ready))
                for st in range(TT):
                    mm = pe.matmul(bank[4 + hd % 2][:, st * S:(st + 1) * S], K_[r, c * S + st * P:c * S + (st + 1) * P],
                                   Q_[r, c * S:(c + 1) * S], start=True, stop=True)
                mm.then_inc(z_ready, 1)

            def output(hd):
                r, c = head_rows(hd)
                pe.wait_ge(att_ready, after(pe, att_ready))
                if hd % 2 == 0 and hd >= 4:
                    pe.wait_ge(heads_taken, after(pe, heads_taken))
                for st in range(TT):
                    mm = pe.matmul(bank[c % 2][r, 0:S], VT_[:, st * D + hd * DH:st * D + (hd + 1) * DH],
                                   SB_ATT[hd % 2][:, st * S:(st + 1) * S], start=st == 0, stop=st == TT - 1)
                if hd % 2:
                    mm.then_inc(heads_out, 1)

            scores(0)
            for hd in range(H):
                if hd + 1 < H:
                    scores(hd + 1)
                pe.wait_ge(later_in, after(pe, later_in))
                m, o = SB_MASKED[hd % 2], bank[6 + hd % 2]
                pe.matmul(o[:, 0:S], const("after"), m[:, 0:S], start=True, stop=False)
                pe.matmul(o[:, 0:S], ones[:, :], m[:, S:2 * S], start=False, stop=True)
                pe.matmul(o[:, S:2 * S], const("after"), m[:, S:2 * S], start=True, stop=True).then_inc(later_ready, 1)
                if hd:
                    output(hd - 1)
            output(H - 1)
            pe.wait_ge(logit_ready, after(pe, logit_ready, 2))
            pe.wait_ge(heads_taken, after(pe, heads_taken, 2))
            pe_panels(pe, "sb.out")

        def act_sb(act):
            act_norm(act, X, W[8])
            for n in "qkv":
                act_panels(act, f"sb.{n}")

            def softplus(hd):
                e = SB_E[hd % 2]
                act.wait_ge(z_ready, after(act, z_ready))
                if hd >= 2:
                    act.wait_ge(later_in, after(act, later_in))
                act.activation(e, bank[4 + hd % 2][:, :], ACT.Abs).then_inc(act_step, 1)
                act.wait_ge(act_step, after(act, act_step))
                act.activation(e, e, ACT.Exp, scale=-1.0).then_inc(act_step, 1)
                act.wait_ge(act_step, after(act, act_step))
                act.activation(e, e, ACT.Ln, bias=1.0).then_inc(exps_ready, 1)

            softplus(0)
            for hd in range(H):
                if hd + 1 < H:
                    softplus(hd + 1)
                act.wait_ge(logit_ready, after(act, logit_ready))
                if hd % 2 == 0 and hd:
                    act.wait_ge(heads_out, after(act, heads_out))
                act.activation(SB_ATT[hd % 2], SB_LOG[hd % 2], ACT.Exp).then_inc(att_raw, 1)
            act.wait_ge(later_in, after(act, later_in, 2))
            act.wait_ge(heads_out, after(act, heads_out))
            act_panels(act, "sb.out")

        def dve_sb(dve, layer):
            dve_norm(dve, X, lambda c: vec("norm_mix", layer, c), W[0])
            dve_tiles(dve, "sb.q", take_copy(dve, Q_, DH ** -0.5))
            dve_tiles(dve, "sb.k", take_copy(dve, K_))
            dve_tiles(dve, "sb.v", take_tokens(dve, VT_[:, :].rearrange("p (a m) -> p a m", m=D)))

            def masked(hd):
                b = hd % 2
                dve.wait_ge(exps_ready, after(dve, exps_ready))
                ps = bank[4 + b][:, :]
                dve.scalar_tensor_tensor(SB_SP[b], ps, 0.0, SB_E[b], ALU.max, ALU.add).then_inc(dve_step, 1)
                dve.wait_ge(dve_step, after(dve, dve_step))
                dve.tensor_tensor(SB_MASKED[b], SB_SP[b], const("earlier"), ALU.mult).then_inc(later_in, 1)
                dve.wait_ge(later_in, after(dve, later_in))
                dve.tensor_tensor(SB_Z[b], ps, SB_SP[b], ALU.subtract).then_inc(dve_step, 1)
                dve.wait_ge(dve_step, after(dve, dve_step))

            def logits(hd):
                b = hd % 2
                dve.wait_ge(later_ready, after(dve, later_ready))
                dve.tensor_tensor(SB_LOG[b], SB_Z[b], bank[6 + b][:, :], ALU.subtract).then_inc(logit_ready, 1)
                dve.wait_ge(logit_ready, after(dve, logit_ready))

            def weights(hd):
                dve.wait_ge(att_raw, after(dve, att_raw))
                dve.tensor_tensor(SB_ATT[hd % 2], SB_ATT[hd % 2], const("earlier"), ALU.mult).then_inc(att_ready, 1)
                dve.wait_ge(att_ready, after(dve, att_ready))
                if hd % 2:
                    dve.wait_ge(heads_out, after(dve, heads_out))
                    c = hd // 2
                    dve.tensor_copy(O_[:, c * S:(c + 1) * S], bank[c % 2][:, 0:S]).then_inc(heads_taken, 1)
                    dve.wait_ge(heads_taken, after(dve, heads_taken))

            masked(0)
            for hd in range(H):
                if hd + 1 < H:
                    masked(hd + 1)
                logits(hd)
                weights(hd)
            split(dve, O_)
            dve_tiles(dve, "sb.out", take_residual(dve, X))

        DS_QI, DS_T = W[5], W[6]
        DS_Q, DS_K, DS_V, DS_O = W[1], W[2], W[3], W[4]
        kiw = sb("kiw", C * P, at=l_at)
        wiw = sb("wiw", C * IDX_H, at=l_at + C * P * 4)
        WI = sb("WI", TT * IDX_H)
        SC, SC2, SEL = W[7][:, 0:HS], W[7][:, HS:2 * HS], W[7][:, 2 * HS:3 * HS]
        IDX = [W[8][:, k * HS:(k + 1) * HS] for k in range(2)]
        best = sb("best", TT * 8)
        DS_L = slots(W[0])[0:2]
        DS_PT = slots(W[0])[2:4]
        top = sb("top", 4 * TT)
        DS_COLS = 3 * D + IDX_H * DH

        def sp_ds_small(sp):
            w = a["ds_w_in"][0]
            for k in range(2):
                sp.dma_start(
                    kiw[:, :].rearrange("p (c m) -> p c m", m=P)[:, :, k * DH:(k + 1) * DH],
                    w[:, DS_COLS:DS_COLS + DH].rearrange("(c p) m -> p c m", p=P)).then_inc(small_landed, 16)
            sp.dma_start(wiw[:, :].rearrange("p (c m) -> p c m", m=IDX_H),
                                         w[:, DS_COLS + DH:DS_COLS + DH + IDX_H].rearrange("(c p) m -> p c m", p=P)).then_inc(small_landed, 16)

        def pe_ds(pe):
            pe_norm(pe, W[8])
            pe_panels(pe, "ds.q")
            pe.wait_ge(small_landed, after(pe, small_landed, 48))
            for c in range(C):
                mm = pe.matmul(bank[4][:, 0:S], kiw[:, c * P:(c + 1) * P], W[0][:, c * S:(c + 1) * S],
                               start=c == 0, stop=c == C - 1)
            mm.then_inc(small_ready, 1)
            for tt in range(TT):
                for c in range(C):
                    mm = pe.matmul(bank[5][:, tt * IDX_H:(tt + 1) * IDX_H], W[0][:, c * S + tt * P:c * S + (tt + 1) * P],
                                   wiw[:, c * IDX_H:(c + 1) * IDX_H], start=c == 0, stop=c == C - 1)
            mm.then_inc(small_ready, 1)
            for n in ("k", "v", "qi"):
                pe_panels(pe, f"ds.{n}", fills=0)
            for t in (DS_Q, DS_K):
                pe_heads(pe, const("headones"), DS_T)
                pe_heads(pe, const("rot_head"), t)
            pe_heads(pe, const("rot_head"), DS_QI, chunks=5)
            pe.wait_ge(head_in, after(pe, head_in))
            for hd in range(IDX_H):
                r, c = head_rows(hd)
                if hd >= 2:
                    pe.wait_ge(idx_act, after(pe, idx_act))
                for qt in range(TT):
                    mm = pe.matmul(bank[4 + hd % 2][:, qt * S:(qt + 1) * S],
                                   DS_QI[r, c * S + qt * P:c * S + (qt + 1) * P], DS_QI[r, 4 * S:5 * S],
                                   start=True, stop=True)
                mm.then_inc(idx_ready, 1)
            pe.wait_ge(idx_act, after(pe, idx_act, 2))
            pe.wait_ge(bank_free, tiles_of("ds.qi"))

            def scores(hd):
                r, c = head_rows(hd)
                if hd >= 2:
                    pe.wait_ge(logit_ready, after(pe, logit_ready))
                for qt in range(TT):
                    mm = pe.matmul(bank[4 + hd % 2][:, qt * S:(qt + 1) * S], DS_Q[r, c * S + qt * P:c * S + (qt + 1) * P],
                                   DS_K[r, c * S:(c + 1) * S], start=True, stop=True)
                mm.then_inc(ds_z_ready, 1)

            def turn(hd):
                pe.wait_ge(att_ready, after(pe, att_ready))
                for qt in range(TT):
                    for st in range(TT):
                        mm = pe.transpose(bank[6 + hd % 2][:, st * S + qt * P:st * S + (qt + 1) * P],
                                          DS_L[hd % 2][:, qt * S + st * P:qt * S + (st + 1) * P], const("ident"))
                mm.then_inc(att_turned, 1)

            def output(hd):
                r, c = head_rows(hd)
                pe.wait_ge(att_turned_taken, after(pe, att_turned_taken))
                if hd % 2 == 0 and hd >= 4:
                    pe.wait_ge(heads_taken, after(pe, heads_taken))
                for st in range(TT):
                    mm = pe.matmul(bank[c % 2][r, 0:S], DS_V[:, st * D + hd * DH:st * D + (hd + 1) * DH],
                                   DS_PT[hd % 2][:, st * S:(st + 1) * S], start=st == 0, stop=st == TT - 1)
                mm.then_inc(heads_out, 1)

            scores(0)
            scores(1)
            for hd in range(H):
                turn(hd)
                if hd + 2 < H:
                    scores(hd + 2)
                if hd:
                    output(hd - 1)
            output(H - 1)
            pe.wait_ge(logit_ready, after(pe, logit_ready, 2))
            pe.wait_ge(heads_taken, after(pe, heads_taken, 2))
            pe_panels(pe, "ds.out")

        def act_ds(act):
            act_norm(act, X, W[8])
            act_panels(act, "ds.q")
            for n in ("k", "v", "qi"):
                act_panels(act, f"ds.{n}")
            for _ in range(2):
                act.wait_ge(head_taken, after(act, head_taken))
                act.activation(DS_T[:, :], DS_T[:, :], ACT.Sqrt).then_inc(root_ready, 1)
            for n in range(IDX_H):
                act.wait_ge(idx_ready, after(act, idx_ready))
                if n >= 2:
                    act.wait_ge(idx_taken, after(act, idx_taken))
                act.activation(IDX[n % 2], bank[4 + n % 2][:, :], ACT.Relu).then_inc(idx_act, 1)
            act.wait_ge(idx_taken, after(act, idx_taken, 2))

            def powers(hd):
                b = hd % 2
                act.wait_ge(logit_ready, after(act, logit_ready))
                for qt in range(TT):
                    l = DS_L[b][:, qt * S:(qt + 1) * S]
                    op = act.activation(l, l, ACT.Exp, bias=top[:, 4 * b + qt:4 * b + qt + 1],
                                        accum_out=top[:, 4 * b + 2 + qt:4 * b + 3 + qt])
                op.then_inc(exps_ready, 1)

            def turned(hd):
                act.wait_ge(att_turned, after(act, att_turned))
                if hd >= 2:
                    act.wait_ge(heads_out, after(act, heads_out))
                act.activation(DS_PT[hd % 2], bank[6 + hd % 2][:, :], ACT.Copy).then_inc(att_turned_taken, 1)

            powers(0)
            for hd in range(H):
                if hd + 1 < H:
                    powers(hd + 1)
                turned(hd)
            act.wait_ge(heads_out, after(act, heads_out, 2))
            act_panels(act, "ds.out")

        def dve_ds(dve, layer):
            dve_norm(dve, X, lambda c: vec("norm_mix", layer, c), W[0])
            dve_tiles(dve, "ds.q", take_copy(dve, DS_Q))
            dve.wait_ge(small_ready, after(dve, small_ready))
            dve.tensor_copy(DS_QI[:, 4 * S:5 * S], bank[4][:, 0:S])
            dve.wait_ge(small_ready, after(dve, small_ready))
            dve.tensor_scalar(WI[:, :], bank[5][:, 0:TT * IDX_H], IDX_H ** -0.5 * DH ** -0.5, None, ALU.mult)
            dve_tiles(dve, "ds.k", take_copy(dve, DS_K))
            dve_tiles(dve, "ds.v", take_tokens(dve, DS_V[:, :].rearrange("p (a m) -> p a m", m=D)))
            dve_tiles(dve, "ds.qi", take_copy(dve, DS_QI))

            def rope(t, chunks=C):
                n = chunks * S

                def over(name, k):
                    return const(name).unsqueeze(1).to_broadcast([P, k, S])

                def times_sin(s, ps):
                    k = (s.stop - s.start) // S
                    return dve.tensor_tensor(DS_T[:, s].rearrange("p (c t) -> p c t", t=S),
                                             ps.rearrange("p (c t) -> p c t", t=S), over("sin_head", k), ALU.mult)
                dve_heads(dve, times_sin, chunks)
                v = v3(t)[:, 0:chunks]
                dve.tensor_tensor(v, v, over("cos_head", chunks), ALU.mult).then_inc(dve_step, 1)
                dve.wait_ge(dve_step, after(dve, dve_step))
                return dve.tensor_tensor(t[:, 0:n], t[:, 0:n], DS_T[:, 0:n], ALU.add)

            for k, t in enumerate((DS_Q, DS_K)):
                dve.tensor_tensor(DS_T[:, :], t[:, :], t[:, :], ALU.mult).then_inc(head_in, 1)
                dve.wait_ge(head_in, after(dve, head_in))
                dve_heads(dve, lambda s, ps: dve.tensor_scalar(DS_T[:, s], ps, 1.0 / DH, EPS, ALU.mult, ALU.add)).then_inc(head_taken, 1)
                dve.wait_ge(head_taken, after(dve, head_taken))
                dve.wait_ge(root_ready, after(dve, root_ready))
                dve.reciprocal(DS_T[:, :], DS_T[:, :]).then_inc(dve_step, 1)
                dve.wait_ge(dve_step, after(dve, dve_step))
                dve.scalar_tensor_tensor(t[:, :], t[:, :], VEC3[:, k:k + 1], DS_T[:, :], ALU.mult, ALU.mult).then_inc(head_in, 1)
                dve.wait_ge(head_in, after(dve, head_in))
                rope(t).then_inc(dve_step, 1)
                dve.wait_ge(dve_step, after(dve, dve_step))
            dve.memset(SC, 0.0).then_inc(dve_step, 1)
            dve.wait_ge(dve_step, after(dve, dve_step))
            dve.memset(SEL, 0.0).then_inc(head_in, 1)
            dve.wait_ge(head_in, after(dve, head_in))
            rope(DS_QI, 5).then_inc(head_in, 1)
            dve.wait_ge(head_in, after(dve, head_in))
            for hd in range(IDX_H):
                dve.wait_ge(idx_act, after(dve, idx_act))
                for qt in range(TT):
                    o = SC[:, qt * S:(qt + 1) * S]
                    op = dve.scalar_tensor_tensor(o, IDX[hd % 2][:, qt * S:(qt + 1) * S],
                                                  WI[:, qt * IDX_H + hd:qt * IDX_H + hd + 1], o, ALU.mult, ALU.add)
                op.then_inc(idx_taken, 1)
                dve.wait_ge(idx_taken, after(dve, idx_taken))
            for qt in range(TT):
                for hh in range(2):
                    seen = qt * P + (hh + 1) * CHUNK
                    if seen < S:
                        op = dve.memset(SC[hh * DH:(hh + 1) * DH, qt * S + seen:(qt + 1) * S], NEG)
            op.then_inc(dve_step, 1)
            dve.wait_ge(dve_step, after(dve, dve_step))
            dve.tensor_copy(SC2, SC).then_inc(dve_step, 1)
            dve.wait_ge(dve_step, after(dve, dve_step))
            for n in range(TOPK // 8):
                for qt in range(TT):
                    op = dve.max(best[:, qt * 8:(qt + 1) * 8], SC2[:, qt * S:(qt + 1) * S])
                op.then_inc(dve_step, 1)
                dve.wait_ge(dve_step, after(dve, dve_step))
                for qt in range(TT):
                    o = SC2[:, qt * S:(qt + 1) * S]
                    op = dve.match_replace(o, best[:, qt * 8:(qt + 1) * 8], o, TAKEN)
                op.then_inc(dve_step, 1)
                dve.wait_ge(dve_step, after(dve, dve_step))
            dve.tensor_tensor(SEL, SC2, SC, ALU.is_equal).then_inc(dve_step, 1)
            dve.wait_ge(dve_step, after(dve, dve_step))
            dve.tensor_scalar(SEL, SEL, HIDE, None, ALU.mult).then_inc(dve_step, 1)
            dve.wait_ge(dve_step, after(dve, dve_step))

            def logits(hd):
                b = hd % 2
                dve.wait_ge(ds_z_ready, after(dve, ds_z_ready))
                if hd >= 2:
                    dve.wait_ge(att_turned, after(dve, att_turned))
                l = DS_L[b]
                dve.scalar_tensor_tensor(l, bank[4 + b][:, :], DH ** -0.5, SEL, ALU.mult, ALU.add).then_inc(dve_step, 1)
                dve.wait_ge(dve_step, after(dve, dve_step))
                t = top[:, 4 * b:4 * b + 2]
                dve.tensor_reduce(t, l.rearrange("p (a s) -> p a s", s=S), AX_X, ALU.max).then_inc(dve_step, 1)
                dve.wait_ge(dve_step, after(dve, dve_step))
                dve.tensor_scalar(t, t, -1.0, None, ALU.mult).then_inc(logit_ready, 1)
                dve.wait_ge(logit_ready, after(dve, logit_ready))

            def weights(hd):
                b = hd % 2
                dve.wait_ge(exps_ready, after(dve, exps_ready))
                t = top[:, 4 * b + 2:4 * b + 4]
                dve.reciprocal(t, t).then_inc(dve_step, 1)
                dve.wait_ge(dve_step, after(dve, dve_step))
                for qt in range(TT):
                    l = DS_L[b][:, qt * S:(qt + 1) * S]
                    op = dve.tensor_scalar(l, l, t[:, qt:qt + 1], None, ALU.mult)
                op.then_inc(att_ready, 1)
                dve.wait_ge(att_ready, after(dve, att_ready))

            def store(hd):
                dve.wait_ge(heads_out, after(dve, heads_out, 2))
                c = hd // 2
                dve.tensor_copy(DS_O[:, c * S:(c + 1) * S], bank[c % 2][:, 0:S]).then_inc(heads_taken, 1)
                dve.wait_ge(heads_taken, after(dve, heads_taken))

            logits(0)
            for hd in range(H):
                if hd + 1 < H:
                    logits(hd + 1)
                weights(hd)
                if hd % 2 == 0 and hd:
                    store(hd - 1)
            store(H - 1)
            dve.wait_ge(att_turned, after(dve, att_turned, 2))
            split(dve, DS_O)
            dve_tiles(dve, "ds.out", take_residual(dve, X))

        ROWS, ROWS2, ROWS3, XROWS = W[0], W[1][:, 0:CF_W], W[1][:, CF_W:CF_W + P], W[2]
        OUTROWS = W[2]

        def table_view(name):
            t = a[name]
            if name == "rw_mix":
                return t.rearrange("a b d -> (a b) d")
            if name == "rw_r_k":
                return t.rearrange("a h d -> a (h d)")
            if name == "b_ada_2":
                return t.rearrange("l (n d) -> (l n) d", d=D)
            if name in ("norm_g_2", "conv_a_w_2", "conf_dw_2"):
                return t.rearrange("l k d -> (l k) d")
            if name in ("c_ctx_2", "final_g_2"):
                return t.rearrange("(a d) -> a d", a=1)
            return t

        def sp_setup(sp):
            sp.dma_start(cst[:, :], a["const"]).then_inc(const_landed, 16)
            sp.dma_start(XROWS[:, :].rearrange("p (a d) -> p a d", d=D),
                                          a["x"][0].rearrange("(a p) d -> p a d", p=P)).then_inc(x_rows_landed, 16)
            for name, at, k in VEC_ROWS:
                sp.dma_start(ROWS[at:at + k, 0:D], table_view(name)).then_inc(rows_landed, 16)
            for name, at, k in VEC2_ROWS:
                sp.dma_start(ROWS2[at:at + k, :], table_view(name)).then_inc(rows_landed, 16)
            for half in range(2):
                o = slice(half * DH, half * DH + DH)
                sp.dma_start(ROWS3[0:1, o], a["ds_q_norm"]).then_inc(rows_landed, 16)
                sp.dma_start(ROWS3[1:2, o], a["ds_k_norm"]).then_inc(rows_landed, 16)
                sp.dma_start(ROWS3[2:10, o], a["lam_p_2"].rearrange("l k d -> (l k) d")).then_inc(rows_landed, 16)
            sp.dma_start(ROWS3[10:12, :], a["subln_g_2"]).then_inc(rows_landed, 16)

        N_TABLES = len(VEC_ROWS) + len(VEC2_ROWS) + 7

        def pe_turn_in(pe, src):
            for k in range(4):
                for c in (2 * k, 2 * k + 1):
                    for tt in range(TT):
                        o = (c % 2) * S + tt * P
                        mm = pe.transpose(bank[k][:, o:o + P], src[:, tt * D + c * P:tt * D + (c + 1) * P], const("ident"))
                mm.then_inc(x_turned, 1)

        def pe_setup(pe):
            pe.wait_ge(const_landed, after(pe, const_landed, 16))
            pe.wait_ge(x_rows_landed, after(pe, x_rows_landed, 16))
            pe_turn_in(pe, XROWS)
            pe.wait_ge(rows_landed, after(pe, rows_landed, 16 * N_TABLES))
            for c in range(C):
                mm = pe.transpose(bank[4][:, c * NV:(c + 1) * NV], ROWS[0:NV, c * P:(c + 1) * P], const("ident")[0:NV, 0:NV])
            mm.then_inc(vec_turned, 1)
            for c in range(2):
                pe.transpose(bank[5][:, c * NV2:(c + 1) * NV2], ROWS2[0:NV2, c * P:(c + 1) * P], const("ident")[0:NV2, 0:NV2])
            pe.transpose(bank[5][:, 2 * NV2:2 * NV2 + 12], ROWS3[0:12, :], const("ident")[0:12, 0:12]).then_inc(vec_turned, 1)
            pe.wait_ge(consts_set, after(pe, consts_set))

        def dve_turn_in(dve, dst):
            for k in range(4):
                dve.wait_ge(x_turned, after(dve, x_turned))
                dve.tensor_copy(dst[:, k * 2 * S:(k + 1) * 2 * S], bank[k][:, :]).then_inc(x_ready, 1)
                dve.wait_ge(x_ready, after(dve, x_ready))

        def dve_setup(dve):
            dve.memset(eps[:, 0:1], EPS)
            dve.memset(cond[:, :], 0.0)
            dve.memset(ones[:, :], 1.0).then_inc(consts_set, 1)
            dve.wait_ge(consts_set, after(dve, consts_set))
            dve_turn_in(dve, X)
            dve.wait_ge(vec_turned, after(dve, vec_turned))
            dve.tensor_copy(VEC[:, :], bank[4][:, 0:C * NV]).then_inc(vec_ready, 1)
            dve.wait_ge(vec_ready, after(dve, vec_ready))
            dve.wait_ge(vec_turned, after(dve, vec_turned))
            dve.tensor_copy(VEC2[:, :], bank[5][:, 0:2 * NV2])
            dve.tensor_copy(VEC3[:, :], bank[5][:, 2 * NV2:2 * NV2 + 12]).then_inc(vec_ready, 1)
            dve.wait_ge(vec_ready, after(dve, vec_ready))

        def act_input(act):
            act.wait_ge(consts_set, after(act, consts_set))
            act.wait_ge(vec_ready, after(act, vec_ready, 2))
            act.wait_ge(x_ready, after(act, x_ready, 4))

        def pe_turn_out(pe, src):
            pe.wait_ge(turn_in, after(pe, turn_in))
            for k in range(4):
                tt, half = k // 2, k % 2
                for q in range(4):
                    c = half * 4 + q
                    mm = pe.transpose(bank[k][:, q * P:(q + 1) * P], src[:, c * S + tt * P:c * S + (tt + 1) * P], const("ident"))
                mm.then_inc(turned_out, 1)

        def dve_turn_out(dve):
            for k in range(4):
                dve.wait_ge(turned_out, after(dve, turned_out))
                dve.tensor_copy(OUTROWS[:, k * 512:(k + 1) * 512], bank[k][:, :]).then_inc(out_ready, 1)
                dve.wait_ge(out_ready, after(dve, out_ready))

        def sp_out(sp):
            for tt in range(TT):
                sp.wait_ge(out_ready, after(sp, out_ready, 2))
                sp.dma_start(out[0, tt * P:(tt + 1) * P, :], OUTROWS[:, tt * D:(tt + 1) * D]).then_inc(out_landed, 16)
            sp.wait_ge(out_landed, after(sp, out_landed, 16 * TT))

        STREAM = {"x": X, "c": CTX}
        MOD = {s: sb(f"mod_{s}", N_MOD * C) for s in "xc"}
        GAIN = {s: sb(f"gain_{s}", 3 * C) for s in "xc"}
        LAM = sb("LAM", 8)
        lam_init = [0.8 - 0.6 * float(np.exp(-0.3 * l)) for l in range(D2)]

        def act_cond(act):
            for n, name in enumerate(("c_2", "c_ctx_2")):
                op = act.activation(cond[:, :].rearrange("p (c n) -> p c n", n=32)[:, :, n:n + 1],
                                    VEC_v[:, :, VAT[name]:VAT[name] + 1], ACT.Silu)
            op.then_inc(cond_ready, 1)

        def act_ada(act):
            act.wait_ge(lam_sums, after(act, lam_sums))
            act.activation(LAM[:, 0:2], bank[5][:, 0:2], ACT.Exp).then_inc(lam_exp, 1)

        def pe_ada(pe):
            pe.wait_ge(lam_in, after(pe, lam_in))
            pe.matmul(bank[5][:, 0:2], const("headones"), LAM[:, 2:4], start=True, stop=True).then_inc(lam_sums, 1)

        def dve_ada(dve, l):
            dve.wait_ge(ada_ready, (1 + NCH) * (l + 1))
            b4 = both[l][:, :].rearrange("p (n c s) -> p n c s", c=C, s=2)
            row = VAT["b_ada_2"] + l * N_MOD
            bias = VEC_v[:, :, row:row + N_MOD].rearrange("p c n -> p n c")
            for k, s in enumerate("xc"):
                m = MOD[s][:, :]
                dve.tensor_tensor(m.rearrange("p (n c) -> p n c", c=C), b4[:, :, :, k], bias, ALU.add).then_inc(dve_step, 1)
                dve.wait_ge(dve_step, after(dve, dve_step))
                for n in range(3):
                    g = VAT["norm_g_2"] + 3 * l + n
                    dve.scalar_tensor_tensor(
                        GAIN[s][:, n * C:(n + 1) * C], m[:, (3 * n + 1) * C:(3 * n + 2) * C], 1.0,
                        VEC_v[:, :, g], ALU.add, ALU.mult).then_inc(dve_step, 1)
                    dve.wait_ge(dve_step, after(dve, dve_step))
                for n in (0, 2):
                    o = m[:, (3 * n + 2) * C:(3 * n + 3) * C]
                    dve.tensor_scalar(o, o, 0.5, None, ALU.mult).then_inc(dve_step, 1)
                    dve.wait_ge(dve_step, after(dve, dve_step))
            v = VEC3[:, 2 + 4 * l:6 + 4 * l].rearrange("p (a b) -> p a b", b=2)
            dve.tensor_tensor(LAM[:, 2:4], v[:, :, 0], v[:, :, 1], ALU.mult).then_inc(lam_in, 1)
            dve.wait_ge(lam_in, after(dve, lam_in))
            dve.wait_ge(lam_exp, after(dve, lam_exp))
            dve.tensor_tensor(LAM[:, 4:5], LAM[:, 1:2], LAM[:, 0:1], ALU.subtract).then_inc(dve_step, 1)
            dve.wait_ge(dve_step, after(dve, dve_step))
            dve.tensor_scalar(LAM[:, 5:6], LAM[:, 4:5], -lam_init[l], None, ALU.add).then_inc(dve_step, 1)
            dve.wait_ge(dve_step, after(dve, dve_step))

        def mod(s, n):
            return lambda c: MOD[s][:, n * C + c:n * C + c + 1]

        def mod_gate(s, n):
            return MOD[s][:, n * C:(n + 1) * C]

        def gain(s, n):
            return lambda c: GAIN[s][:, n * C + c:n * C + c + 1]

        def dve_ffn2(dve, name, s, n):
            dve_ffn(dve, name, STREAM[s], gain(s, n), mod(s, 3 * n), mod_gate(s, 3 * n + 2))

        AB = sb("AB", 10 * S, at=w_at[0])
        D_ = W[2][:, 0:4 * S]
        LN_SQ = W[2][:, 4 * S:6 * S]
        LN_STD = W[2][:, 6 * S:7 * S]
        MERGED = W[3]
        DQ, DK = W[4][:, 0:4 * S], W[4][:, 4 * S:8 * S]
        KC, VC = VF[:, 0:4 * S], VF[:, 4 * S:8 * S]
        DV, DO = W[5][:, 0:4 * S], W[5][:, 4 * S:8 * S]
        DP = [[W[6][:, (2 * b + m) * HS:(2 * b + m + 1) * HS] for m in range(2)] for b in range(2)]
        DAT = [W[7][:, b * HS:(b + 1) * HS] for b in range(2)]
        da_top = sb("da_top", 8)
        T2 = W[7][:, 2 * HS:4 * HS]
        V_TOK = W[8][:, 0:HS]
        SGW, SGWT = W[8][:, HS:2 * HS], W[8][:, 2 * HS:3 * HS]
        SGB = W[8][:, 3 * HS:3 * HS + 2 * P]
        PADW = S + CF_K - 1
        PAD = AB[:, 0:2 * PADW]

        def v2vec(name, row, c):
            o = V2AT[name] + row
            return VEC2_v[:, c, o:o + 1]

        def sp_gated_unit(sp, l):
            sp.wait_ge(sgu_free, after(sp, sgu_free))
            sp.dma_start(SGW.rearrange("p (g q) -> p g q", q=P),
                                       a["sgu_w_2"][l].rearrange("g p q -> p g q")).then_inc(sgu_landed, 16)
            for g in range(SG_G):
                sp.dma_start(SGB[DH * (g % 2):DH * (g % 2) + DH, (g // 2) * P:(g // 2 + 1) * P],
                                           a["sgu_b_2"][l, g].partition_broadcast(DH)).then_inc(sgu_landed, 16)

        def keys_of(s):
            return [(DK, DV), (KC, VC)] if s == "x" else [(KC, VC)]

        def pe_total(pe, src, chunks=2):
            pe.wait_ge(head_in, after(pe, head_in))
            for c in range(chunks):
                mm = pe.matmul(bank[4][:, 0:S], ones[:, :], src[:, c * S:(c + 1) * S], start=c == 0, stop=c == chunks - 1)
            mm.then_inc(head_sums, 1)

        def dve_layer_norm(dve, t):
            def centre():
                dve.wait_ge(head_sums, after(dve, head_sums))
                for c in range(2):
                    o = t[:, c * S:(c + 1) * S]
                    op = dve.scalar_tensor_tensor(o, bank[4][:, 0:S], -1.0 / CF_W, o, ALU.mult, ALU.add)
                op.then_inc(dve_step, 1)
                dve.wait_ge(dve_step, after(dve, dve_step))
                dve.tensor_tensor(LN_SQ, t, t, ALU.mult).then_inc(head_in, 1)
                dve.wait_ge(head_in, after(dve, head_in))

            def variance():
                dve.wait_ge(head_sums, after(dve, head_sums))
                dve.tensor_scalar(LN_STD, bank[4][:, 0:S], 1.0 / CF_W, EPS, ALU.mult, ALU.add).then_inc(head_taken, 1)
                dve.wait_ge(head_taken, after(dve, head_taken))

            def divide():
                dve.wait_ge(root_ready, after(dve, root_ready))
                dve.reciprocal(LN_STD, LN_STD).then_inc(dve_step, 1)
                dve.wait_ge(dve_step, after(dve, dve_step))
                v = t.rearrange("p (c t) -> p c t", t=S)
                return dve.tensor_tensor(v, v, LN_STD.unsqueeze(1).to_broadcast([P, 2, S]), ALU.mult)
            return centre, variance, divide

        def act_root(act, t):
            act.wait_ge(head_taken, after(act, head_taken))
            act.activation(t, t, ACT.Sqrt).then_inc(root_ready, 1)

        UNITS = [(h, qt) for h in range(DA_H) for qt in range(TT)]

        def pe_diff(pe, s):
            parts = keys_of(s)
            nkt = TT * len(parts)

            def scores(u):
                h, qt = UNITS[u]
                if u:
                    pe.wait_ge(da_exp, after(pe, da_exp))
                for m in range(2):
                    r = slice(DA_D * m, DA_D * m + DA_D)
                    for k, (keys, _) in enumerate(parts):
                        mm = pe.matmul(bank[4 + m][:, k * S:(k + 1) * S], DQ[r, h * S + qt * P:h * S + (qt + 1) * P],
                                       keys[r, h * S:(h + 1) * S], start=True, stop=True)
                mm.then_inc(da_scores, 1)

            def turn(u):
                pe.wait_ge(da_mix, after(pe, da_mix))
                for kt in range(nkt):
                    mm = pe.transpose(bank[6][:, kt * P:(kt + 1) * P], DP[u % 2][0][:, kt * P:(kt + 1) * P], const("ident"))
                mm.then_inc(da_turned, 1)

            def output(u):
                h, qt = UNITS[u]
                pe.wait_ge(da_copied, after(pe, da_copied))
                if u:
                    pe.wait_ge(da_stored, after(pe, da_stored))
                for kt in range(nkt):
                    v = parts[kt // TT][1]
                    o = (kt % TT) * DA_W + h * P
                    mm = pe.matmul(bank[7][:, 0:P], v[:, o:o + P], DAT[u % 2][:, kt * P:(kt + 1) * P],
                                   start=kt == 0, stop=kt == nkt - 1)
                mm.then_inc(da_out, 1)
            return scores, turn, output

        def act_diff(act, s):
            nk = S * len(keys_of(s))

            def powers(u):
                b = u % 2
                act.wait_ge(da_max, after(act, da_max))
                for m in range(2):
                    op = act.activation(DP[b][m][:, 0:nk], bank[4 + m][:, 0:nk], ACT.Exp, scale=DA_D ** -0.5,
                                        bias=da_top[:, 4 * b + m:4 * b + m + 1],
                                        accum_out=da_top[:, 4 * b + 2 + m:4 * b + 3 + m])
                op.then_inc(da_exp, 1)

            def copied(u):
                act.wait_ge(da_turned, after(act, da_turned))
                if u >= 2:
                    act.wait_ge(da_out, after(act, da_out))
                act.activation(DAT[u % 2][:, 0:nk], bank[6][:, 0:nk], ACT.Copy).then_inc(da_copied, 1)
            return powers, copied

        def dve_diff(dve, s):
            nk = S * len(keys_of(s))

            def maxima(u):
                b = u % 2
                dve.wait_ge(da_scores, after(dve, da_scores))
                t = da_top[:, 4 * b:4 * b + 2]
                for m in range(2):
                    op = dve.tensor_reduce(t[:, m:m + 1], bank[4 + m][:, 0:nk], AX_X, ALU.max)
                op.then_inc(dve_step, 1)
                dve.wait_ge(dve_step, after(dve, dve_step))
                dve.tensor_scalar(t, t, -(DA_D ** -0.5), None, ALU.mult).then_inc(da_max, 1)
                dve.wait_ge(da_max, after(dve, da_max))

            def mix(u):
                b = u % 2
                dve.wait_ge(da_exp, after(dve, da_exp))
                t = da_top[:, 4 * b + 2:4 * b + 4]
                dve.reciprocal(t, t).then_inc(dve_step, 1)
                dve.wait_ge(dve_step, after(dve, dve_step))
                dve.tensor_scalar(t[:, 1:2], t[:, 1:2], LAM[:, 5:6], None, ALU.mult).then_inc(dve_step, 1)
                p0, p1 = (x[:, 0:nk] for x in DP[b])
                dve.tensor_scalar(p0, p0, t[:, 0:1], None, ALU.mult).then_inc(dve_step, 1)
                dve.wait_ge(dve_step, after(dve, dve_step, 2))
                dve.scalar_tensor_tensor(p0, p1, t[:, 1:2], p0, ALU.mult, ALU.add).then_inc(da_mix, 1)
                dve.wait_ge(da_mix, after(dve, da_mix))

            def store(u):
                h, qt = UNITS[u]
                dve.wait_ge(da_out, after(dve, da_out))
                dve.tensor_copy(DO[:, h * S + qt * P:h * S + (qt + 1) * P], bank[7][:, 0:P]).then_inc(da_stored, 1)
                dve.wait_ge(da_stored, after(dve, da_stored))
            return maxima, mix, store

        def branch_parts(b):
            c0, width = BRANCH[b]
            return tuple(t[:, c0 * S:c0 * S + width // P * S] for t in (BRH, BRL))

        NU = len(UNITS)

        def pe_mix(pe, l, s):
            pre = f"mix{l}{s}"
            pe_norm(pe, W[8])
            pe_panels(pe, f"{pre}.k")
            if (l, s) not in FULL:
                pe_panels(pe, f"{pre}.v", fills=0)
                return
            pe_panels(pe, f"{pre}.q", fills=0)
            pe_panels(pe, f"{pre}.v", fills=0)
            if s == "x":
                pe_heads(pe, const("rot_axial"), DQ, chunks=4)
                pe_heads(pe, const("rot_axial"), DK, chunks=4, first=6)
            pe_panels(pe, f"{pre}.ab", fills=0)
            pe_panels(pe, f"{pre}.d", fills=0)

            def turn_weights():
                pe.wait_ge(sgu_landed, after(pe, sgu_landed, 16 * (1 + SG_G)))
                for g in range(SG_G):
                    mm = pe.transpose(bank[5][:, g * P:(g + 1) * P], SGW[:, g * P:(g + 1) * P], const("ident"))
                mm.then_inc(sgu_turned, 1)

            def turn_v():
                pe.wait_ge(head_in, after(pe, head_in))
                for tt in range(TT):
                    for c in range(2):
                        mm = pe.transpose(bank[6][:, tt * S + c * P:tt * S + (c + 1) * P],
                                          AB[:, (8 + c) * S + tt * P:(8 + c) * S + (tt + 1) * P], const("ident"))
                mm.then_inc(sgu_turned, 1)

            def mix_tokens():
                pe.wait_ge(sgu_copied, after(pe, sgu_copied, 2))
                for g in range(SG_G):
                    for tt in range(TT):
                        mm = pe.matmul(bank[4 + 3 * (g // 2)][DH * (g % 2):DH * (g % 2) + DH, tt * P:(tt + 1) * P],
                                       V_TOK[:, tt * SG_W + g * DH:tt * SG_W + (g + 1) * DH], SGWT[:, g * P:(g + 1) * P],
                                       start=True, stop=True)
                mm.then_inc(sgu_out, 1)

            between = {0: lambda: pe_total(pe, AB[:, 8 * S:10 * S]),
                       1: lambda: pe_total(pe, LN_SQ),
                       3: turn_weights, 4: turn_v, 6: mix_tokens}
            tile = pe_panels(pe, f"{pre}.aout", by_hand=True)
            for st in range(C):
                tile(st)
                if st in between:
                    between[st]()
            tile = pe_panels(pe, f"{pre}.bout", by_hand=True)
            scores, turn, output = pe_diff(pe, s)
            scores(0)
            for u in range(NU):
                tile(u)
                if u:
                    output(u - 1)
                turn(u)
                if u + 1 < NU:
                    scores(u + 1)
            pe.wait_ge(da_exp, after(pe, da_exp))
            pe_total(pe, D_)
            output(NU - 1)
            pe_total(pe, LN_SQ)
            pe_heads(pe, ones[:, :], W[6], chunks=4, first=5)
            pe.wait_ge(da_stored, after(pe, da_stored))
            pe_panels(pe, f"{pre}.dout")
            pe_panels(pe, f"{pre}.cout")
            pe_panels(pe, f"{pre}.o")

        def act_mix(act, l, s):
            pre = f"mix{l}{s}"
            act_norm(act, STREAM[s], W[8])
            act_panels(act, f"{pre}.k")
            if (l, s) not in FULL:
                act_panels(act, f"{pre}.v")
                return
            for n in ("q", "v", "ab"):
                act_panels(act, f"{pre}.{n}")
            act.wait_ge(bank_free, tiles_of(f"{pre}.ab"))
            t = AB[:, 6 * S:10 * S]
            act.activation(t, t, ACT.Gelu_apprx_tanh).then_inc(glu_ready, 1)
            act_panels(act, f"{pre}.d")
            act.wait_ge(bank_free, tiles_of(f"{pre}.d"))
            t = D_[:, 2 * S:4 * S]
            act.activation(t, t, ACT.Sigmoid).then_inc(glu_ready, 1)

            def gated(b, by_hand=False):
                g = G[f"{pre}.{b}out"]

                def gate(st, j, k):
                    if k == 1:
                        n = after(act, merged_step)
                        if n is not None:
                            act.wait_ge(merged_step, n)
                        act.activation(silu[j % 2][:, :], bank[(g.t0 + j * g.tiles + 1) % RING][:, 0:S],
                                       ACT.Sigmoid).then_inc(silu_ready, 1)
                gate.per = {merged_step: 2}
                return act_panels(act, g.name, gate, by_hand=by_hand)

            def copy_weights():
                act.wait_ge(sgu_turned, after(act, sgu_turned))
                act.activation(SGWT, bank[5][:, :], ACT.Copy).then_inc(sgu_copied, 1)

            def copy_v():
                act.wait_ge(sgu_turned, after(act, sgu_turned))
                act.activation(V_TOK, bank[6][:, :], ACT.Copy).then_inc(sgu_copied, 1)

            between = {1: lambda: act_root(act, LN_STD), 3: copy_weights, 4: copy_v}
            tile = gated("a", by_hand=True)
            for st in range(C):
                tile(st)
                if st in between:
                    between[st]()
            tile = gated("b", by_hand=True)
            powers, copied = act_diff(act, s)
            powers(0)
            for u in range(NU):
                tile(u)
                copied(u)
                if u + 1 < NU:
                    powers(u + 1)
            act_root(act, LN_STD)
            act.wait_ge(da_out, after(act, da_out, 2))
            act_root(act, W[6][:, 0:4 * S])
            act.wait_ge(conf_ready, after(act, conf_ready))
            for c in range(2):
                o = D_[:, c * S:(c + 1) * S]
                op = act.activation(o, o, ACT.Silu, scale=v2vec("conf_ln_g_2", l, c), bias=v2vec("conf_ln_b_2", l, c))
            op.then_inc(conf_act, 1)
            gated("d")
            gated("c")
            act_panels(act, f"{pre}.o")

        def dve_rope(dve, t, first):
            def over(name, k):
                return const(name).unsqueeze(1).to_broadcast([P, k, S])

            rot = W[6][:, 0:4 * S]

            def times_sin(c, ps):
                return dve.tensor_tensor(rot[:, c].rearrange("p (c t) -> p c t", t=S),
                                         ps.rearrange("p (c t) -> p c t", t=S), over("sin_axial", 2), ALU.mult)
            dve_heads(dve, times_sin, 4, first)
            v = t.rearrange("p (c t) -> p c t", t=S)
            dve.tensor_tensor(v, v, over("cos_axial", 4), ALU.mult).then_inc(dve_step, 1)
            dve.wait_ge(dve_step, after(dve, dve_step))
            dve.tensor_tensor(t, t, rot, ALU.add).then_inc(dve_step, 1)
            dve.wait_ge(dve_step, after(dve, dve_step))

        def dve_mix(dve, l, s):
            pre = f"mix{l}{s}"
            k_dst, v_dst = (KC, VC) if s == "c" else (DK, DV)
            dve_norm(dve, STREAM[s], gain(s, 1), W[7], mod(s, 3))
            full = (l, s) in FULL
            if full:
                dve.memset(LAM[:, 6:7], 0.0).then_inc(sgu_free, 1)
                dve.wait_ge(sgu_free, after(dve, sgu_free))
            dve_tiles(dve, f"{pre}.k", take_copy(dve, k_dst))
            if full:
                dve_tiles(dve, f"{pre}.q", take_copy(dve, DQ))
                if s == "x":
                    for _ in range(2):
                        dve.memset(da_top[:, 0:1], 0.0).then_inc(head_in, 1)
                        dve.wait_ge(head_in, after(dve, head_in))
            dve_tiles(dve, f"{pre}.v", take_tokens(dve, v_dst.rearrange("p (a m) -> p a m", m=DA_W)))
            if not full:
                return
            if s == "x":
                dve_rope(dve, DQ, 4)
                dve_rope(dve, DK, 6)
            dve_tiles(dve, f"{pre}.ab", take_copy(dve, AB))
            bg, cg, xin = (AB[:, 2 * k * S:2 * (k + 1) * S] for k in range(3))
            y = T2[:, 0:2 * S]
            dve.tensor_tensor(xin, cg, xin, ALU.mult).then_inc(dve_step, 1)
            dve.wait_ge(dve_step, after(dve, dve_step))
            taps = [[v2vec("conv_a_w_2", CA_K * l + k, c) for k in range(CA_K)] for c in range(2)]
            ins = [xin[:, c * S:(c + 1) * S] for c in range(2)]
            outs = [y[:, c * S:(c + 1) * S] for c in range(2)]
            for i, o, w in zip(ins, outs, taps):
                op = dve.tensor_scalar(o, i, w[1], None, ALU.mult)
            op.then_inc(dve_step, 1)
            dve.wait_ge(dve_step, after(dve, dve_step))
            for i, o, w in zip(ins, outs, taps):
                op = dve.scalar_tensor_tensor(o[:, 1:S], i[:, 0:S - 1], w[0], o[:, 1:S], ALU.mult, ALU.add)
            op.then_inc(dve_step, 1)
            dve.wait_ge(dve_step, after(dve, dve_step))
            for i, o, w in zip(ins, outs, taps):
                op = dve.scalar_tensor_tensor(o[:, 0:S - 1], i[:, 1:S], w[2], o[:, 0:S - 1], ALU.mult, ALU.add)
            op.then_inc(dve_step, 1)
            dve.wait_ge(dve_step, after(dve, dve_step))
            dve.tensor_tensor(y, y, bg, ALU.mult).then_inc(dve_step, 1)
            dve.wait_ge(dve_step, after(dve, dve_step))
            split(dve, y, branch_parts("a"))
            dve_tiles(dve, f"{pre}.d", take_copy(dve, D_))

            def merged(b, by_hand=False):
                def take(st, j, banks):
                    dve.wait_ge(silu_ready, after(dve, silu_ready))
                    o = MERGED[:, st * S:(st + 1) * S] if isinstance(st, int) else MERGED[:, bass.ds(st * S, S)]
                    if b == MERGE_ORDER[0]:
                        dve.tensor_tensor(o, silu[j % 2][:, :], banks[0][:, 0:S], ALU.mult).then_inc(bank_free, 2)
                        dve.wait_ge(bank_free, after(dve, bank_free, 2))
                        dve.memset(hid[:, 0:2], 0.0).then_inc(merged_step, 1)
                        dve.wait_ge(merged_step, after(dve, merged_step))
                    else:
                        dve.tensor_tensor(hid[:, :], silu[j % 2][:, :], banks[0][:, 0:S], ALU.mult).then_inc(bank_free, 2)
                        dve.wait_ge(bank_free, after(dve, bank_free, 2))
                        dve.tensor_tensor(o, o, hid[:, :], ALU.add).then_inc(merged_step, 1)
                        dve.wait_ge(merged_step, after(dve, merged_step))
                name = f"{pre}.{b}out"
                counts.start(dve, bank_free, G[name].t0)
                return dve_tiles(dve, name, take, {silu_ready: 1, bank_free: 2, merged_step: 1}, by_hand)

            dve.wait_ge(glu_ready, after(dve, glu_ready))
            u_, v_ = AB[:, 6 * S:8 * S], AB[:, 8 * S:10 * S]
            dve.memset(da_top[:, 0:1], 0.0).then_inc(head_in, 1)
            dve.wait_ge(head_in, after(dve, head_in))
            centre, variance, divide = dve_layer_norm(dve, v_)

            def normed():
                divide().then_inc(head_in, 1)
                dve.wait_ge(head_in, after(dve, head_in))

            def gated_unit():
                dve.wait_ge(sgu_out, after(dve, sgu_out))
                for k in range(2):
                    op = dve.tensor_tensor(
                        y[:, k * S:(k + 1) * S].rearrange("p (n t) -> p n t", t=P),
                        bank[4 + 3 * k][:, 0:S].rearrange("p (n t) -> p n t", t=P),
                        SGB[:, k * P:(k + 1) * P].unsqueeze(1).to_broadcast([P, TT, P]), ALU.add)
                op.then_inc(dve_step, 1)
                dve.wait_ge(dve_step, after(dve, dve_step))
                dve.tensor_tensor(y, y, u_, ALU.mult).then_inc(dve_step, 1)
                dve.wait_ge(dve_step, after(dve, dve_step))
                split(dve, y, branch_parts("b"))

            between = {0: centre, 1: variance, 2: normed, 6: gated_unit}
            tile = merged("a", by_hand=True)
            for st in range(C):
                tile(st)
                if st in between:
                    between[st]()
            dve.wait_ge(glu_ready, after(dve, glu_ready))
            pad = PAD.rearrange("p (c t) -> p c t", t=PADW)
            edge = CF_K // 2
            dve.memset(pad[:, :, 0:edge], 0.0)
            dve.memset(pad[:, :, edge + S:PADW], 0.0)
            z = D_.rearrange("p (c t) -> p c t", t=S)
            acc = D_[:, 0:2 * S]
            per_unit = -(-CF_K // NU)

            def taps_of(u):
                for k in range(u * per_unit, min(CF_K, (u + 1) * per_unit)):
                    for c in range(2):
                        i, o, w = pad[:, c, k:k + S], acc[:, c * S:(c + 1) * S], v2vec("conf_dw_2", CF_K * l + k, c)
                        if k == 0:
                            op = dve.tensor_scalar(o, i, w, v2vec("conf_db_2", l, c), ALU.mult, ALU.add)
                        else:
                            op = dve.scalar_tensor_tensor(o, i, w, o, ALU.mult, ALU.add)
                    if k < CF_K - 1:
                        op.then_inc(dve_step, 1)
                        dve.wait_ge(dve_step, after(dve, dve_step))
                    else:
                        op.then_inc(head_in, 1)
                        dve.wait_ge(head_in, after(dve, head_in))

            maxima, mix, store = dve_diff(dve, s)
            tile = merged("b", by_hand=True)
            maxima(0)
            dve.tensor_tensor(pad[:, :, edge:edge + S], z[:, 0:2], z[:, 2:4], ALU.mult).then_inc(dve_step, 1)
            dve.wait_ge(dve_step, after(dve, dve_step))
            for u in range(NU):
                mix(u)
                tile(u)
                if u:
                    store(u - 1)
                if u + 1 < NU:
                    maxima(u + 1)
                taps_of(u)
            centre, variance, divide = dve_layer_norm(dve, acc)
            centre()
            store(NU - 1)
            t = W[6][:, 0:4 * S]
            dve.tensor_tensor(t, DO, DO, ALU.mult).then_inc(head_in, 1)
            dve.wait_ge(head_in, after(dve, head_in))
            variance()
            dve_heads(dve, lambda c, ps: dve.tensor_scalar(t[:, c], ps, 1.0 / P, EPS, ALU.mult, ALU.add), 4, 5).then_inc(head_taken, 1)
            dve.wait_ge(head_taken, after(dve, head_taken))
            divide().then_inc(conf_ready, 1)
            dve.wait_ge(conf_ready, after(dve, conf_ready))
            dve.wait_ge(conf_act, after(dve, conf_act))
            split(dve, acc, branch_parts("d"))
            dve.wait_ge(root_ready, after(dve, root_ready))
            dve.reciprocal(t, t).then_inc(dve_step, 1)
            dve.wait_ge(dve_step, after(dve, dve_step))
            dve.tensor_scalar(t, t, 1.0 - lam_init[l], None, ALU.mult).then_inc(dve_step, 1)
            dve.wait_ge(dve_step, after(dve, dve_step))
            dve.scalar_tensor_tensor(DO, DO, VEC3[:, 10 + l:11 + l], t, ALU.mult, ALU.mult).then_inc(dve_step, 1)
            dve.wait_ge(dve_step, after(dve, dve_step))
            split(dve, DO, branch_parts("c"))
            merged("d")
            merged("c")
            split(dve, MERGED)
            dve_tiles(dve, f"{pre}.o", take_residual(dve, STREAM[s], mod_gate(s, 5)))

        CROWS = W[6]

        def sp_ctx(sp):
            sp.dma_start(CROWS[:, :].rearrange("p (a d) -> p a d", d=D),
                                       a["ctx_2"][0].rearrange("(a p) d -> p a d", p=P)).then_inc(ctx_landed, 16)

        def act_second(act):
            act_ada(act)
            act_ffn(act, "f10x", X)
            act.wait_ge(x_ready, after(act, x_ready, 4))
            act_ffn(act, "f10c", CTX)
            act.wait_ge(bank_free, tiles_of("f10c.down"))
            act_mix(act, 0, "c")
            act.wait_ge(bank_free, tiles_of("mix0c.o"))
            act_ffn(act, "f20c", CTX)
            act.wait_ge(bank_free, tiles_of("f20c.down"))
            act_mix(act, 0, "x")
            act.wait_ge(bank_free, tiles_of("mix0x.o"))
            act_ffn(act, "f20x", X)
            act_ada(act)
            act_ffn(act, "f11x", X)
            act.wait_ge(bank_free, tiles_of("f11x.down"))
            act_ffn(act, "f11c", CTX)
            act.wait_ge(bank_free, tiles_of("f11c.down"))
            act_mix(act, 1, "c")
            act_mix(act, 1, "x")
            act.wait_ge(bank_free, tiles_of("mix1x.o"))
            act_ffn(act, "f21x", X)
            act.wait_ge(bank_free, tiles_of("f21x.down"))
            act_norm(act, X, W[8])

        def pe_second(pe):
            pe.wait_ge(bank_free, tiles_of("ffn3.down"))
            pe.wait_ge(ctx_landed, after(pe, ctx_landed, 16))
            pe_turn_in(pe, CROWS)
            pe.wait_ge(x_ready, after(pe, x_ready, 4))
            pe_ada(pe)
            pe_ffn(pe, "f10x")
            pe_ffn(pe, "f10c")
            pe_mix(pe, 0, "c")
            pe_ffn(pe, "f20c")
            pe_mix(pe, 0, "x")
            pe_ffn(pe, "f20x")
            pe_ada(pe)
            pe_ffn(pe, "f11x")
            pe_ffn(pe, "f11c")
            pe_mix(pe, 1, "c")
            pe_mix(pe, 1, "x")
            pe_ffn(pe, "f21x")
            pe_norm(pe, W[8])
            pe.wait_ge(bank_free, tiles_of("f21x.down"))
            pe_turn_out(pe, W[7])

        def dve_second(dve):
            dve_turn_in(dve, CTX)
            dve_ada(dve, 0)
            dve_ffn2(dve, "f10x", "x", 0)
            dve_ffn2(dve, "f10c", "c", 0)
            dve_mix(dve, 0, "c")
            dve_ffn2(dve, "f20c", "c", 2)
            dve_mix(dve, 0, "x")
            dve_ffn2(dve, "f20x", "x", 2)
            dve_ada(dve, 1)
            dve_ffn2(dve, "f11x", "x", 0)
            dve_ffn2(dve, "f11c", "c", 0)
            dve_mix(dve, 1, "c")
            dve_mix(dve, 1, "x")
            dve_ffn2(dve, "f21x", "x", 2)
            dve_norm(dve, X, lambda c: vec("final_g_2", 0, c), W[7], to_operand=False)
            dve.memset(eps[:, 1:2], 0.0).then_inc(turn_in, 1)
            dve.wait_ge(turn_in, after(dve, turn_in))
            dve_turn_out(dve)

        block = ctx.enter_context(nc.Block())
        FIRST = [f"rw{0}", "sb", "ds", f"rw{3}"]

        @block.sync
        def _(sp):
            sp_setup(sp)
            sp_lora(sp, 0)
            for g in order:
                if g.name == "ds.q":
                    sp_ds_small(sp)
                if g.name == "rw3.r":
                    sp_lora(sp, 1)
                if g.name == "f10x.up":
                    sp_ctx(sp)
                if g.name.endswith(".q") and g.name[:5] in [f"mix{l}{s}" for l, s in FULL]:
                    sp_gated_unit(sp, int(g.name[3]))
                if g.direct:
                    sp_direct(sp, g.name)
                else:
                    sp_panels(sp, g.name)
            sp_out(sp)

        @block.gpsimd
        def _(pool):
            for g in order:
                if not g.direct:
                    pool_panels(pool, g.name)

        @block.scalar
        def _(act):
            for q in range(RING):
                act_round(act, order[0], q)
            act_input(act)
            act_cond(act)
            act_rwkv(act, 0)
            act.wait_ge(bank_free, tiles_of("rw0.out"))
            act_ffn(act, "ffn0", X)
            act.wait_ge(bank_free, tiles_of("ffn0.down"))
            act_sb(act)
            act.wait_ge(bank_free, tiles_of("sb.out"))
            act_ffn(act, "ffn1", X)
            act.wait_ge(bank_free, tiles_of("ffn1.down"))
            act_ds(act)
            act.wait_ge(bank_free, tiles_of("ds.out"))
            act_ffn(act, "ffn2", X)
            act.wait_ge(bank_free, tiles_of("ffn2.down"))
            act_rwkv(act, 3)
            act.wait_ge(bank_free, tiles_of("rw3.out"))
            act_ffn(act, "ffn3", X)
            act_second(act)

        @block.tensor
        def _(pe):
            pe_setup(pe)
            pe_rwkv(pe, 0)
            pe_ffn(pe, "ffn0")
            pe_sb(pe)
            pe_ffn(pe, "ffn1")
            pe_ds(pe)
            pe_ffn(pe, "ffn2")
            pe_rwkv(pe, 3)
            pe_ffn(pe, "ffn3")
            pe_second(pe)

        @block.vector
        def _(dve):
            dve_setup(dve)
            dve_rwkv(dve, 0)
            dve_ffn(dve, "ffn0", X, lambda c: vec("norm_ffn", 0, c))
            dve_sb(dve, 1)
            dve_ffn(dve, "ffn1", X, lambda c: vec("norm_ffn", 1, c))
            dve_ds(dve, 2)
            dve_ffn(dve, "ffn2", X, lambda c: vec("norm_ffn", 2, c))
            dve_rwkv(dve, 3)
            dve_ffn(dve, "ffn3", X, lambda c: vec("norm_ffn", 3, c))
            dve_second(dve)


def kernel(**inputs):
    import concourse.bacc as bacc
    from concourse.bass_utils import run_bass_kernel_spmd

    nc = bacc.Bacc("TRN2", target_bir_lowering=False, num_devices=1)
    table, at = constants()
    arrays, views = {}, {}
    for name, value in [*inputs.items(), ("const", table)]:
        array = np.ascontiguousarray(value)
        arrays[f"in_{name}"] = array
        views[name] = nc.dram_tensor(f"in_{name}", array.shape, F32, kind="ExternalInput").ap()
    out = nc.dram_tensor("out", (1, S, D), F32, kind="ExternalOutput").ap()
    build(nc, views, out, at)
    return run_bass_kernel_spmd(nc, [arrays], core_ids=[0]).results[0]["out"]
```

```python
from contextlib import ExitStack, contextmanager

import numpy as np

import concourse.bass as bass
import concourse.mybir as mybir

F32 = mybir.dt.float32
F32R = mybir.dt.float32r
ACT = mybir.ActivationFunctionType
ALU = mybir.AluOpType
AX_X = mybir.AxisListType.X

P = 128
S = 256
TT = S // P
D = 1024
C = D // P
H = 16
DH = 64
DEPTH = 4
F = 2816
FC = F // P
CHUNK = 64
NCH = S // CHUNK
L_W, L_A, L_G, L_V = 64, 64, 160, 32
IDX_H = 8
TOPK = S // 4
EPS = 1e-6
GN_EPS = DH * 1e-5
DECAY = float(np.exp(np.float64(-0.5)))
NEG = -3.0e38
TAKEN = -3.2e38
HIDE = -1.0e30

RING = 4
KPAN = 8

D2 = 2
N_MOD = 9
CA_W, CA_K = 256, 3
SG_W, SG_G = 256, 4
DA_H, DA_D = 4, 64
DA_W = DA_H * 2 * DA_D
CF_W, CF_K = 256, 31
N_BR = 4
A_OFF = 0
B_OFF = A_OFF + 3 * CA_W
Q_OFF = B_OFF + 2 * SG_W
K_OFF = Q_OFF + DA_W
V_OFF = K_OFF + DA_W
D_OFF = V_OFF + DA_W
G_OFF = D_OFF + 2 * CF_W


def name_of(eng):
    return str(eng.engine).split(".")[-1]


class Counts:

    def __init__(self):
        self.seen = {}
        self.turns = {}

    def at(self, eng, sem):
        return self.seen.get((sem, name_of(eng)), 0)

    def start(self, eng, sem, value):
        self.seen[sem, name_of(eng)] = value

    def after(self, eng, sem, n=1):
        have = self.at(eng, sem) + n
        self.start(eng, sem, have)
        if (sem, name_of(eng)) in self.turns:
            i, per = self.turns[sem, name_of(eng)]
            assert have > 0
            return i * per + have
        return have if have > 0 else None

    @contextmanager
    def repeat(self, eng, n, per):
        with eng.Fori(0, n) as i:
            at = {sem: self.at(eng, sem) for sem in per}
            for sem, k in per.items():
                self.turns[sem, name_of(eng)] = (i, k)
            yield i
        for sem, k in per.items():
            assert self.at(eng, sem) == at[sem] + k
            self.start(eng, sem, at[sem] + n * k)
            del self.turns[sem, name_of(eng)]


class Projection:

    def __init__(self, name, steps, panels, tokens_out=False, direct=False):
        self.name, self.steps, self.panels = name, steps, panels
        self.tokens_out = tokens_out
        self.width = S if tokens_out else P
        self.direct = direct
        self.pps = len(panels)
        self.tiles = TT if tokens_out else 1 + max(p[4] for p in panels)
        self.body = RING // self.tiles
        self.n_panels = steps * self.pps
        self.n_tiles = 0 if direct else steps * self.tiles


def dense(name, w, col, n_out, operand, kc=C, tokens_out=False):
    deep, width = (KPAN * P // S, S) if tokens_out else (KPAN, P)
    groups = [(k0, min(deep, kc - k0)) for k0 in range(0, kc, deep)]
    return Projection(name, n_out // width, [(w, col, k0, nk, 0, operand) for k0, nk in groups], tokens_out)


def pair(name, w_a, col_a, kc_a, w_b, col_b, kc_b, n_out, operand_a, operand_b):
    return Projection(name, n_out // P, [(w_a, col_a, 0, kc_a, 0, operand_a), (w_b, col_b, 0, kc_b, 1, operand_b)])


def constants():
    p = np.arange(P)[:, None]
    f = np.arange(P)[None, :]
    t = np.arange(S)[None, :]
    parts = {}
    parts["ident"] = p == f
    parts["headones"] = p // DH == f // DH
    half = DH // 2
    rot = np.zeros((P, P))
    for m in range(P):
        if m % DH < half:
            rot[m + half, m] = -1.0
        else:
            rot[m - half, m] = 1.0
    parts["rot_head"] = rot
    nf = DA_D // 4
    rot = np.zeros((P, P))
    for m in range(P):
        if m % (2 * nf) < nf:
            rot[m + nf, m] = -1.0
        else:
            rot[m - nf, m] = 1.0
    parts["rot_axial"] = rot
    inv = (1.0 / (np.float32(10000.0) ** (np.arange(half, dtype=np.float32) / np.float32(half)))).astype(np.float32)
    ang = (np.arange(S, dtype=np.float32)[None, :] * inv[np.arange(P) % half][:, None]).astype(np.float32)
    parts["cos_head"], parts["sin_head"] = np.cos(ang), np.sin(ang)
    inv = (np.float32(10000.0) ** (-np.arange(nf, dtype=np.float32) / np.float32(nf))).astype(np.float32)
    grid = np.stack([np.arange(S) // 64, np.arange(S) % 64]).astype(np.float32)
    d = np.arange(P) % DA_D
    ang = (grid[d // (2 * nf)] * inv[d % nf][:, None]).astype(np.float32)
    parts["cos_axial"], parts["sin_axial"] = np.cos(ang), np.sin(ang)
    parts["earlier"] = np.concatenate([(st * P + p) < t[:, st * P:] for st in range(TT)], axis=1)
    parts["after"] = p > f
    j, i = np.arange(P)[:, None] % CHUNK, np.arange(CHUNK)[None, :]
    parts["before"] = j < i
    parts["upto"] = j <= i
    parts["below"] = j > i
    for lv in range(6):
        b = 2 ** lv
        parts[f"upper{lv}"] = ((j // b) % 2 == 0) & (i // b == j // b + 1)
        parts[f"lower{lv}"] = ((i // b) % 2 == 0) & (j // b == i // b + 1)
    parts["eye64"] = j == i
    parts["carry"] = np.broadcast_to(t % CHUNK != 0, (P, S))
    at, cols, n = {}, [], 0
    for name, a in parts.items():
        a = np.asarray(a, np.float32)
        at[name] = (n, a.shape[1])
        cols.append(a)
        n += a.shape[1]
    return np.ascontiguousarray(np.concatenate(cols, axis=1)), at


def vector_rows():
    rows, at, n = [], {}, 0
    for name, k in (("norm_mix", DEPTH), ("norm_ffn", DEPTH), ("rw_mix", 12), ("rw_w0", 2), ("rw_a0", 2),
                    ("rw_k_k", 2), ("rw_k_a", 2), ("rw_r_k", 2), ("rw_ln_w", 2), ("rw_ln_b", 2), ("rw_v0", 1),
                    ("norm_g_2", 3 * D2), ("b_ada_2", N_MOD * D2), ("c_2", 1), ("c_ctx_2", 1), ("final_g_2", 1)):
        at[name] = n
        rows.append((name, n, k))
        n += k
    return rows, at, n


def vector_rows_256():
    rows, at, n = [], {}, 0
    for name, k in (("conv_a_w_2", CA_K * D2), ("conf_dw_2", CF_K * D2), ("conf_db_2", D2),
                    ("conf_ln_g_2", D2), ("conf_ln_b_2", D2)):
        at[name] = n
        rows.append((name, n, k))
        n += k
    return rows, at, n


def build(nc, a, out, CONST_AT):
    VEC_ROWS, VAT, NV = vector_rows()
    VEC2_ROWS, V2AT, NV2 = vector_rows_256()
    with ExitStack() as ctx:
        place = [-(-nc.sbuf_base // 64) * 64]

        def sb(name, cols, dt=F32, at=None):
            off = place[0] if at is None else at
            t = nc.alloc_sbuf_tensor_at(name, [P, cols], dt, offset=off)
            if at is None:
                place[0] += -(-cols * 4 // 64) * 64
            return t

        def sem(name):
            return ctx.enter_context(nc.semaphore(name))

        def v3(t, n=S):
            return t[:, :].rearrange("p (c t) -> p c t", t=n)

        SLOT = KPAN * P
        raw = [sb(f"raw{i}", SLOT) for i in range(RING)]
        whi = [sb(f"whi{i}", SLOT, F32R) for i in range(RING)]
        wlo = [sb(f"wlo{i}", SLOT, F32R) for i in range(RING)]
        X = sb("X", C * S)
        CTX = sb("CTX", C * S)
        a_at = place[0]
        AH, AL = sb("AH", C * S, F32R), sb("AL", C * S, F32R)
        cst = sb("cst", sum(n for _, n in CONST_AT.values()))
        VEC = sb("VEC", C * NV)
        VEC2 = sb("VEC2", 2 * NV2)
        VEC3 = sb("VEC3", 12)
        ones = sb("ones", P)
        eps = sb("eps", 2)
        STD = sb("STD", S)
        RSTD = sb("RSTD", S)
        silu = [sb(f"silu{i}", S) for i in range(2)]
        hid = sb("hid", S)
        w_at = []
        W = []
        for i in range(9):
            w_at.append(place[0])
            W.append(sb(f"W{i}", C * S))
        HH = sb("HH", FC * S, F32R, at=w_at[0])
        HL = sb("HL", FC * S, F32R, at=w_at[0] + FC * S * 4)
        VF = sb("VF", C * S)
        l_at = place[0]
        lw1, la1, lg1, lv1 = sb("lw1", C * L_W), sb("la1", C * L_A), sb("lg1", C * L_G), sb("lv1", C * L_V)
        lwa2 = sb("lwa2", D)
        lg2 = sb("lg2", D)
        lgv2 = sb("lgv2", D)
        BRH, BRL = sb("BRH", 10 * S, F32R, at=l_at), sb("BRL", 10 * S, F32R, at=l_at + 10 * S * 4)
        assert place[0] <= nc.sbuf_usable_end, (place[0], nc.sbuf_usable_end)
        bank = [ctx.enter_context(nc.psum_tensor(f"bank{i}", [P, 512], F32)) for i in range(8)]

        def const(name):
            o, n = CONST_AT[name]
            return cst[:, o:o + n]

        VEC_v, VEC2_v = v3(VEC, NV), v3(VEC2, NV2)

        def vec(name, row, c):
            return VEC_v[:, c, VAT[name] + row:VAT[name] + row + 1]

        def vec_b(name, row):
            return VEC_v[:, :, VAT[name] + row:VAT[name] + row + 1].to_broadcast([P, C, S])

        counts = Counts()
        after, repeat = counts.after, counts.repeat

        const_landed = sem("const_landed")
        rows_landed = sem("rows_landed")
        x_rows_landed = sem("x_rows_landed")
        lora_landed = sem("lora_landed")
        raw_landed = [sem(f"raw_landed{i}") for i in range(RING)]
        hi_ready = sem("hi_ready")
        lo_ready = sem("lo_ready")
        panels_done = sem("panels_done")
        bank_free = sem("bank_free")
        operand_ready = sem("operand_ready")
        consts_set = sem("consts_set")
        vec_turned = sem("vec_turned")
        vec_ready = sem("vec_ready")
        x_turned = sem("x_turned")
        x_ready = sem("x_ready")
        squares_ready = sem("squares_ready")
        sums_ready = sem("sums_ready")
        std_ready = sem("std_ready")
        silu_ready = sem("silu_ready")
        hidden_ready = sem("hidden_ready")
        dve_step = sem("dve_step")
        act_step = sem("act_step")
        out_landed = sem("out_landed")
        head_in = sem("head_in")
        head_sums = sem("head_sums")
        head_taken = sem("head_taken")
        root_ready = sem("root_ready")
        lora_in = sem("lora_in")
        lora_mid = sem("lora_mid")
        lora_act = sem("lora_act")
        lora_out = sem("lora_out")
        lora_taken = sem("lora_taken")
        ada_rows = sem("ada_rows")
        ada_turned = sem("ada_turned")
        ada_ready = sem("ada_ready")
        direct_used = sem("direct_used")
        exp_ready = sem("exp_ready")
        decay_ready = sem("decay_ready")
        scan_in = sem("scan_in")
        gram_ready = sem("gram_ready")
        turned_ready = sem("turned_ready")
        turned_taken = sem("turned_taken")
        gram_taken = sem("gram_taken")
        inv_half = sem("inv_half")
        inv_half_taken = sem("inv_half_taken")
        inv_off = sem("inv_off")
        inv_taken = sem("inv_taken")
        rhs_ready = sem("rhs_ready")
        rhs_taken = sem("rhs_taken")
        sol_ready = sem("sol_ready")
        sol_taken = sem("sol_taken")
        chunk_out = sem("chunk_out")
        state_ready = sem("state_ready")
        z_ready = sem("z_ready")
        ds_z_ready = sem("ds_z_ready")
        att_raw = sem("att_raw")
        exps_ready = sem("exps_ready")
        later_in = sem("later_in")
        later_ready = sem("later_ready")
        logit_ready = sem("logit_ready")
        att_ready = sem("att_ready")
        heads_out = sem("heads_out")
        heads_taken = sem("heads_taken")
        idx_ready = sem("idx_ready")
        idx_act = sem("idx_act")
        idx_taken = sem("idx_taken")
        att_turned = sem("att_turned")
        att_turned_taken = sem("att_turned_taken")
        small_landed = sem("small_landed")
        small_ready = sem("small_ready")
        h_ready = sem("h_ready")
        hi_part = sem("hi_part")
        turn_in = sem("turn_in")
        turned_out = sem("turned_out")
        out_ready = sem("out_ready")
        ctx_landed = sem("ctx_landed")
        cond_ready = sem("cond_ready")
        lam_in = sem("lam_in")
        lam_sums = sem("lam_sums")
        lam_exp = sem("lam_exp")
        sgu_free = sem("sgu_free")
        sgu_landed = sem("sgu_landed")
        sgu_turned = sem("sgu_turned")
        sgu_copied = sem("sgu_copied")
        sgu_out = sem("sgu_out")
        glu_ready = sem("glu_ready")
        conf_ready = sem("conf_ready")
        conf_act = sem("conf_act")
        merged_step = sem("merged_step")
        da_scores = sem("da_scores")
        da_max = sem("da_max")
        da_exp = sem("da_exp")
        da_mix = sem("da_mix")
        da_turned = sem("da_turned")
        da_copied = sem("da_copied")
        da_out = sem("da_out")
        da_stored = sem("da_stored")

        counts.start(nc.sync, lo_ready, -RING)
        counts.start(nc.tensor, bank_free, -RING)
        counts.start(nc.scalar, hidden_ready, -2)
        counts.start(nc.scalar, merged_step, -2)

        A = (v3(AH), v3(AL))
        HID = (v3(HH), v3(HL))
        BR = (v3(BRH), v3(BRL))
        G = {}
        order = []

        def plan(g):
            g.p0 = sum(x.n_panels for x in order)
            g.t0 = sum(x.n_tiles for x in order)
            order.append(g)
            G[g.name] = g

        def plan_ffn(name, w_gate, gate_col, w_up, up_col, w_down):
            plan(pair(f"{name}.up", w_gate, gate_col, C, w_up, up_col, C, F, A, A))
            plan(dense(f"{name}.down", w_down, 0, D, HID, kc=FC))

        ADA_N = 512
        ADA_ROWS = D // RING
        ADA_PANELS = N_MOD * D // ADA_N * RING
        for layer in range(DEPTH):
            if layer % 3 == 0:
                for j, n in enumerate("rkv"):
                    plan(dense(f"rw{layer}.{n}", a["rw_w_rkv"][layer // 3, j], 0, D, A))
                plan(Projection(f"ada{layer // 3}", ADA_PANELS, [(a["w_ada_2"][layer // 3], 0, 0, C, 0, None)], direct=True))
                plan(dense(f"rw{layer}.out", a["rw_w_out"][layer // 3], 0, D, A))
            elif layer % 3 == 1:
                for j, n in enumerate("qkv"):
                    plan(dense(f"sb.{n}", a["sb_w_qkv"][0], j * D, D, A, tokens_out=n == "v"))
                plan(dense("sb.out", a["sb_w_out"][0], 0, D, A))
            else:
                plan(dense("ds.q", a["ds_w_in"][0], 0, D, A))
                plan(dense("ds.qi", a["ds_w_in"][0], 3 * D, IDX_H * DH, A))
                plan(dense("ds.k", a["ds_w_in"][0], D, D, A))
                plan(dense("ds.v", a["ds_w_in"][0], 2 * D, D, A, tokens_out=True))
                plan(dense("ds.out", a["ds_w_out"][0], 0, D, A))
            plan_ffn(f"ffn{layer}", a["ffn_w_gu"][layer], 0, a["ffn_w_gu"][layer], F, a["ffn_w_down"][layer])
        BRANCH = {"a": (0, CA_W), "b": (2, SG_W), "c": (4, DA_W), "d": (8, CF_W)}
        MERGE_ORDER = "abdc"
        FULL = [(0, "c"), (0, "x"), (1, "x")]

        def plan_mix(l, s):
            w = a["w_in_2"][l]
            pre = f"mix{l}{s}"
            plan(dense(f"{pre}.k", w, K_OFF, DA_W, A))
            if (l, s) in FULL:
                plan(dense(f"{pre}.q", w, Q_OFF, DA_W, A))
            plan(dense(f"{pre}.v", w, V_OFF, DA_W, A, tokens_out=True))
            if (l, s) not in FULL:
                return
            plan(dense(f"{pre}.ab", w, A_OFF, Q_OFF - A_OFF, A))
            plan(dense(f"{pre}.d", w, D_OFF, 2 * CF_W, A))
            for b in MERGE_ORDER:
                n, (c0, width) = "abcd".index(b), BRANCH[b]
                opnd = tuple(t[:, c0:c0 + width // P] for t in BR)
                plan(pair(f"{pre}.{b}out", a[f"w_{b}_out_2"][l], 0, width // P, w, G_OFF + n * D, C, D, opnd, A))
            plan(dense(f"{pre}.o", a["w_o_2"][l], 0, D, A))

        for l in range(D2):
            for s in "xc":
                plan_ffn(f"f1{l}{s}", a["ffn1_w1_2"][l], 0, a["ffn1_w3_2"][l], 0, a["ffn1_w2_2"][l])
            for s in "cx":
                plan_mix(l, s)
                if (l, s) in FULL:
                    plan_ffn(f"f2{l}{s}", a["ffn2_w1_2"][l], 0, a["ffn2_w3_2"][l], 0, a["ffn2_w2_2"][l])

        NORM_AFTER = {n: (X, True) for n in ("rw0.out", "ffn0.down", "sb.out", "ffn1.down", "ds.out", "ffn2.down", "rw3.out",
                                             "ffn3.down", "mix0x.o", "f20x.down", "mix1x.o", "f21x.down")}
        NORM_AFTER |= {n: (CTX, True) for n in ("f10c.down", "mix0c.o", "f11c.down")}
        NORM_AFTER |= {n: (CTX, False) for n in ("f10x.down", "f11x.down")}
        NORM_AFTER |= {n: (X, False) for n in ("f20c.down", "mix1c.v")}

        def steps_of(eng, g, per, step, peel=False, last_straight=False):
            full = g.steps // g.body
            first = 1 if peel or any(counts.at(eng, x) < 0 for x in per) else 0
            last = full - (1 if last_straight else 0)
            for s in range(first * g.body):
                step(s, s % g.body)
            if last - first > 1:
                with repeat(eng, last - first, per) as i:
                    for j in range(g.body):
                        step((i + first) * g.body + j, j)
                begin = last * g.body
            else:
                begin = first * g.body
            for s in range(begin, g.steps):
                step(s, s % g.body)

        def load_panel(sp, g, s, slot, k=0):
            w, col, k0, nk, _, _ = g.panels[k]
            src = w[k0 * P:(k0 + nk) * P, bass.ds(s * g.width + col, g.width)].rearrange("(c p) m -> p c m", p=P)
            sp.dma_start(raw[slot][:, 0:nk * g.width].rearrange("p (c m) -> p c m", m=g.width), src).then_inc(raw_landed[slot], 16)

        def sp_direct(sp, name):
            g = G[name]

            def load(group, j):
                src = g.panels[0][0][j * ADA_ROWS:(j + 1) * ADA_ROWS, bass.ds(group * ADA_N, ADA_N)]
                sp.dma_start(raw[j][:, :].rearrange("p (c m) -> p c m", m=ADA_N),
                             src.rearrange("(c p) m -> p c m", p=P)).then_inc(raw_landed[j], 16)

            for j in range(RING):
                sp.wait_ge(lo_ready, after(sp, lo_ready))
                load(0, j)
            with repeat(sp, g.steps // RING - 1, {direct_used: RING}) as i:
                for j in range(RING):
                    sp.wait_ge(direct_used, after(sp, direct_used))
                    load(i + 1, j)

        def sp_panels(sp, name):
            g = G[name]
            at = order.index(g)
            behind_direct = at > 0 and order[at - 1].direct

            def step(s, j):
                for k in range(g.pps):
                    slot = (g.p0 + j * g.pps + k) % RING
                    if behind_direct and isinstance(s, int) and s * g.pps + k < RING:
                        sp.wait_ge(direct_used, after(sp, direct_used))
                    else:
                        n = after(sp, lo_ready)
                        if n is not None:
                            sp.wait_ge(lo_ready, n)
                    load_panel(sp, g, s, slot, k)

            steps_of(sp, g, {lo_ready: g.body * g.pps}, step, peel=behind_direct)

        def pool_panels(pool, name):
            g = G[name]

            def step(s, j):
                for k, (_, _, _, nk, _, _) in enumerate(g.panels):
                    slot = (g.p0 + j * g.pps + k) % RING
                    n = nk * g.width
                    pool.wait_ge(hi_ready, after(pool, hi_ready))
                    pool.tensor_tensor(wlo[slot][:, 0:n], raw[slot][:, 0:n], whi[slot][:, 0:n],
                                                   ALU.subtract).then_inc(lo_ready, 1)

            steps_of(pool, g, {hi_ready: g.body * g.pps}, step)

        def act_round(act, g, q):
            slot, n = (g.p0 + q) % RING, g.panels[q % g.pps][3] * g.width
            act.wait_ge(raw_landed[slot], after(act, raw_landed[slot], 16))
            act.activation(whi[slot][:, 0:n], raw[slot][:, 0:n], ACT.Copy).then_inc(hi_ready, 1)

        def act_panels(act, name, work=None, by_hand=False):
            g = G[name]
            x_next, own = NORM_AFTER.get(name, (None, False))
            at = order.index(g)
            following = order[at + 1] if at + 1 < len(order) else None

            def step(s, j):
                for k in range(g.pps):
                    act.wait_ge(panels_done, after(act, panels_done))
                    if work:
                        work(s, j, k)
                    q = j * g.pps + k + RING
                    if isinstance(s, int) and s * g.pps + k + RING >= g.n_panels:
                        if following and not following.direct:
                            act_round(act, following, s * g.pps + k + RING - g.n_panels)
                    else:
                        act_round(act, g, q)
                if x_next is not None and isinstance(s, int):
                    if own and s > squared[0]:
                        act.wait_ge(bank_free, g.t0 + s)
                    act_squares(act, x_next, s if own else min(C, squared[0] + 2))

            if by_hand:
                return lambda s: step(s, s % g.body)
            n = g.body * g.pps
            per = {panels_done: n, **{r: 16 * n // RING for r in raw_landed}}
            if work:
                per |= work.per
            steps_of(act, g, per, step, last_straight=True)

        squared = [0]

        def act_squares(act, x, until):
            for c in range(squared[0], until):
                o = slice(c * S, (c + 1) * S)
                act.activation(W[8][:, o], x[:, o], ACT.Square).then_inc(squares_ready, 1)
            squared[0] = max(squared[0], until)

        def pe_panels(pe, name, fills=1, by_hand=False, chunked=False):
            g = G[name]
            if not chunked:
                pe.wait_ge(operand_ready, after(pe, operand_ready, fills))

            def free_bank():
                n = after(pe, bank_free)
                if n is not None:
                    pe.wait_ge(bank_free, n)

            def tokens_step(s, j):
                for k, (_, _, k0, nk, _, (oh, ol)) in enumerate(g.panels):
                    slot = (g.p0 + j * g.pps + k) % RING
                    pe.wait_ge(lo_ready, after(pe, lo_ready))
                    for tt in range(TT):
                        if k == 0:
                            free_bank()
                        ps = bank[(g.t0 + j * g.tiles + tt) % RING][:, 0:g.width]
                        for c in range(nk):
                            wh, wl = (t[slot][:, c * g.width:(c + 1) * g.width] for t in (whi, wlo))
                            xh, xl = (t[:, k0 + c, tt * P:(tt + 1) * P] for t in (oh, ol))
                            for n, (w, o) in enumerate(((wh, xh), (wl, xh), (wh, xl))):
                                mm = pe.matmul(ps, o, w, start=k == c == n == 0,
                                               stop=k == g.pps - 1 and c == nk - 1 and n == 2)
                    mm.then_inc(panels_done, 1)

            def step(s, j):
                if g.tokens_out:
                    return tokens_step(s, j)
                started = set()
                for k, (_, _, k0, nk, tile, (oh, ol)) in enumerate(g.panels):
                    slot = (g.p0 + j * g.pps + k) % RING
                    ps = bank[(g.t0 + j * g.tiles + tile) % RING]
                    if tile not in started:
                        free_bank()
                    pe.wait_ge(lo_ready, after(pe, lo_ready))
                    last_panel = tile not in [x[4] for x in g.panels[k + 1:]]
                    for c in range(nk):
                        if chunked and isinstance(s, int) and s == k == 0:
                            pe.wait_ge(operand_ready, after(pe, operand_ready))
                        wh, wl = (t[slot][:, c * P:(c + 1) * P] for t in (whi, wlo))
                        for n, (w, o) in enumerate(((wh, oh), (wh, ol), (wl, oh))):
                            mm = pe.matmul(ps[:, 0:o.shape[2]], w, o[:, k0 + c, :], start=tile not in started and c == n == 0,
                                           stop=last_panel and c == nk - 1 and n == 2)
                    started.add(tile)
                    mm.then_inc(panels_done, 1)

            if by_hand:
                return lambda s: step(s, s % g.body)
            n = g.body * g.pps
            steps_of(pe, g, {bank_free: RING, lo_ready: n}, step, peel=chunked)

        def dve_tiles(dve, name, take, per=None, by_hand=False):
            g = G[name]

            def step(s, j):
                dve.wait_ge(panels_done, after(dve, panels_done, g.pps))
                take(s, j, [bank[(g.t0 + j * g.tiles + t) % RING] for t in range(g.tiles)])

            if by_hand:
                return lambda s: step(s, s % g.body)
            steps_of(dve, g, {panels_done: g.body * g.pps, **{k: v * g.body for k, v in (per or {}).items()}}, step)
            dve.wait_ge(bank_free, tiles_of(name))

        def take_copy(dve, dst, scale=None):
            def take(s, j, banks):
                o = dst[:, bass.ds(s * S, S)]
                if scale is None:
                    dve.tensor_copy(o, banks[0][:, 0:S]).then_inc(bank_free, 1)
                else:
                    dve.tensor_scalar(o, banks[0][:, 0:S], scale, None, ALU.mult).then_inc(bank_free, 1)
            return take

        def take_tokens(dve, dst):
            def take(s, j, banks):
                for tt in range(TT):
                    dve.tensor_copy(dst[:, tt, bass.ds(s * S, S)], banks[tt][:, 0:S]).then_inc(bank_free, 1)
            return take

        def take_residual(dve, x, gate=None):
            def take(s, j, banks):
                o = x[:, bass.ds(s * S, S)]
                if gate is None:
                    dve.tensor_tensor(o, o, banks[0][:, 0:S], ALU.add).then_inc(bank_free, 1)
                else:
                    dve.scalar_tensor_tensor(o, banks[0][:, 0:S], gate[:, bass.ds(s, 1)], o,
                                                          ALU.mult, ALU.add).then_inc(bank_free, 1)
            return take

        def split(dve, src, dst=None):
            hi, lo = dst or (AH, AL)
            n = src.shape[1]
            dve.tensor_copy(hi[:, 0:n], src[:, :]).then_inc(dve_step, 1)
            dve.wait_ge(dve_step, after(dve, dve_step))
            dve.tensor_tensor(lo[:, 0:n], src[:, :], hi[:, 0:n], ALU.subtract).then_inc(operand_ready, 1)
            dve.wait_ge(operand_ready, after(dve, operand_ready))

        def act_norm(act, x, h=None, shift=None):
            act_squares(act, x, C)
            squared[0] = 0
            act.wait_ge(sums_ready, after(act, sums_ready))
            act.activation(STD[:, :], bank[4][:, 0:S], ACT.Sqrt, bias=eps[:, 0:1], scale=1.0 / D).then_inc(std_ready, 1)
            if h is None:
                return
            for c in range(C):
                o, i = AH[:, c * S:(c + 1) * S], h[:, c * S:(c + 1) * S]
                act.wait_ge(h_ready, after(act, h_ready))
                if shift:
                    act.activation(o, i, ACT.Identity, bias=shift(c)).then_inc(hi_part, 1)
                else:
                    act.activation(o, i, ACT.Copy).then_inc(hi_part, 1)

        def pe_norm(pe):
            for c in range(C):
                pe.wait_ge(squares_ready, after(pe, squares_ready))
                mm = pe.matmul(bank[4][:, 0:S], ones[:, :], W[8][:, c * S:(c + 1) * S], start=c == 0, stop=c == C - 1)
            mm.then_inc(sums_ready, 1)

        def dve_norm(dve, x, gain, h, shift=None, to_operand=True):
            dve.wait_ge(std_ready, after(dve, std_ready))
            dve.reciprocal(RSTD[:, :], STD[:, :]).then_inc(dve_step, 1)
            dve.wait_ge(dve_step, after(dve, dve_step))

            def rest(c):
                o = slice(c * S, (c + 1) * S)
                dve.wait_ge(h_ready, after(dve, h_ready))
                dve.wait_ge(hi_part, after(dve, hi_part))
                if shift:
                    op = dve.scalar_tensor_tensor(AL[:, o], h[:, o], shift(c), AH[:, o], ALU.add, ALU.subtract)
                else:
                    op = dve.tensor_tensor(AL[:, o], h[:, o], AH[:, o], ALU.subtract)
                op.then_inc(operand_ready, 1)

            for c in range(C):
                o = slice(c * S, (c + 1) * S)
                op = dve.scalar_tensor_tensor(h[:, o], x[:, o], gain(c), RSTD[:, :], ALU.mult, ALU.mult)
                if to_operand:
                    op.then_inc(h_ready, 1)
                    if c >= 2:
                        rest(c - 2)
            if to_operand:
                rest(C - 2)
                rest(C - 1)
                dve.wait_ge(operand_ready, after(dve, operand_ready, C))
            else:
                op.then_inc(dve_step, 1)
                dve.wait_ge(dve_step, after(dve, dve_step))

        def tiles_of(name):
            return G[name].t0 + G[name].n_tiles

        def act_ffn(act, name, x, shift=None):
            act_norm(act, x, W[7], shift)

            def gate(s, j, k):
                if k == 0:
                    n = after(act, hidden_ready)
                    if n is not None:
                        act.wait_ge(hidden_ready, n)
                    g = G[f"{name}.up"]
                    ps = bank[(g.t0 + j * g.tiles) % RING]
                    act.activation(silu[j % 2][:, :], ps[:, 0:S], ACT.Silu).then_inc(silu_ready, 1)
            gate.per = {hidden_ready: 2}
            act_panels(act, f"{name}.up", gate)
            act_panels(act, f"{name}.down")

        def pe_ffn(pe, name):
            pe_norm(pe)
            pe_panels(pe, f"{name}.up", chunked=True)
            pe.wait_ge(hidden_ready, after(pe, hidden_ready, FC))
            pe_panels(pe, f"{name}.down", fills=0)

        def dve_ffn(dve, name, x, gain, shift=None, out_gate=None):
            dve_norm(dve, x, gain, W[7], shift)

            def take(s, j, banks):
                dve.wait_ge(silu_ready, after(dve, silu_ready))
                o = bass.ds(s * S, S)
                dve.tensor_tensor(hid[:, :], silu[j % 2][:, :], banks[1][:, 0:S], ALU.mult).then_inc(bank_free, 2)
                dve.wait_ge(bank_free, after(dve, bank_free, 2))
                dve.tensor_copy(HH[:, o], hid[:, :]).then_inc(dve_step, 1)
                dve.wait_ge(dve_step, after(dve, dve_step))
                dve.tensor_tensor(HL[:, o], hid[:, :], HH[:, o], ALU.subtract).then_inc(hidden_ready, 1)
                dve.wait_ge(hidden_ready, after(dve, hidden_ready))
            counts.start(dve, bank_free, G[f"{name}.up"].t0)
            dve_tiles(dve, f"{name}.up", take, {silu_ready: 1, bank_free: 2, dve_step: 1, hidden_ready: 1})
            dve_tiles(dve, f"{name}.down", take_residual(dve, x, out_gate))

        def pe_heads(pe, mat, src, chunks=C, first=4):
            pe.wait_ge(head_in, after(pe, head_in))
            for c in range(chunks):
                mm = pe.matmul(bank[first + c // 2][:, (c % 2) * S:(c % 2 + 1) * S], mat, src[:, c * S:(c + 1) * S],
                               start=True, stop=True)
                if c % 2 or c == chunks - 1:
                    mm.then_inc(head_sums, 1)

        def dve_heads(dve, take, chunks=C, first=4):
            for c in range(0, chunks, 2):
                dve.wait_ge(head_sums, after(dve, head_sums))
                n = min(2, chunks - c) * S
                op = take(slice(c * S, c * S + n), bank[first + c // 2][:, 0:n])
            return op

        def act_inverse_root(act, t):
            act.activation(t, t, ACT.Ln).then_inc(act_step, 1)
            act.wait_ge(act_step, after(act, act_step))
            act.activation(t, t, ACT.Exp, scale=-0.5).then_inc(root_ready, 1)

        RW_H, RW_D, RW_XA, RW_XB, RW_R, RW_K, RW_A, RW_CUM, RW_G = W[0], W[1], W[2], CTX, W[3], W[4], W[6], W[7], W[8]
        RW_Q, RW_P, RW_B, RW_C, RW_Y, RW_BONUS = W[3], W[0], W[1], W[4], W[6], W[2]
        lora_wa, lora_g, lora_gv = silu[0], silu[1], hid
        WEND = sb("WEND", C * NCH)
        Q4 = 512
        N_, GBQ, GCP, GCQ = (CTX[:, k * Q4:(k + 1) * Q4] for k in range(4))
        L_, VT, BT, CT = (W[7][:, k * Q4:(k + 1) * Q4] for k in range(4))
        work = [sb(f"scan{k}", Q4, at=a_at + k * Q4 * 4) for k in range(7)]
        IY, IX, IT, LOFF, RHS, SOL, STATE = (t[:, :] for t in work)
        KK_MIN = 1e-24
        HALF = [slice(h * Q4 // 2, (h + 1) * Q4 // 2) for h in range(2)]
        INV_BANKS = [(bank[0], bank[1], bank[2]), (bank[3], bank[4], bank[6])]
        OUT_BANKS, STATE_BANKS = (bank[5], bank[4]), (bank[2], bank[6])
        ADA_BANK = bank[7]
        VISITS = 1 + 5 * 4 + 4
        ADA_FIRST = N_MOD * D // ADA_N - 4 * NCH
        cond = sb("cond", C * 32)
        ada_tok = sb("ada_tok", ADA_N, at=a_at + 7 * Q4 * 4)
        both = [sb(f"both{l}", N_MOD * C * 2) for l in range(D2)]

        def rw_values(layer):
            return VF if layer == 0 else W[5]

        def lora_parts(layer):
            parts = [("w", RW_XB, lw1, L_W), ("a", RW_XB, la1, L_A)]
            if layer:
                parts.append(("v", RW_XA, lv1, L_V))
            return parts + [("g", RW_XB, lg1, L_G)]

        def sp_lora(sp, j):
            for t, w, n in ((lw1, "rw_w1", L_W), (la1, "rw_a1", L_A), (lg1, "rw_g1", L_G)):
                sp.dma_start(t[:, :].rearrange("p (c m) -> p c m", m=n),
                                            a[w][j].rearrange("(c p) m -> p c m", p=P)).then_inc(lora_landed, 16)
            sp.dma_start(lwa2[0:64, :], a["rw_w2"][j]).then_inc(lora_landed, 16)
            sp.dma_start(lwa2[64:128, :], a["rw_a2"][j]).then_inc(lora_landed, 16)
            sp.dma_start(lg2[:, :], a["rw_g2"][j][0:P, :]).then_inc(lora_landed, 16)
            sp.dma_start(lgv2[0:32, :], a["rw_g2"][j][P:L_G, :]).then_inc(lora_landed, 16)
            if j:
                sp.dma_start(lv1[:, :].rearrange("p (c m) -> p c m", m=L_V),
                                            a["rw_v1"][j - 1].rearrange("(c p) m -> p c m", p=P)).then_inc(lora_landed, 16)
                sp.dma_start(lgv2[32:64, :], a["rw_v2"][j - 1]).then_inc(lora_landed, 16)

        def pe_lora(pe, part, first=False):
            name, x, w1, n = part
            pe.wait_ge(lora_in, after(pe, lora_in))
            if not first:
                pe.wait_ge(lora_taken, after(pe, lora_taken, 4))
            base = {"w": 0, "a": 64, "v": 32, "g": 0}[name]
            m = min(n, P)
            w3 = w1[:, :].rearrange("p (c m) -> p c m", m=n)
            for c in range(C):
                mm = pe.matmul(bank[4][base:base + m, 0:S], w3[:, c, 0:m], x[:, c * S:(c + 1) * S],
                               start=c == 0, stop=c == C - 1)
            if n > P:
                for c in range(C):
                    mm = pe.matmul(bank[5][0:n - P, 0:S], w3[:, c, P:n], x[:, c * S:(c + 1) * S],
                                   start=c == 0, stop=c == C - 1)
            mm.then_inc(lora_mid, 1)
            pe.wait_ge(lora_act, after(pe, lora_act))
            for t in range(C):
                if t >= 4:
                    pe.wait_ge(lora_taken, after(pe, lora_taken))
                o, cols = bank[4 + t % 4][:, 0:S], slice(t * P, (t + 1) * P)
                if name == "w":
                    mm = pe.matmul(o, lwa2[0:64, cols], lora_wa[0:64, :], start=True, stop=True)
                elif name == "a":
                    mm = pe.matmul(o, lwa2[64:128, cols], lora_wa[64:128, :], start=True, stop=True)
                elif name == "v":
                    mm = pe.matmul(o, lgv2[32:64, cols], lora_gv[32:64, :], start=True, stop=True)
                else:
                    pe.matmul(o, lg2[:, cols], lora_g[:, :], start=True, stop=False)
                    mm = pe.matmul(o, lgv2[0:32, cols], lora_gv[0:32, :], start=False, stop=True)
                mm.then_inc(lora_out, 1)

        def act_lora(act, part, j):
            name = part[0]
            act.wait_ge(lora_mid, after(act, lora_mid))
            if name == "w":
                op = act.activation(lora_wa[0:64, :], bank[4][0:64, 0:S], ACT.Tanh)
            elif name == "a":
                op = act.activation(lora_wa[64:128, :], bank[4][64:128, 0:S], ACT.Copy)
            elif name == "v":
                op = act.activation(lora_gv[32:64, :], bank[4][32:64, 0:S], ACT.Copy)
            else:
                act.activation(lora_g[:, :], bank[4][:, 0:S], ACT.Sigmoid)
                op = act.activation(lora_gv[0:32, :], bank[5][0:32, 0:S], ACT.Sigmoid)
            op.then_inc(lora_act, 1)
            dst = {"w": RW_CUM, "a": RW_A, "v": RW_XA, "g": RW_G}[name]
            for t in range(C):
                act.wait_ge(lora_out, after(act, lora_out))
                o, i = dst[:, t * S:(t + 1) * S], bank[4 + t % 4][:, 0:S]
                if name == "g":
                    op = act.activation(o, i, ACT.Copy)
                else:
                    b = vec("rw_v0", 0, t) if name == "v" else vec(f"rw_{name}0", j, t)
                    op = act.activation(o, i, ACT.Sigmoid, bias=b)
                op.then_inc(lora_taken, 1)

        def act_rwkv(act, layer):
            j = layer // 3
            parts = lora_parts(layer)
            act_norm(act, X)
            act_panels(act, f"rw{layer}.r")
            act_lora(act, parts[0], j)
            act_panels(act, f"rw{layer}.k")
            act_lora(act, parts[1], j)
            act_panels(act, f"rw{layer}.v")
            for part in parts[2:]:
                act_lora(act, part, j)
            act.wait_ge(head_taken, after(act, head_taken))
            act_inverse_root(act, RW_BONUS[:, :])
            act.wait_ge(decay_ready, after(act, decay_ready))
            act.activation(RW_CUM[:, :], RW_XB[:, :], ACT.Exp, scale=-DECAY).then_inc(exp_ready, 1)
            act.activation(RW_XB[:, :], RW_XB[:, :], ACT.Exp, scale=DECAY).then_inc(exp_ready, 1)
            act_ada_rows(act, bank[0], ADA_FIRST)
            act_ada_place(act, layer // 3, bank[0], 0, ADA_FIRST)
            for ch in range(NCH):
                for k, t in enumerate((VT, BT, CT)):
                    act.wait_ge(turned_ready, after(act, turned_ready))
                    act.activation(t, bank[5 + k % 2][:, :], ACT.Copy).then_inc(turned_taken, 1)
                act.wait_ge(rhs_ready, after(act, rhs_ready))
                act.activation(RHS, bank[3][:, :], ACT.Copy).then_inc(rhs_taken, 1)
                for lv in range(1, 6):
                    for h, banks in zip(HALF, INV_BANKS):
                        act.wait_ge(inv_half, after(act, inv_half))
                        act.activation(IT[:, h], banks[0][:, h], ACT.Copy).then_inc(inv_half_taken, 1)
                act_ada_rows(act, ADA_BANK, 4)
                for h, banks in zip(HALF, INV_BANKS):
                    act.wait_ge(sol_ready, after(act, sol_ready))
                    act.activation(SOL[:, h], banks[0][:, h], ACT.Copy, scale=-1.0).then_inc(sol_taken, 1)
                act_ada_place(act, layer // 3, ADA_BANK, ADA_FIRST + 4 * ch, 4)
            out_panels = G[f"rw{layer}.out"]
            for slot in range(RING):
                counts.start(act, raw_landed[slot], 16 * out_panels.p0 // RING)
                act_round(act, out_panels, slot)
            act.wait_ge(head_taken, after(act, head_taken))
            act_inverse_root(act, RW_Y[:, :])
            act_panels(act, f"rw{layer}.out")

        def pe_ada_panel(pe, group, j, ps, row):
            pe.wait_ge(raw_landed[j], after(pe, raw_landed[j], 16))
            for k in range(ADA_ROWS // P):
                c = j * (ADA_ROWS // P) + k
                mm = pe.matmul(ps[32 * row:32 * row + 32, :], cond[:, 32 * c:32 * c + 32], raw[j][:, k * ADA_N:(k + 1) * ADA_N],
                               start=c == 0, stop=c == C - 1)
            mm.then_inc(direct_used, 1)

        def pe_ada_turn(pe, ps, groups):
            n = 32 * groups
            pe.wait_ge(ada_rows, after(pe, ada_rows))
            for k in range(ADA_N // P):
                mm = pe.transpose(ps[:, k * P:k * P + n], ada_tok[0:n, k * P:(k + 1) * P], const("ident")[0:n, 0:n])
            mm.then_inc(ada_turned, 1)

        def act_ada_rows(act, ps, groups):
            act.wait_ge(direct_used, after(act, direct_used, RING * groups))
            act.activation(ada_tok[0:32 * groups, :], ps[0:32 * groups, :], ACT.Copy).then_inc(ada_rows, 1)

        def act_ada_place(act, l, ps, first, groups):
            act.wait_ge(ada_turned, after(act, ada_turned))
            k = ADA_N // P
            o = both[l][:, first * k * 2:(first + groups) * k * 2].rearrange("p (g k s) -> p g k s", k=k, s=2)
            for g in range(groups):
                op = act.activation(o[:, g], ps[:, :].rearrange("p (k m) -> p k m", k=k)[:, :, 32 * g:32 * g + 2], ACT.Copy)
            op.then_inc(ada_ready, 1)

        def pe_ada_start(pe, layer):
            for slot in range(RING):
                counts.start(pe, raw_landed[slot], 16 * G[f"ada{layer // 3}"].p0 // RING)
            pe.wait_ge(bank_free, tiles_of(f"rw{layer}.v"))
            for group in range(ADA_FIRST):
                for j in range(RING):
                    pe_ada_panel(pe, group, j, bank[0], group)
            pe_ada_turn(pe, bank[0], ADA_FIRST)

        def pe_scan(pe, layer):
            V = rw_values(layer)
            halves = [[(c, slice(DH * hh, DH * hh + DH)) for c in range(C // 2 * h, C // 2 * (h + 1)) for hh in range(2)]
                      for h in range(2)]
            heads = halves[0] + halves[1]
            visits = [0]

            def fill():
                ch, v = visits[0] // VISITS, visits[0] % VISITS
                visits[0] += 1
                if v < 4 * RING:
                    if ch and v == 0:
                        pe.wait_ge(ada_ready, after(pe, ada_ready))
                    pe_ada_panel(pe, ADA_FIRST + 4 * ch + v // RING, v % RING, ADA_BANK, v // RING)
                elif v == 4 * RING + 5:
                    pe_ada_turn(pe, ADA_BANK, 4)

            pe.wait_ge(scan_in, after(pe, scan_in))
            pe.wait_ge(ada_ready, after(pe, ada_ready))
            for ch in range(NCH):
                def tok(t, c, r):
                    return t[r, c * S + ch * CHUNK:c * S + (ch + 1) * CHUNK]

                def sq(t, c, r):
                    return t[r, c * DH:(c + 1) * DH]

                for k, (l, r_) in enumerate(((RW_B, RW_P), (RW_P, RW_B), (RW_C, RW_P), (RW_B, RW_Q), (RW_C, RW_Q))):
                    if ch and k == 2:
                        pe.wait_ge(state_ready, after(pe, state_ready, 2))
                    for c, r in heads:
                        mm = pe.matmul(sq(bank[k], c, r), tok(l, c, r), tok(r_, c, r), start=True, stop=True)
                    mm.then_inc(gram_ready, 1)
                for k, t in enumerate((V, RW_B, RW_C)):
                    if k == 2:
                        pe.wait_ge(turned_taken, after(pe, turned_taken))
                    for c, r in heads:
                        mm = pe.matmul(sq(bank[5 + k % 2], c, r), tok(t, c, r), const("ident")[r, r], start=True, stop=True)
                    mm.then_inc(turned_ready, 1)
                fill()
                pe.wait_ge(turned_taken, after(pe, turned_taken, 2))
                pe.wait_ge(gram_taken, after(pe, gram_taken, 5))
                for c, r in heads:
                    if ch:
                        pe.matmul(sq(bank[3], c, r), tok(RW_P, c, r), sq(STATE, c, r), start=True, stop=False)
                    mm = pe.matmul(sq(bank[3], c, r), sq(GCP, c, r), sq(VT, c, r), start=not ch, stop=True)
                mm.then_inc(rhs_ready, 1)
                for lv in range(1, 6):
                    for h in range(2):
                        fill()
                        pe.wait_ge(inv_taken, after(pe, inv_taken))
                        if lv == 1 and h == 1:
                            pe.wait_ge(rhs_taken, after(pe, rhs_taken))
                        for c, r in halves[h]:
                            mm = pe.matmul(sq(INV_BANKS[h][0], c, r), sq(LOFF, c, r), sq(IY, c, r), start=True, stop=True)
                        mm.then_inc(inv_half, 1)
                    for h in range(2):
                        fill()
                        pe.wait_ge(inv_half_taken, after(pe, inv_half_taken))
                        for c, r in halves[h]:
                            mm = pe.matmul(sq(INV_BANKS[h][1], c, r), sq(IX, c, r), sq(IT, c, r), start=True, stop=True)
                            if lv < 5:
                                mm = pe.matmul(sq(INV_BANKS[h][2], c, r), sq(IT, c, r), sq(IX, c, r), start=True, stop=True)
                        mm.then_inc(inv_off, 1)
                for h in range(2):
                    fill()
                    pe.wait_ge(inv_taken, after(pe, inv_taken))
                    for c, r in halves[h]:
                        mm = pe.matmul(sq(INV_BANKS[h][0], c, r), sq(IY, c, r), sq(RHS, c, r), start=True, stop=True)
                    mm.then_inc(sol_ready, 1)
                for h in range(2):
                    fill()
                    pe.wait_ge(sol_taken, after(pe, sol_taken))
                    for c, r in halves[h]:
                        o = sq(OUT_BANKS[h], c, r)
                        if ch:
                            pe.matmul(o, sq(STATE, c, r), tok(RW_Q, c, r), start=True, stop=False)
                        pe.matmul(o, sq(VT, c, r), sq(GCQ, c, r), start=not ch, stop=False)
                        mm = pe.matmul(o, sq(SOL, c, r), sq(GBQ, c, r), start=False, stop=True)
                    if ch < NCH - 1:
                        for c, r in halves[h]:
                            o = sq(STATE_BANKS[h], c, r)
                            pe.matmul(o, sq(CT, c, r), sq(VT, c, r), start=True, stop=False)
                            mm = pe.matmul(o, sq(BT, c, r), sq(SOL, c, r), start=False, stop=True)
                    mm.then_inc(chunk_out, 1)
            assert visits[0] == NCH * VISITS
            pe.wait_ge(ada_ready, after(pe, ada_ready))

        def pe_rwkv(pe, layer):
            parts = lora_parts(layer)
            pe_norm(pe)
            pe_panels(pe, f"rw{layer}.r")
            pe.wait_ge(lora_landed, after(pe, lora_landed, 16 * (9 if layer else 7)))
            pe_lora(pe, parts[0], first=True)
            pe_panels(pe, f"rw{layer}.k")
            pe_lora(pe, parts[1])
            pe_panels(pe, f"rw{layer}.v")
            for part in parts[2:]:
                pe_lora(pe, part)
            pe.wait_ge(lora_taken, after(pe, lora_taken, 4))
            pe_heads(pe, const("headones"), RW_D)
            pe_heads(pe, const("headones"), RW_D)
            pe_ada_start(pe, layer)
            pe_scan(pe, layer)
            pe_heads(pe, const("headones"), RW_Y)
            pe_heads(pe, const("headones"), RW_D)
            pe_panels(pe, f"rw{layer}.out")

        def dve_scan(dve, layer):
            def masked(dst, src, mask):
                return dve.tensor_tensor(dst.rearrange("p (c t) -> p c t", t=DH), src.rearrange("p (c t) -> p c t", t=DH),
                                         const(mask).unsqueeze(1).to_broadcast([P, dst.shape[1] // DH, DH]), ALU.mult)

            def eye_minus(t):
                v = t.rearrange("p (c t) -> p c t", t=DH)
                return dve.scalar_tensor_tensor(v, v, -1.0, const("eye64").unsqueeze(1).to_broadcast([P, C, DH]),
                                                ALU.mult, ALU.add)

            wend = WEND[:, :].rearrange("p (c n) -> p c n", n=NCH)
            for ch in range(NCH):
                for k, (dst, mask) in enumerate(((N_, "before"), (L_, "below"), (GCP, "before"), (GBQ, "upto"), (GCQ, "upto"))):
                    dve.wait_ge(gram_ready, after(dve, gram_ready))
                    masked(dst, bank[k][:, :], mask).then_inc(gram_taken, 1)
                    dve.wait_ge(gram_taken, after(dve, gram_taken))
                masked(IY, N_, "upper0")
                masked(IX, L_, "lower0").then_inc(dve_step, 1)
                dve.wait_ge(dve_step, after(dve, dve_step))
                eye_minus(IY).then_inc(dve_step, 1)
                dve.wait_ge(dve_step, after(dve, dve_step))
                eye_minus(IX)
                for h in HALF:
                    masked(LOFF[:, h], L_[:, h], "lower1").then_inc(inv_taken, 1)
                dve.wait_ge(inv_taken, after(dve, inv_taken, 2))
                for lv in range(1, 6):
                    for h, banks in zip(HALF, INV_BANKS):
                        dve.wait_ge(inv_off, after(dve, inv_off))
                        last = dve.tensor_tensor(IY[:, h], IY[:, h], banks[1][:, h], ALU.subtract)
                        if lv < 5:
                            dve.tensor_tensor(IX[:, h], IX[:, h], banks[2][:, h], ALU.subtract)
                            last = masked(LOFF[:, h], L_[:, h], f"lower{lv + 1}")
                        last.then_inc(inv_taken, 1)
                        dve.wait_ge(inv_taken, after(dve, inv_taken))
                for k, h in enumerate(HALF):
                    dve.wait_ge(chunk_out, after(dve, chunk_out))
                    cs = slice(k * C // 2, (k + 1) * C // 2)
                    y = dve.tensor_copy(v3(RW_Y)[:, cs, ch * CHUNK:(ch + 1) * CHUNK],
                                        OUT_BANKS[k][:, h].rearrange("p (c t) -> p c t", t=CHUNK))
                    if ch == NCH - 1:
                        continue
                    src = STATE_BANKS[k][:, h]
                    if ch:
                        dve.tensor_tensor(STATE[:, h], STATE[:, h], src, ALU.add).then_inc(dve_step, 1)
                        dve.wait_ge(dve_step, after(dve, dve_step))
                        src = STATE[:, h]
                    dve.tensor_tensor(STATE[:, h].rearrange("p (c t) -> p c t", t=DH), src.rearrange("p (c t) -> p c t", t=DH),
                                      wend[:, cs, ch:ch + 1].to_broadcast([P, C // 2, DH]), ALU.mult).then_inc(state_ready, 1)
                    dve.wait_ge(state_ready, after(dve, state_ready))
            y.then_inc(head_in, 1)
            dve.wait_ge(head_in, after(dve, head_in))

        def dve_rwkv(dve, layer):
            j = layer // 3
            V = rw_values(layer)
            dve_norm(dve, X, lambda c: vec("norm_mix", layer, c), RW_H, to_operand=False)
            h, d = v3(RW_H), v3(RW_D)
            dve.tensor_scalar(d[:, :, 0:1], h[:, :, 0:1], -1.0, None, ALU.mult)
            dve.tensor_tensor(d[:, :, 1:S], h[:, :, 0:S - 1], h[:, :, 1:S], ALU.subtract).then_inc(dve_step, 1)
            dve.wait_ge(dve_step, after(dve, dve_step))

            def mixed(k, dst):
                for c in range(C):
                    cs = slice(c * S, (c + 1) * S)
                    op = dve.scalar_tensor_tensor(dst[:, cs], RW_D[:, cs], vec("rw_mix", 6 * j + k, c), RW_H[:, cs],
                                                  ALU.mult, ALU.add)
                return op

            mixed(0, RW_XA).then_inc(dve_step, 1)
            dve.wait_ge(dve_step, after(dve, dve_step))
            split(dve, RW_XA)
            mixed(3, RW_XB).then_inc(lora_in, 1)
            dve.wait_ge(lora_in, after(dve, lora_in))
            mixed(1, RW_XA).then_inc(dve_step, 1)
            dve.wait_ge(dve_step, after(dve, dve_step))
            dve_tiles(dve, f"rw{layer}.r", take_copy(dve, RW_R))
            split(dve, RW_XA)
            dve.wait_ge(lora_mid, after(dve, lora_mid))
            mixed(4, RW_XB).then_inc(lora_in, 1)
            dve.wait_ge(lora_in, after(dve, lora_in))
            op = mixed(2, RW_XA)
            if layer:
                op.then_inc(lora_in, 1)
                dve.wait_ge(lora_in, after(dve, lora_in))
            else:
                op.then_inc(dve_step, 1)
                dve.wait_ge(dve_step, after(dve, dve_step))
            dve_tiles(dve, f"rw{layer}.k", take_copy(dve, RW_K))
            split(dve, RW_XA)
            dve.wait_ge(lora_mid, after(dve, lora_mid))
            mixed(5, RW_XB).then_inc(lora_in, 1)
            dve.wait_ge(lora_in, after(dve, lora_in))
            dve_tiles(dve, f"rw{layer}.v", take_copy(dve, V))
            dve.wait_ge(lora_taken, after(dve, lora_taken, 16))
            if layer:
                dve.wait_ge(lora_mid, after(dve, lora_mid))
                dve.wait_ge(lora_taken, after(dve, lora_taken, 8))
                dve.tensor_tensor(RW_D[:, :], VF[:, :], V[:, :], ALU.subtract).then_inc(dve_step, 1)
                dve.wait_ge(dve_step, after(dve, dve_step))
                dve.tensor_tensor(RW_D[:, :], RW_D[:, :], RW_XA[:, :], ALU.mult).then_inc(dve_step, 1)
                dve.wait_ge(dve_step, after(dve, dve_step))
                dve.tensor_tensor(V[:, :], V[:, :], RW_D[:, :], ALU.add)
            kk, b = RW_P, RW_B
            dve.tensor_tensor(v3(kk), v3(RW_K), vec_b("rw_k_k", j), ALU.mult).then_inc(dve_step, 1)
            dve.wait_ge(dve_step, after(dve, dve_step))
            dve.tensor_tensor(b[:, :], kk[:, :], kk[:, :], ALU.mult).then_inc(head_in, 1)
            dve.wait_ge(head_in, after(dve, head_in))
            t = RW_BONUS
            dve.scalar_tensor_tensor(v3(t), v3(RW_A), -1.0, vec_b("rw_k_a", j), ALU.add, ALU.mult).then_inc(dve_step, 1)
            dve.wait_ge(dve_step, after(dve, dve_step))
            dve.scalar_tensor_tensor(RW_K[:, :], t[:, :], 1.0, RW_K[:, :], ALU.add, ALU.mult).then_inc(dve_step, 1)
            dve.wait_ge(dve_step, after(dve, dve_step))
            dve_heads(dve, lambda s, ps: dve.tensor_scalar(t[:, s], ps, KK_MIN, None, ALU.max)).then_inc(head_taken, 1)
            dve.wait_ge(head_taken, after(dve, head_taken))
            dve.wait_ge(lora_mid, after(dve, lora_mid))
            for c in range(C):
                cs = slice(c * S, (c + 1) * S)
                op = dve.tensor_tensor_scan(RW_XB[:, cs], const("carry"), RW_CUM[:, cs], 0.0, ALU.mult, ALU.add)
            op.then_inc(decay_ready, 1)
            dve.wait_ge(decay_ready, after(dve, decay_ready))
            dve.tensor_tensor(b[:, :], RW_R[:, :], RW_K[:, :], ALU.mult).then_inc(dve_step, 1)
            dve.wait_ge(dve_step, after(dve, dve_step))
            dve.tensor_tensor(v3(b), v3(b), vec_b("rw_r_k", j), ALU.mult).then_inc(head_in, 1)
            dve.wait_ge(head_in, after(dve, head_in))
            dve.wait_ge(root_ready, after(dve, root_ready))
            dve.tensor_tensor(kk[:, :], kk[:, :], t[:, :], ALU.mult).then_inc(dve_step, 1)
            dve.wait_ge(dve_step, after(dve, dve_step))
            dve_heads(dve, lambda s, ps: dve.tensor_tensor(t[:, s], ps, V[:, s], ALU.mult))
            dve.tensor_tensor(b[:, :], kk[:, :], RW_A[:, :], ALU.mult).then_inc(dve_step, 1)
            dve.wait_ge(dve_step, after(dve, dve_step))
            dve.wait_ge(exp_ready, after(dve, exp_ready))
            g64 = [x[:, :].rearrange("p (g t) -> p g t", t=CHUNK) for x in (kk, RW_CUM)]
            dve.tensor_tensor(g64[0][:, :, 1:CHUNK], g64[0][:, :, 1:CHUNK], g64[1][:, :, 0:CHUNK - 1], ALU.mult)
            dve.tensor_copy(WEND[:, :].unsqueeze(2), g64[1][:, :, CHUNK - 1:CHUNK])
            dve.tensor_tensor(RW_Q[:, :], RW_R[:, :], RW_CUM[:, :], ALU.mult)
            dve.wait_ge(exp_ready, after(dve, exp_ready))
            dve.tensor_tensor(RW_C[:, :], RW_K[:, :], RW_XB[:, :], ALU.mult)
            dve.tensor_tensor(b[:, :], b[:, :], RW_XB[:, :], ALU.mult).then_inc(scan_in, 1)
            dve.wait_ge(scan_in, after(dve, scan_in))
            dve_scan(dve, layer)
            y, yc = RW_Y, RW_P
            dve_heads(dve, lambda s, ps: dve.scalar_tensor_tensor(
                yc[:, s], ps, -1.0 / DH, y[:, s], ALU.mult, ALU.add)).then_inc(dve_step, 1)
            dve.wait_ge(dve_step, after(dve, dve_step))
            dve.tensor_tensor(b[:, :], yc[:, :], yc[:, :], ALU.mult).then_inc(head_in, 1)
            dve.wait_ge(head_in, after(dve, head_in))
            dve_heads(dve, lambda s, ps: dve.tensor_scalar(y[:, s], ps, 1.0 / DH, GN_EPS, ALU.mult, ALU.add)).then_inc(head_taken, 1)
            dve.wait_ge(head_taken, after(dve, head_taken))
            dve.wait_ge(root_ready, after(dve, root_ready))
            dve.tensor_tensor(yc[:, :], yc[:, :], y[:, :], ALU.mult).then_inc(dve_step, 1)
            dve.wait_ge(dve_step, after(dve, dve_step))
            dve.wait_ge(lora_taken, after(dve, lora_taken, 8))
            for c in range(C):
                cs = slice(c * S, (c + 1) * S)
                op = dve.scalar_tensor_tensor(yc[:, cs], yc[:, cs], vec("rw_ln_w", j, c), RW_BONUS[:, cs], ALU.mult, ALU.add)
            op.then_inc(dve_step, 1)
            dve.wait_ge(dve_step, after(dve, dve_step))
            for c in range(C):
                cs = slice(c * S, (c + 1) * S)
                op = dve.scalar_tensor_tensor(yc[:, cs], yc[:, cs], vec("rw_ln_b", j, c), RW_G[:, cs], ALU.add, ALU.mult)
            op.then_inc(dve_step, 1)
            dve.wait_ge(dve_step, after(dve, dve_step))
            split(dve, yc)
            dve_tiles(dve, f"rw{layer}.out", take_residual(dve, X))

        Q_, K_, VT_, O_ = W[3], W[4], W[5], W[6]
        HS = TT * S

        def slots(t, n=4):
            return [t[:, k * HS:(k + 1) * HS] for k in range(n)]

        SB_AT = [sum(S - j * P for j in range(st)) for st in range(TT + 1)]
        SB_N = SB_AT[TT]

        def sb_slot(t, k):
            return t[:, k * HS:k * HS + SB_N]

        SB_SP = [sb_slot(W[0], k) for k in range(4)]
        SB_MASKED = [sb_slot(W[1], k) for k in range(4)]
        SB_LOG = [sb_slot(t, k) for t in (W[2], W[7]) for k in range(4)]
        SB_BANK = (4, 5, 2, 3)

        def head_rows(hd):
            return slice(DH * (hd % 2), DH * (hd % 2) + DH), hd // 2

        def pe_sb(pe):
            pe_norm(pe)
            for n in "qkv":
                pe_panels(pe, f"sb.{n}", fills=0, chunked=n == "q")
            pe.wait_ge(bank_free, tiles_of("sb.v"))

            def scores(hd):
                r, c = head_rows(hd)
                if hd >= 4:
                    pe.wait_ge(logit_ready, after(pe, logit_ready))
                for st in range(TT):
                    mm = pe.matmul(bank[SB_BANK[hd % 4]][:, SB_AT[st]:SB_AT[st + 1]], K_[r, c * S + st * P:c * S + (st + 1) * P],
                                   Q_[r, c * S + st * P:(c + 1) * S], start=True, stop=True)
                mm.then_inc(z_ready, 1)

            def later(hd):
                pe.wait_ge(later_in, after(pe, later_in))
                m, o = SB_MASKED[hd % 4], bank[6 + hd % 2]
                for st in range(TT):
                    for qt in range(st, TT):
                        for kt in range(st, qt + 1):
                            at = [SB_AT[x] + (qt - x) * P for x in (st, kt)]
                            mm = pe.matmul(o[:, at[0]:at[0] + P], const("after") if kt == st else ones[:, :],
                                           m[:, at[1]:at[1] + P], start=kt == st, stop=kt == qt)
                mm.then_inc(later_ready, 1)

            def output(hd):
                r, c = head_rows(hd)
                pe.wait_ge(att_ready, after(pe, att_ready))
                if hd % 2 == 0 and hd >= 4:
                    pe.wait_ge(heads_taken, after(pe, heads_taken))
                for qt in range(TT):
                    for st in range(qt + 1):
                        at = SB_AT[st] + (qt - st) * P
                        mm = pe.matmul(bank[c % 2][r, qt * P:(qt + 1) * P], VT_[:, st * D + hd * DH:st * D + (hd + 1) * DH],
                                       SB_LOG[hd % 8][:, at:at + P], start=st == 0, stop=st == qt)
                if hd % 2:
                    mm.then_inc(heads_out, 1)

            pairs = [(hd, hd + 1) for hd in range(0, H, 2)]
            for hd in pairs[0]:
                scores(hd)
            for g, pair_ in enumerate(pairs):
                if g + 1 < len(pairs):
                    for hd in pairs[g + 1]:
                        scores(hd)
                else:
                    pe.wait_ge(logit_ready, after(pe, logit_ready, 2))
                for hd in pair_:
                    later(hd)
                if g:
                    for hd in pairs[g - 1]:
                        output(hd)
            for hd in pairs[-1]:
                output(hd)
            pe.wait_ge(logit_ready, after(pe, logit_ready, 2))
            pe.wait_ge(heads_taken, after(pe, heads_taken, 2))
            pe_panels(pe, "sb.out")

        def act_sb(act):
            act_norm(act, X, W[0])
            for n in "qkv":
                act_panels(act, f"sb.{n}")

            pairs = [(hd, hd + 1) for hd in range(0, H, 2)]

            def softplus(pair_):
                for hd in pair_:
                    act.wait_ge(z_ready, after(act, z_ready))
                    act.activation(SB_SP[hd % 4], bank[SB_BANK[hd % 4]][:, 0:SB_N], ACT.Abs).then_inc(act_step, 1)
                for hd in pair_:
                    act.wait_ge(act_step, after(act, act_step))
                    act.activation(SB_SP[hd % 4], SB_SP[hd % 4], ACT.Exp, scale=-1.0).then_inc(act_step, 1)
                for hd in pair_:
                    act.wait_ge(act_step, after(act, act_step))
                    act.activation(SB_SP[hd % 4], SB_SP[hd % 4], ACT.Ln, bias=1.0).then_inc(exps_ready, 1)

            softplus(pairs[0])
            for g, pair_ in enumerate(pairs):
                if g + 1 < len(pairs):
                    softplus(pairs[g + 1])
                for hd in pair_:
                    act.wait_ge(logit_ready, after(act, logit_ready))
                    act.activation(SB_LOG[hd % 8], SB_LOG[hd % 8], ACT.Exp).then_inc(att_raw, 1)
            act.wait_ge(later_in, after(act, later_in, H))
            act.wait_ge(heads_out, after(act, heads_out, H // 2))
            act_panels(act, "sb.out")

        def dve_sb(dve, layer):
            dve_norm(dve, X, lambda c: vec("norm_mix", layer, c), W[0])
            dve_tiles(dve, "sb.q", take_copy(dve, Q_, DH ** -0.5))
            dve_tiles(dve, "sb.k", take_copy(dve, K_))
            dve_tiles(dve, "sb.v", take_tokens(dve, VT_[:, :].rearrange("p (a m) -> p a m", m=D)))

            def masked(hd):
                b = hd % 4
                dve.wait_ge(exps_ready, after(dve, exps_ready))
                ps = bank[SB_BANK[b]][:, 0:SB_N]
                dve.scalar_tensor_tensor(SB_SP[b], ps, 0.0, SB_SP[b], ALU.max, ALU.add).then_inc(dve_step, 1)
                dve.wait_ge(dve_step, after(dve, dve_step))
                dve.tensor_tensor(SB_MASKED[b], SB_SP[b], const("earlier"), ALU.mult).then_inc(later_in, 1)
                dve.tensor_tensor(SB_LOG[hd % 8], ps, SB_SP[b], ALU.subtract).then_inc(dve_step, 1)
                dve.wait_ge(dve_step, after(dve, dve_step))
                dve.wait_ge(later_in, after(dve, later_in))

            def logits(hd):
                dve.wait_ge(later_ready, after(dve, later_ready))
                o = SB_LOG[hd % 8]
                dve.tensor_tensor(o, o, bank[6 + hd % 2][:, 0:SB_N], ALU.subtract).then_inc(logit_ready, 1)

            def weights(hd):
                dve.wait_ge(att_raw, after(dve, att_raw))
                o = SB_LOG[hd % 8]
                dve.tensor_tensor(o, o, const("earlier"), ALU.mult).then_inc(att_ready, 1)

            def store(pair_):
                dve.wait_ge(heads_out, after(dve, heads_out))
                c = pair_[0] // 2
                dve.tensor_copy(O_[:, c * S:(c + 1) * S], bank[c % 2][:, 0:S]).then_inc(heads_taken, 1)

            pairs = [(hd, hd + 1) for hd in range(0, H, 2)]
            for hd in pairs[0]:
                masked(hd)
            for g, pair_ in enumerate(pairs):
                for hd in pair_:
                    logits(hd)
                if g + 1 < len(pairs):
                    for hd in pairs[g + 1]:
                        masked(hd)
                for hd in pair_:
                    weights(hd)
                if g:
                    store(pairs[g - 1])
            store(pairs[-1])
            dve.wait_ge(logit_ready, after(dve, logit_ready, H))
            dve.wait_ge(att_ready, after(dve, att_ready, H))
            dve.wait_ge(heads_taken, after(dve, heads_taken, H // 2))
            split(dve, O_)
            dve_tiles(dve, "sb.out", take_residual(dve, X))

        DS_QI, DS_T = W[5], W[6]
        DS_Q, DS_K, DS_V, DS_O = W[1], W[2], W[3], W[4]
        kiw = sb("kiw", C * P, at=l_at)
        wiw = sb("wiw", C * IDX_H, at=l_at + C * P * 4)
        WI = sb("WI", TT * IDX_H)
        SC, SC2, SEL = W[7][:, 0:HS], W[7][:, HS:2 * HS], W[7][:, 2 * HS:3 * HS]
        IDX = [W[8][:, k * HS:(k + 1) * HS] for k in range(2)]
        best = sb("best", TT * 8)
        DS_L = slots(W[0])[0:2] + [SC, SC2]
        DS_PT = slots(W[0])[2:4]
        top = sb("top", 4 * 2 * TT)
        DS_COLS = 3 * D + IDX_H * DH

        def sp_ds_small(sp):
            w = a["ds_w_in"][0]
            for k in range(2):
                sp.dma_start(
                    kiw[:, :].rearrange("p (c m) -> p c m", m=P)[:, :, k * DH:(k + 1) * DH],
                    w[:, DS_COLS:DS_COLS + DH].rearrange("(c p) m -> p c m", p=P)).then_inc(small_landed, 16)
            sp.dma_start(wiw[:, :].rearrange("p (c m) -> p c m", m=IDX_H),
                                         w[:, DS_COLS + DH:DS_COLS + DH + IDX_H].rearrange("(c p) m -> p c m", p=P)).then_inc(small_landed, 16)

        def pe_ds(pe):
            pe_norm(pe)
            pe_panels(pe, "ds.q", chunked=True)
            pe.wait_ge(small_landed, after(pe, small_landed, 48))
            for c in range(C):
                mm = pe.matmul(bank[4][:, 0:S], kiw[:, c * P:(c + 1) * P], W[0][:, c * S:(c + 1) * S],
                               start=c == 0, stop=c == C - 1)
            mm.then_inc(small_ready, 1)
            for tt in range(TT):
                for c in range(C):
                    mm = pe.matmul(bank[5][:, tt * IDX_H:(tt + 1) * IDX_H], W[0][:, c * S + tt * P:c * S + (tt + 1) * P],
                                   wiw[:, c * IDX_H:(c + 1) * IDX_H], start=c == 0, stop=c == C - 1)
            mm.then_inc(small_ready, 1)
            pe_panels(pe, "ds.qi", fills=0)

            def index(hd):
                r, c = head_rows(hd)
                if hd >= 2:
                    pe.wait_ge(idx_act, after(pe, idx_act))
                for qt in range(TT):
                    mm = pe.matmul(bank[4 + hd % 2][:, qt * S:(qt + 1) * S],
                                   DS_QI[r, c * S + qt * P:c * S + (qt + 1) * P], DS_QI[r, 4 * S:5 * S],
                                   start=True, stop=True)
                mm.then_inc(idx_ready, 1)

            between = {0: lambda: pe_heads(pe, const("rot_head"), DS_QI, chunks=5),
                       3: lambda: pe_heads(pe, const("headones"), DS_T),
                       6: lambda: pe_heads(pe, const("rot_head"), DS_Q)}
            tile = pe_panels(pe, "ds.k", fills=0, by_hand=True)
            for st in range(C):
                tile(st)
                if st in between:
                    between[st]()
            tile = pe_panels(pe, "ds.v", fills=0, by_hand=True)
            for st in range(G["ds.v"].steps):
                tile(st)
                if st == 0:
                    pe_heads(pe, const("headones"), DS_T)
                elif st == 2:
                    pe_heads(pe, const("rot_head"), DS_K)
            pe.wait_ge(head_in, after(pe, head_in))
            for hd in range(IDX_H):
                index(hd)
            pe.wait_ge(idx_act, after(pe, idx_act, 2))
            pe.wait_ge(bank_free, tiles_of("ds.v"))

            def scores(hd):
                r, c = head_rows(hd)
                if hd >= 2:
                    pe.wait_ge(logit_ready, after(pe, logit_ready))
                for qt in range(TT):
                    mm = pe.matmul(bank[4 + hd % 2][:, qt * S:(qt + 1) * S], DS_Q[r, c * S + qt * P:c * S + (qt + 1) * P],
                                   DS_K[r, c * S:(c + 1) * S], start=True, stop=True)
                mm.then_inc(ds_z_ready, 1)

            def turn(hd):
                pe.wait_ge(att_ready, after(pe, att_ready))
                for qt in range(TT):
                    for st in range(TT):
                        mm = pe.transpose(bank[6 + hd % 2][:, st * S + qt * P:st * S + (qt + 1) * P],
                                          DS_L[hd % 4][:, qt * S + st * P:qt * S + (st + 1) * P], const("ident"))
                mm.then_inc(att_turned, 1)

            def output(hd):
                r, c = head_rows(hd)
                pe.wait_ge(att_turned_taken, after(pe, att_turned_taken))
                if hd % 2 == 0 and hd >= 4:
                    pe.wait_ge(heads_taken, after(pe, heads_taken))
                for st in range(TT):
                    mm = pe.matmul(bank[c % 2][r, 0:S], DS_V[:, st * D + hd * DH:st * D + (hd + 1) * DH],
                                   DS_PT[hd % 2][:, st * S:(st + 1) * S], start=st == 0, stop=st == TT - 1)
                mm.then_inc(heads_out, 1)

            scores(0)
            scores(1)
            for hd in range(H):
                if hd + 2 < H:
                    scores(hd + 2)
                turn(hd)
                if hd:
                    output(hd - 1)
            output(H - 1)
            pe.wait_ge(logit_ready, after(pe, logit_ready, 2))
            pe.wait_ge(heads_taken, after(pe, heads_taken, 2))
            pe_panels(pe, "ds.out")

        def act_ds(act):
            act_norm(act, X, W[0])
            act_panels(act, "ds.q")
            act_panels(act, "ds.qi")

            def inverse_norms():
                act.wait_ge(head_taken, after(act, head_taken))
                act_inverse_root(act, DS_T[:, :])

            def index(n):
                act.wait_ge(idx_ready, after(act, idx_ready))
                if n >= 2:
                    act.wait_ge(idx_taken, after(act, idx_taken))
                act.activation(IDX[n % 2], bank[4 + n % 2][:, :], ACT.Relu).then_inc(idx_act, 1)

            tile = act_panels(act, "ds.k", by_hand=True)
            for st in range(C):
                tile(st)
                if st == 3:
                    inverse_norms()
            tile = act_panels(act, "ds.v", by_hand=True)
            for st in range(G["ds.v"].steps):
                tile(st)
                if st == 0:
                    inverse_norms()
            for hd in range(IDX_H):
                index(hd)
            act.wait_ge(idx_taken, after(act, idx_taken, 2))

            def powers(hd):
                b = hd % 4
                act.wait_ge(logit_ready, after(act, logit_ready))
                for qt in range(TT):
                    l = DS_L[b][:, qt * S:(qt + 1) * S]
                    op = act.activation(l, l, ACT.Exp, bias=top[:, 4 * b + qt:4 * b + qt + 1],
                                        accum_out=top[:, 4 * b + 2 + qt:4 * b + 3 + qt])
                op.then_inc(exps_ready, 1)

            def turned(hd):
                act.wait_ge(att_turned, after(act, att_turned))
                if hd >= 2:
                    act.wait_ge(heads_out, after(act, heads_out))
                act.activation(DS_PT[hd % 2], bank[6 + hd % 2][:, :], ACT.Copy).then_inc(att_turned_taken, 1)

            powers(0)
            powers(1)
            for hd in range(H):
                turned(hd)
                if hd + 2 < H:
                    powers(hd + 2)
            act.wait_ge(heads_out, after(act, heads_out, 2))
            act_panels(act, "ds.out")

        def dve_ds(dve, layer):
            dve_norm(dve, X, lambda c: vec("norm_mix", layer, c), W[0])
            dve_tiles(dve, "ds.q", take_copy(dve, DS_Q))
            dve.wait_ge(small_ready, after(dve, small_ready))
            dve.tensor_copy(DS_QI[:, 4 * S:5 * S], bank[4][:, 0:S])
            dve.wait_ge(small_ready, after(dve, small_ready))
            dve.tensor_scalar(WI[:, :], bank[5][:, 0:TT * IDX_H], IDX_H ** -0.5 * DH ** -0.5, None, ALU.mult)
            dve_tiles(dve, "ds.qi", take_copy(dve, DS_QI))
            dve.memset(SC, 0.0).then_inc(head_in, 1)
            dve.wait_ge(head_in, after(dve, head_in))

            def rope(t, chunks=C):
                n = chunks * S

                def over(name, k):
                    return const(name).unsqueeze(1).to_broadcast([P, k, S])

                def times_sin(s, ps):
                    k = (s.stop - s.start) // S
                    return dve.tensor_tensor(DS_T[:, s].rearrange("p (c t) -> p c t", t=S),
                                             ps.rearrange("p (c t) -> p c t", t=S), over("sin_head", k), ALU.mult)
                dve_heads(dve, times_sin, chunks)
                v = v3(t)[:, 0:chunks]
                dve.tensor_tensor(v, v, over("cos_head", chunks), ALU.mult).then_inc(dve_step, 1)
                dve.wait_ge(dve_step, after(dve, dve_step))
                return dve.tensor_tensor(t[:, 0:n], t[:, 0:n], DS_T[:, 0:n], ALU.add)

            def squares(t):
                dve.tensor_tensor(DS_T[:, :], t[:, :], t[:, :], ALU.mult).then_inc(head_in, 1)
                dve.wait_ge(head_in, after(dve, head_in))

            def mean_squares():
                dve_heads(dve, lambda s, ps: dve.tensor_scalar(DS_T[:, s], ps, 1.0 / DH, EPS, ALU.mult, ALU.add)).then_inc(head_taken, 1)
                dve.wait_ge(head_taken, after(dve, head_taken))

            def normed(k, t):
                dve.wait_ge(root_ready, after(dve, root_ready))
                dve.scalar_tensor_tensor(t[:, :], t[:, :], VEC3[:, k:k + 1], DS_T[:, :], ALU.mult, ALU.mult).then_inc(head_in, 1)
                dve.wait_ge(head_in, after(dve, head_in))

            def rotated(t, chunks=C, signal=dve_step):
                rope(t, chunks).then_inc(signal, 1)
                dve.wait_ge(signal, after(dve, signal))

            def index(hd):
                dve.wait_ge(idx_act, after(dve, idx_act))
                for qt in range(TT):
                    o = SC[:, qt * S:(qt + 1) * S]
                    op = dve.scalar_tensor_tensor(o, IDX[hd % 2][:, qt * S:(qt + 1) * S],
                                                  WI[:, qt * IDX_H + hd:qt * IDX_H + hd + 1], o, ALU.mult, ALU.add)
                op.then_inc(idx_taken, 1)
                dve.wait_ge(idx_taken, after(dve, idx_taken))

            tile = dve_tiles(dve, "ds.k", take_copy(dve, DS_K), by_hand=True)
            for st in range(C):
                tile(st)
                if st == 0:
                    rotated(DS_QI, 5)
                    squares(DS_Q)
                elif st == 3:
                    mean_squares()
                elif st == 5:
                    normed(0, DS_Q)
            dve.wait_ge(bank_free, tiles_of("ds.k"))
            rotated(DS_Q)
            squares(DS_K)
            tile = dve_tiles(dve, "ds.v", take_tokens(dve, DS_V[:, :].rearrange("p (a m) -> p a m", m=D)), by_hand=True)
            for st in range(G["ds.v"].steps):
                tile(st)
                if st == 0:
                    mean_squares()
                elif st == 1:
                    normed(1, DS_K)
                elif st == 2:
                    rotated(DS_K, signal=head_in)
            for hd in range(IDX_H):
                index(hd)
            for qt in range(TT):
                for hh in range(2):
                    seen = qt * P + (hh + 1) * CHUNK
                    if seen < S:
                        op = dve.memset(SC[hh * DH:(hh + 1) * DH, qt * S + seen:(qt + 1) * S], NEG)
            op.then_inc(dve_step, 1)
            dve.wait_ge(dve_step, after(dve, dve_step))
            dve.tensor_copy(SC2, SC).then_inc(dve_step, 1)
            dve.wait_ge(dve_step, after(dve, dve_step))
            for n in range(TOPK // 8):
                for qt in range(TT):
                    op = dve.max(best[:, qt * 8:(qt + 1) * 8], SC2[:, qt * S:(qt + 1) * S])
                op.then_inc(dve_step, 1)
                dve.wait_ge(dve_step, after(dve, dve_step))
                for qt in range(TT):
                    o = SC2[:, qt * S:(qt + 1) * S]
                    op = dve.match_replace(o, best[:, qt * 8:(qt + 1) * 8], o, TAKEN)
                op.then_inc(dve_step, 1)
                dve.wait_ge(dve_step, after(dve, dve_step))
            dve.tensor_tensor(SEL, SC2, SC, ALU.is_equal).then_inc(dve_step, 1)
            dve.wait_ge(dve_step, after(dve, dve_step))
            dve.tensor_scalar(SEL, SEL, HIDE, None, ALU.mult).then_inc(dve_step, 1)
            dve.wait_ge(dve_step, after(dve, dve_step))

            def logits(hd):
                b = hd % 4
                dve.wait_ge(ds_z_ready, after(dve, ds_z_ready))
                if hd >= 4:
                    dve.wait_ge(att_turned, after(dve, att_turned))
                l = DS_L[b]
                dve.scalar_tensor_tensor(l, bank[4 + hd % 2][:, :], DH ** -0.5, SEL, ALU.mult, ALU.add).then_inc(dve_step, 1)
                dve.wait_ge(dve_step, after(dve, dve_step))
                t = top[:, 4 * b:4 * b + 2]
                dve.tensor_reduce(t, l.rearrange("p (a s) -> p a s", s=S), AX_X, ALU.max).then_inc(dve_step, 1)
                dve.wait_ge(dve_step, after(dve, dve_step))
                dve.tensor_scalar(t, t, -1.0, None, ALU.mult).then_inc(logit_ready, 1)
                dve.wait_ge(logit_ready, after(dve, logit_ready))

            def weights(hd):
                b = hd % 4
                dve.wait_ge(exps_ready, after(dve, exps_ready))
                t = top[:, 4 * b + 2:4 * b + 4]
                dve.reciprocal(t, t).then_inc(dve_step, 1)
                dve.wait_ge(dve_step, after(dve, dve_step))
                for qt in range(TT):
                    l = DS_L[b][:, qt * S:(qt + 1) * S]
                    op = dve.tensor_scalar(l, l, t[:, qt:qt + 1], None, ALU.mult)
                op.then_inc(att_ready, 1)
                dve.wait_ge(att_ready, after(dve, att_ready))

            def store(hd):
                dve.wait_ge(heads_out, after(dve, heads_out, 2))
                c = hd // 2
                dve.tensor_copy(DS_O[:, c * S:(c + 1) * S], bank[c % 2][:, 0:S]).then_inc(heads_taken, 1)
                dve.wait_ge(heads_taken, after(dve, heads_taken))

            logits(0)
            logits(1)
            for hd in range(H):
                weights(hd)
                if hd + 2 < H:
                    logits(hd + 2)
                if hd % 2 == 0 and hd:
                    store(hd - 1)
            store(H - 1)
            dve.wait_ge(att_turned, after(dve, att_turned, 4))
            split(dve, DS_O)
            dve_tiles(dve, "ds.out", take_residual(dve, X))

        ROWS, ROWS2, ROWS3, XROWS = W[0], W[1][:, 0:CF_W], W[1][:, CF_W:CF_W + P], W[2]
        OUTROWS = W[2]

        def table_view(name):
            t = a[name]
            if name == "rw_mix":
                return t.rearrange("a b d -> (a b) d")
            if name == "rw_r_k":
                return t.rearrange("a h d -> a (h d)")
            if name == "b_ada_2":
                return t.rearrange("l (n d) -> (l n) d", d=D)
            if name in ("norm_g_2", "conv_a_w_2", "conf_dw_2"):
                return t.rearrange("l k d -> (l k) d")
            if name in ("c_ctx_2", "final_g_2"):
                return t.rearrange("(a d) -> a d", a=1)
            return t

        def sp_setup(sp):
            sp.dma_start(cst[:, :], a["const"]).then_inc(const_landed, 16)
            sp.dma_start(XROWS[:, :].rearrange("p (a d) -> p a d", d=D),
                                          a["x"][0].rearrange("(a p) d -> p a d", p=P)).then_inc(x_rows_landed, 16)
            for name, at, k in VEC_ROWS:
                sp.dma_start(ROWS[at:at + k, 0:D], table_view(name)).then_inc(rows_landed, 16)
            for name, at, k in VEC2_ROWS:
                sp.dma_start(ROWS2[at:at + k, :], table_view(name)).then_inc(rows_landed, 16)
            for half in range(2):
                o = slice(half * DH, half * DH + DH)
                sp.dma_start(ROWS3[0:1, o], a["ds_q_norm"]).then_inc(rows_landed, 16)
                sp.dma_start(ROWS3[1:2, o], a["ds_k_norm"]).then_inc(rows_landed, 16)
                sp.dma_start(ROWS3[2:10, o], a["lam_p_2"].rearrange("l k d -> (l k) d")).then_inc(rows_landed, 16)
            sp.dma_start(ROWS3[10:12, :], a["subln_g_2"]).then_inc(rows_landed, 16)

        N_TABLES = len(VEC_ROWS) + len(VEC2_ROWS) + 7

        def pe_turn_in(pe, src):
            for k in range(4):
                for c in (2 * k, 2 * k + 1):
                    for tt in range(TT):
                        o = (c % 2) * S + tt * P
                        mm = pe.transpose(bank[k][:, o:o + P], src[:, tt * D + c * P:tt * D + (c + 1) * P], const("ident"))
                mm.then_inc(x_turned, 1)

        def pe_setup(pe):
            pe.wait_ge(const_landed, after(pe, const_landed, 16))
            pe.wait_ge(x_rows_landed, after(pe, x_rows_landed, 16))
            pe_turn_in(pe, XROWS)
            pe.wait_ge(rows_landed, after(pe, rows_landed, 16 * N_TABLES))
            for c in range(C):
                mm = pe.transpose(bank[4][:, c * NV:(c + 1) * NV], ROWS[0:NV, c * P:(c + 1) * P], const("ident")[0:NV, 0:NV])
            mm.then_inc(vec_turned, 1)
            for c in range(2):
                pe.transpose(bank[5][:, c * NV2:(c + 1) * NV2], ROWS2[0:NV2, c * P:(c + 1) * P], const("ident")[0:NV2, 0:NV2])
            pe.transpose(bank[5][:, 2 * NV2:2 * NV2 + 12], ROWS3[0:12, :], const("ident")[0:12, 0:12]).then_inc(vec_turned, 1)
            pe.wait_ge(consts_set, after(pe, consts_set))

        def dve_turn_in(dve, dst):
            for k in range(4):
                dve.wait_ge(x_turned, after(dve, x_turned))
                dve.tensor_copy(dst[:, k * 2 * S:(k + 1) * 2 * S], bank[k][:, :]).then_inc(x_ready, 1)
                dve.wait_ge(x_ready, after(dve, x_ready))

        def dve_setup(dve):
            dve.memset(eps[:, 0:1], EPS)
            dve.memset(cond[:, :], 0.0)
            dve.memset(ones[:, :], 1.0).then_inc(consts_set, 1)
            dve.wait_ge(consts_set, after(dve, consts_set))
            dve_turn_in(dve, X)
            dve.wait_ge(vec_turned, after(dve, vec_turned))
            dve.tensor_copy(VEC[:, :], bank[4][:, 0:C * NV]).then_inc(vec_ready, 1)
            dve.wait_ge(vec_ready, after(dve, vec_ready))
            dve.wait_ge(vec_turned, after(dve, vec_turned))
            dve.tensor_copy(VEC2[:, :], bank[5][:, 0:2 * NV2])
            dve.tensor_copy(VEC3[:, :], bank[5][:, 2 * NV2:2 * NV2 + 12]).then_inc(vec_ready, 1)
            dve.wait_ge(vec_ready, after(dve, vec_ready))

        def act_input(act):
            act.wait_ge(consts_set, after(act, consts_set))
            act.wait_ge(vec_ready, after(act, vec_ready, 2))
            act.wait_ge(x_ready, after(act, x_ready, 4))

        def pe_turn_out(pe, src):
            pe.wait_ge(turn_in, after(pe, turn_in))
            for k in range(4):
                tt, half = k // 2, k % 2
                for q in range(4):
                    c = half * 4 + q
                    mm = pe.transpose(bank[k][:, q * P:(q + 1) * P], src[:, c * S + tt * P:c * S + (tt + 1) * P], const("ident"))
                mm.then_inc(turned_out, 1)

        def dve_turn_out(dve):
            for k in range(4):
                dve.wait_ge(turned_out, after(dve, turned_out))
                dve.tensor_copy(OUTROWS[:, k * 512:(k + 1) * 512], bank[k][:, :]).then_inc(out_ready, 1)
                dve.wait_ge(out_ready, after(dve, out_ready))

        def sp_out(sp):
            for tt in range(TT):
                sp.wait_ge(out_ready, after(sp, out_ready, 2))
                sp.dma_start(out[0, tt * P:(tt + 1) * P, :], OUTROWS[:, tt * D:(tt + 1) * D]).then_inc(out_landed, 16)
            sp.wait_ge(out_landed, after(sp, out_landed, 16 * TT))

        STREAM = {"x": X, "c": CTX}
        MOD = {s: sb(f"mod_{s}", N_MOD * C) for s in "xc"}
        GAIN = {s: sb(f"gain_{s}", 3 * C) for s in "xc"}
        LAM = sb("LAM", 8)
        lam_init = [0.8 - 0.6 * float(np.exp(-0.3 * l)) for l in range(D2)]

        def act_cond(act):
            for n, name in enumerate(("c_2", "c_ctx_2")):
                op = act.activation(cond[:, :].rearrange("p (c n) -> p c n", n=32)[:, :, n:n + 1],
                                    VEC_v[:, :, VAT[name]:VAT[name] + 1], ACT.Silu)
            op.then_inc(cond_ready, 1)

        def act_ada(act):
            act.wait_ge(lam_sums, after(act, lam_sums))
            act.activation(LAM[:, 0:2], bank[5][:, 0:2], ACT.Exp).then_inc(lam_exp, 1)

        def pe_ada(pe):
            pe.wait_ge(lam_in, after(pe, lam_in))
            pe.matmul(bank[5][:, 0:2], const("headones"), LAM[:, 2:4], start=True, stop=True).then_inc(lam_sums, 1)

        def dve_ada(dve, l):
            dve.wait_ge(ada_ready, (1 + NCH) * (l + 1))
            b4 = both[l][:, :].rearrange("p (n c s) -> p n c s", c=C, s=2)
            row = VAT["b_ada_2"] + l * N_MOD
            bias = VEC_v[:, :, row:row + N_MOD].rearrange("p c n -> p n c")
            for k, s in enumerate("xc"):
                m = MOD[s][:, :]
                dve.tensor_tensor(m.rearrange("p (n c) -> p n c", c=C), b4[:, :, :, k], bias, ALU.add).then_inc(dve_step, 1)
                dve.wait_ge(dve_step, after(dve, dve_step))
                for n in range(3):
                    g = VAT["norm_g_2"] + 3 * l + n
                    dve.scalar_tensor_tensor(
                        GAIN[s][:, n * C:(n + 1) * C], m[:, (3 * n + 1) * C:(3 * n + 2) * C], 1.0,
                        VEC_v[:, :, g], ALU.add, ALU.mult).then_inc(dve_step, 1)
                    dve.wait_ge(dve_step, after(dve, dve_step))
                for n in (0, 2):
                    o = m[:, (3 * n + 2) * C:(3 * n + 3) * C]
                    dve.tensor_scalar(o, o, 0.5, None, ALU.mult).then_inc(dve_step, 1)
                    dve.wait_ge(dve_step, after(dve, dve_step))
            v = VEC3[:, 2 + 4 * l:6 + 4 * l].rearrange("p (a b) -> p a b", b=2)
            dve.tensor_tensor(LAM[:, 2:4], v[:, :, 0], v[:, :, 1], ALU.mult).then_inc(lam_in, 1)
            dve.wait_ge(lam_in, after(dve, lam_in))
            dve.wait_ge(lam_exp, after(dve, lam_exp))
            dve.tensor_tensor(LAM[:, 4:5], LAM[:, 1:2], LAM[:, 0:1], ALU.subtract).then_inc(dve_step, 1)
            dve.wait_ge(dve_step, after(dve, dve_step))
            dve.tensor_scalar(LAM[:, 5:6], LAM[:, 4:5], -lam_init[l], None, ALU.add).then_inc(dve_step, 1)
            dve.wait_ge(dve_step, after(dve, dve_step))

        def mod(s, n):
            return lambda c: MOD[s][:, n * C + c:n * C + c + 1]

        def mod_gate(s, n):
            return MOD[s][:, n * C:(n + 1) * C]

        def gain(s, n):
            return lambda c: GAIN[s][:, n * C + c:n * C + c + 1]

        def dve_ffn2(dve, name, s, n):
            dve_ffn(dve, name, STREAM[s], gain(s, n), mod(s, 3 * n), mod_gate(s, 3 * n + 2))

        AB = sb("AB", 10 * S, at=w_at[0])
        D_ = W[2][:, 0:4 * S]
        LN_SQ = W[2][:, 4 * S:6 * S]
        LN_STD = W[2][:, 6 * S:7 * S]
        MERGED = W[3]
        DQ, DK = W[4][:, 0:4 * S], W[4][:, 4 * S:8 * S]
        KC, VC = VF[:, 0:4 * S], VF[:, 4 * S:8 * S]
        DV, DO = W[5][:, 0:4 * S], W[5][:, 4 * S:8 * S]
        DP = [[W[6][:, (2 * b + m) * HS:(2 * b + m + 1) * HS] for m in range(2)] for b in range(2)]
        DAT = [W[7][:, b * HS:(b + 1) * HS] for b in range(2)]
        da_top = sb("da_top", 8)
        T2 = W[7][:, 2 * HS:4 * HS]
        V_TOK = W[8][:, 0:HS]
        SGW, SGWT = W[8][:, HS:2 * HS], W[8][:, 2 * HS:3 * HS]
        SGB = W[8][:, 3 * HS:3 * HS + 2 * P]
        PADW = S + CF_K - 1
        PAD = AB[:, 0:2 * PADW]

        def v2vec(name, row, c):
            o = V2AT[name] + row
            return VEC2_v[:, c, o:o + 1]

        def sp_gated_unit(sp, l):
            sp.wait_ge(sgu_free, after(sp, sgu_free))
            sp.dma_start(SGW.rearrange("p (g q) -> p g q", q=P),
                                       a["sgu_w_2"][l].rearrange("g p q -> p g q")).then_inc(sgu_landed, 16)
            for g in range(SG_G):
                sp.dma_start(SGB[DH * (g % 2):DH * (g % 2) + DH, (g // 2) * P:(g // 2 + 1) * P],
                                           a["sgu_b_2"][l, g].partition_broadcast(DH)).then_inc(sgu_landed, 16)

        def keys_of(s):
            return [(DK, DV), (KC, VC)] if s == "x" else [(KC, VC)]

        def pe_total(pe, src, chunks=2):
            pe.wait_ge(head_in, after(pe, head_in))
            for c in range(chunks):
                mm = pe.matmul(bank[4][:, 0:S], ones[:, :], src[:, c * S:(c + 1) * S], start=c == 0, stop=c == chunks - 1)
            mm.then_inc(head_sums, 1)

        def dve_layer_norm(dve, t):
            def centre():
                dve.wait_ge(head_sums, after(dve, head_sums))
                for c in range(2):
                    o = t[:, c * S:(c + 1) * S]
                    op = dve.scalar_tensor_tensor(o, bank[4][:, 0:S], -1.0 / CF_W, o, ALU.mult, ALU.add)
                op.then_inc(dve_step, 1)
                dve.wait_ge(dve_step, after(dve, dve_step))
                dve.tensor_tensor(LN_SQ, t, t, ALU.mult).then_inc(head_in, 1)
                dve.wait_ge(head_in, after(dve, head_in))

            def variance():
                dve.wait_ge(head_sums, after(dve, head_sums))
                dve.tensor_scalar(LN_STD, bank[4][:, 0:S], 1.0 / CF_W, EPS, ALU.mult, ALU.add).then_inc(head_taken, 1)
                dve.wait_ge(head_taken, after(dve, head_taken))

            def divide():
                dve.wait_ge(root_ready, after(dve, root_ready))
                dve.reciprocal(LN_STD, LN_STD).then_inc(dve_step, 1)
                dve.wait_ge(dve_step, after(dve, dve_step))
                v = t.rearrange("p (c t) -> p c t", t=S)
                return dve.tensor_tensor(v, v, LN_STD.unsqueeze(1).to_broadcast([P, 2, S]), ALU.mult)
            return centre, variance, divide

        def act_root(act, t):
            act.wait_ge(head_taken, after(act, head_taken))
            act.activation(t, t, ACT.Sqrt).then_inc(root_ready, 1)

        UNITS = [(h, qt) for h in range(DA_H) for qt in range(TT)]

        def pe_diff(pe, s):
            parts = keys_of(s)
            nkt = TT * len(parts)

            def scores(u):
                h, qt = UNITS[u]
                if u:
                    pe.wait_ge(da_exp, after(pe, da_exp))
                for m in range(2):
                    r = slice(DA_D * m, DA_D * m + DA_D)
                    for k, (keys, _) in enumerate(parts):
                        mm = pe.matmul(bank[4 + m][:, k * S:(k + 1) * S], DQ[r, h * S + qt * P:h * S + (qt + 1) * P],
                                       keys[r, h * S:(h + 1) * S], start=True, stop=True)
                mm.then_inc(da_scores, 1)

            def turn(u):
                pe.wait_ge(da_mix, after(pe, da_mix))
                for kt in range(nkt):
                    mm = pe.transpose(bank[6][:, kt * P:(kt + 1) * P], DP[u % 2][0][:, kt * P:(kt + 1) * P], const("ident"))
                mm.then_inc(da_turned, 1)

            def output(u):
                h, qt = UNITS[u]
                pe.wait_ge(da_copied, after(pe, da_copied))
                if u:
                    pe.wait_ge(da_stored, after(pe, da_stored))
                for kt in range(nkt):
                    v = parts[kt // TT][1]
                    o = (kt % TT) * DA_W + h * P
                    mm = pe.matmul(bank[7][:, 0:P], v[:, o:o + P], DAT[u % 2][:, kt * P:(kt + 1) * P],
                                   start=kt == 0, stop=kt == nkt - 1)
                mm.then_inc(da_out, 1)
            return scores, turn, output

        def act_diff(act, s):
            nk = S * len(keys_of(s))

            def powers(u):
                b = u % 2
                act.wait_ge(da_max, after(act, da_max))
                for m in range(2):
                    op = act.activation(DP[b][m][:, 0:nk], bank[4 + m][:, 0:nk], ACT.Exp, scale=DA_D ** -0.5,
                                        bias=da_top[:, 4 * b + m:4 * b + m + 1],
                                        accum_out=da_top[:, 4 * b + 2 + m:4 * b + 3 + m])
                op.then_inc(da_exp, 1)

            def copied(u):
                act.wait_ge(da_turned, after(act, da_turned))
                if u >= 2:
                    act.wait_ge(da_out, after(act, da_out))
                act.activation(DAT[u % 2][:, 0:nk], bank[6][:, 0:nk], ACT.Copy).then_inc(da_copied, 1)
            return powers, copied

        def dve_diff(dve, s):
            nk = S * len(keys_of(s))

            def maxima(u):
                b = u % 2
                dve.wait_ge(da_scores, after(dve, da_scores))
                t = da_top[:, 4 * b:4 * b + 2]
                for m in range(2):
                    op = dve.tensor_reduce(t[:, m:m + 1], bank[4 + m][:, 0:nk], AX_X, ALU.max)
                op.then_inc(dve_step, 1)
                dve.wait_ge(dve_step, after(dve, dve_step))
                dve.tensor_scalar(t, t, -(DA_D ** -0.5), None, ALU.mult).then_inc(da_max, 1)
                dve.wait_ge(da_max, after(dve, da_max))

            def mix(u):
                b = u % 2
                dve.wait_ge(da_exp, after(dve, da_exp))
                t = da_top[:, 4 * b + 2:4 * b + 4]
                dve.reciprocal(t, t).then_inc(dve_step, 1)
                dve.wait_ge(dve_step, after(dve, dve_step))
                dve.tensor_scalar(t[:, 1:2], t[:, 1:2], LAM[:, 5:6], None, ALU.mult).then_inc(dve_step, 1)
                p0, p1 = (x[:, 0:nk] for x in DP[b])
                dve.tensor_scalar(p0, p0, t[:, 0:1], None, ALU.mult).then_inc(dve_step, 1)
                dve.wait_ge(dve_step, after(dve, dve_step, 2))
                dve.scalar_tensor_tensor(p0, p1, t[:, 1:2], p0, ALU.mult, ALU.add).then_inc(da_mix, 1)
                dve.wait_ge(da_mix, after(dve, da_mix))

            def store(u):
                h, qt = UNITS[u]
                dve.wait_ge(da_out, after(dve, da_out))
                dve.tensor_copy(DO[:, h * S + qt * P:h * S + (qt + 1) * P], bank[7][:, 0:P]).then_inc(da_stored, 1)
                dve.wait_ge(da_stored, after(dve, da_stored))
            return maxima, mix, store

        def branch_parts(b):
            c0, width = BRANCH[b]
            return tuple(t[:, c0 * S:c0 * S + width // P * S] for t in (BRH, BRL))

        NU = len(UNITS)

        def pe_mix(pe, l, s):
            pre = f"mix{l}{s}"
            pe_norm(pe)
            pe_panels(pe, f"{pre}.k", chunked=True)
            if (l, s) not in FULL:
                pe_panels(pe, f"{pre}.v", fills=0)
                return
            pe_panels(pe, f"{pre}.q", fills=0)
            pe_panels(pe, f"{pre}.v", fills=0)
            if s == "x":
                pe_heads(pe, const("rot_axial"), DQ, chunks=4)
                pe_heads(pe, const("rot_axial"), DK, chunks=4, first=6)
            pe_panels(pe, f"{pre}.ab", fills=0)
            pe_panels(pe, f"{pre}.d", fills=0)

            def turn_weights():
                pe.wait_ge(sgu_landed, after(pe, sgu_landed, 16 * (1 + SG_G)))
                for g in range(SG_G):
                    mm = pe.transpose(bank[5][:, g * P:(g + 1) * P], SGW[:, g * P:(g + 1) * P], const("ident"))
                mm.then_inc(sgu_turned, 1)

            def turn_v():
                pe.wait_ge(head_in, after(pe, head_in))
                for tt in range(TT):
                    for c in range(2):
                        mm = pe.transpose(bank[6][:, tt * S + c * P:tt * S + (c + 1) * P],
                                          AB[:, (8 + c) * S + tt * P:(8 + c) * S + (tt + 1) * P], const("ident"))
                mm.then_inc(sgu_turned, 1)

            def mix_tokens():
                pe.wait_ge(sgu_copied, after(pe, sgu_copied, 2))
                for g in range(SG_G):
                    for tt in range(TT):
                        mm = pe.matmul(bank[4 + 3 * (g // 2)][DH * (g % 2):DH * (g % 2) + DH, tt * P:(tt + 1) * P],
                                       V_TOK[:, tt * SG_W + g * DH:tt * SG_W + (g + 1) * DH], SGWT[:, g * P:(g + 1) * P],
                                       start=True, stop=True)
                mm.then_inc(sgu_out, 1)

            between = {0: lambda: pe_total(pe, AB[:, 8 * S:10 * S]),
                       1: lambda: pe_total(pe, LN_SQ),
                       3: turn_weights, 4: turn_v, 6: mix_tokens}
            tile = pe_panels(pe, f"{pre}.aout", by_hand=True)
            for st in range(C):
                tile(st)
                if st in between:
                    between[st]()
            tile = pe_panels(pe, f"{pre}.bout", by_hand=True)
            scores, turn, output = pe_diff(pe, s)
            scores(0)
            for u in range(NU):
                tile(u)
                if u:
                    output(u - 1)
                turn(u)
                if u + 1 < NU:
                    scores(u + 1)
            pe.wait_ge(da_exp, after(pe, da_exp))
            pe_total(pe, D_)
            output(NU - 1)
            pe_total(pe, LN_SQ)
            pe_heads(pe, ones[:, :], W[6], chunks=4, first=5)
            pe.wait_ge(da_stored, after(pe, da_stored))
            pe_panels(pe, f"{pre}.dout")
            pe_panels(pe, f"{pre}.cout")
            pe_panels(pe, f"{pre}.o")

        def act_mix(act, l, s):
            pre = f"mix{l}{s}"
            act_norm(act, STREAM[s], W[7], mod(s, 3))
            act_panels(act, f"{pre}.k")
            if (l, s) not in FULL:
                act_panels(act, f"{pre}.v")
                return
            for n in ("q", "v", "ab"):
                act_panels(act, f"{pre}.{n}")
            act.wait_ge(bank_free, tiles_of(f"{pre}.ab"))
            t = AB[:, 6 * S:10 * S]
            act.activation(t, t, ACT.Gelu_apprx_tanh).then_inc(glu_ready, 1)
            act_panels(act, f"{pre}.d")
            act.wait_ge(bank_free, tiles_of(f"{pre}.d"))
            t = D_[:, 2 * S:4 * S]
            act.activation(t, t, ACT.Sigmoid).then_inc(glu_ready, 1)

            def gated(b, by_hand=False):
                g = G[f"{pre}.{b}out"]

                def gate(st, j, k):
                    if k == 1:
                        n = after(act, merged_step)
                        if n is not None:
                            act.wait_ge(merged_step, n)
                        act.activation(silu[j % 2][:, :], bank[(g.t0 + j * g.tiles + 1) % RING][:, 0:S],
                                       ACT.Sigmoid).then_inc(silu_ready, 1)
                gate.per = {merged_step: 2}
                return act_panels(act, g.name, gate, by_hand=by_hand)

            def copy_weights():
                act.wait_ge(sgu_turned, after(act, sgu_turned))
                act.activation(SGWT, bank[5][:, :], ACT.Copy).then_inc(sgu_copied, 1)

            def copy_v():
                act.wait_ge(sgu_turned, after(act, sgu_turned))
                act.activation(V_TOK, bank[6][:, :], ACT.Copy).then_inc(sgu_copied, 1)

            between = {1: lambda: act_root(act, LN_STD), 3: copy_weights, 4: copy_v}
            tile = gated("a", by_hand=True)
            for st in range(C):
                tile(st)
                if st in between:
                    between[st]()
            tile = gated("b", by_hand=True)
            powers, copied = act_diff(act, s)
            powers(0)
            for u in range(NU):
                tile(u)
                copied(u)
                if u + 1 < NU:
                    powers(u + 1)
            act_root(act, LN_STD)
            act.wait_ge(da_out, after(act, da_out, 2))
            act_root(act, W[6][:, 0:4 * S])
            act.wait_ge(conf_ready, after(act, conf_ready))
            for c in range(2):
                o = D_[:, c * S:(c + 1) * S]
                op = act.activation(o, o, ACT.Silu, scale=v2vec("conf_ln_g_2", l, c), bias=v2vec("conf_ln_b_2", l, c))
            op.then_inc(conf_act, 1)
            gated("d")
            gated("c")
            act_panels(act, f"{pre}.o")

        def dve_rope(dve, t, first):
            def over(name, k):
                return const(name).unsqueeze(1).to_broadcast([P, k, S])

            rot = W[6][:, 0:4 * S]

            def times_sin(c, ps):
                return dve.tensor_tensor(rot[:, c].rearrange("p (c t) -> p c t", t=S),
                                         ps.rearrange("p (c t) -> p c t", t=S), over("sin_axial", 2), ALU.mult)
            dve_heads(dve, times_sin, 4, first)
            v = t.rearrange("p (c t) -> p c t", t=S)
            dve.tensor_tensor(v, v, over("cos_axial", 4), ALU.mult).then_inc(dve_step, 1)
            dve.wait_ge(dve_step, after(dve, dve_step))
            dve.tensor_tensor(t, t, rot, ALU.add).then_inc(dve_step, 1)
            dve.wait_ge(dve_step, after(dve, dve_step))

        def dve_mix(dve, l, s):
            pre = f"mix{l}{s}"
            k_dst, v_dst = (KC, VC) if s == "c" else (DK, DV)
            dve_norm(dve, STREAM[s], gain(s, 1), W[7], mod(s, 3))
            full = (l, s) in FULL
            if full:
                dve.memset(LAM[:, 6:7], 0.0).then_inc(sgu_free, 1)
                dve.wait_ge(sgu_free, after(dve, sgu_free))
            dve_tiles(dve, f"{pre}.k", take_copy(dve, k_dst))
            if full:
                dve_tiles(dve, f"{pre}.q", take_copy(dve, DQ))
                if s == "x":
                    for _ in range(2):
                        dve.memset(da_top[:, 0:1], 0.0).then_inc(head_in, 1)
                        dve.wait_ge(head_in, after(dve, head_in))
            dve_tiles(dve, f"{pre}.v", take_tokens(dve, v_dst.rearrange("p (a m) -> p a m", m=DA_W)))
            if not full:
                return
            if s == "x":
                dve_rope(dve, DQ, 4)
                dve_rope(dve, DK, 6)
            dve_tiles(dve, f"{pre}.ab", take_copy(dve, AB))
            bg, cg, xin = (AB[:, 2 * k * S:2 * (k + 1) * S] for k in range(3))
            y = T2[:, 0:2 * S]
            dve.tensor_tensor(xin, cg, xin, ALU.mult).then_inc(dve_step, 1)
            dve.wait_ge(dve_step, after(dve, dve_step))
            taps = [[v2vec("conv_a_w_2", CA_K * l + k, c) for k in range(CA_K)] for c in range(2)]
            ins = [xin[:, c * S:(c + 1) * S] for c in range(2)]
            outs = [y[:, c * S:(c + 1) * S] for c in range(2)]
            for i, o, w in zip(ins, outs, taps):
                op = dve.tensor_scalar(o, i, w[1], None, ALU.mult)
            op.then_inc(dve_step, 1)
            dve.wait_ge(dve_step, after(dve, dve_step))
            for i, o, w in zip(ins, outs, taps):
                op = dve.scalar_tensor_tensor(o[:, 1:S], i[:, 0:S - 1], w[0], o[:, 1:S], ALU.mult, ALU.add)
            op.then_inc(dve_step, 1)
            dve.wait_ge(dve_step, after(dve, dve_step))
            for i, o, w in zip(ins, outs, taps):
                op = dve.scalar_tensor_tensor(o[:, 0:S - 1], i[:, 1:S], w[2], o[:, 0:S - 1], ALU.mult, ALU.add)
            op.then_inc(dve_step, 1)
            dve.wait_ge(dve_step, after(dve, dve_step))
            dve.tensor_tensor(y, y, bg, ALU.mult).then_inc(dve_step, 1)
            dve.wait_ge(dve_step, after(dve, dve_step))
            split(dve, y, branch_parts("a"))
            dve_tiles(dve, f"{pre}.d", take_copy(dve, D_))

            def merged(b, by_hand=False):
                def take(st, j, banks):
                    dve.wait_ge(silu_ready, after(dve, silu_ready))
                    o = MERGED[:, st * S:(st + 1) * S] if isinstance(st, int) else MERGED[:, bass.ds(st * S, S)]
                    if b == MERGE_ORDER[0]:
                        dve.tensor_tensor(o, silu[j % 2][:, :], banks[0][:, 0:S], ALU.mult).then_inc(bank_free, 2)
                        dve.wait_ge(bank_free, after(dve, bank_free, 2))
                        dve.memset(hid[:, 0:2], 0.0).then_inc(merged_step, 1)
                        dve.wait_ge(merged_step, after(dve, merged_step))
                    else:
                        dve.tensor_tensor(hid[:, :], silu[j % 2][:, :], banks[0][:, 0:S], ALU.mult).then_inc(bank_free, 2)
                        dve.wait_ge(bank_free, after(dve, bank_free, 2))
                        dve.tensor_tensor(o, o, hid[:, :], ALU.add).then_inc(merged_step, 1)
                        dve.wait_ge(merged_step, after(dve, merged_step))
                name = f"{pre}.{b}out"
                counts.start(dve, bank_free, G[name].t0)
                return dve_tiles(dve, name, take, {silu_ready: 1, bank_free: 2, merged_step: 1}, by_hand)

            dve.wait_ge(glu_ready, after(dve, glu_ready))
            u_, v_ = AB[:, 6 * S:8 * S], AB[:, 8 * S:10 * S]
            dve.memset(da_top[:, 0:1], 0.0).then_inc(head_in, 1)
            dve.wait_ge(head_in, after(dve, head_in))
            centre, variance, divide = dve_layer_norm(dve, v_)

            def normed():
                divide().then_inc(head_in, 1)
                dve.wait_ge(head_in, after(dve, head_in))

            def gated_unit():
                dve.wait_ge(sgu_out, after(dve, sgu_out))
                for k in range(2):
                    op = dve.tensor_tensor(
                        y[:, k * S:(k + 1) * S].rearrange("p (n t) -> p n t", t=P),
                        bank[4 + 3 * k][:, 0:S].rearrange("p (n t) -> p n t", t=P),
                        SGB[:, k * P:(k + 1) * P].unsqueeze(1).to_broadcast([P, TT, P]), ALU.add)
                op.then_inc(dve_step, 1)
                dve.wait_ge(dve_step, after(dve, dve_step))
                dve.tensor_tensor(y, y, u_, ALU.mult).then_inc(dve_step, 1)
                dve.wait_ge(dve_step, after(dve, dve_step))
                split(dve, y, branch_parts("b"))

            pad = PAD.rearrange("p (c t) -> p c t", t=PADW)
            edge = CF_K // 2
            z = D_.rearrange("p (c t) -> p c t", t=S)
            acc = D_[:, 0:2 * S]
            next_tap = [0]

            def padded():
                dve.wait_ge(glu_ready, after(dve, glu_ready))
                dve.memset(pad[:, :, 0:edge], 0.0)
                dve.memset(pad[:, :, edge + S:PADW], 0.0)
                dve.tensor_tensor(pad[:, :, edge:edge + S], z[:, 0:2], z[:, 2:4], ALU.mult).then_inc(dve_step, 1)
                dve.wait_ge(dve_step, after(dve, dve_step))

            def some_taps(n):
                for k in range(next_tap[0], min(CF_K, next_tap[0] + n)):
                    for c in range(2):
                        i, o, w = pad[:, c, k:k + S], acc[:, c * S:(c + 1) * S], v2vec("conf_dw_2", CF_K * l + k, c)
                        if k == 0:
                            op = dve.tensor_scalar(o, i, w, v2vec("conf_db_2", l, c), ALU.mult, ALU.add)
                        else:
                            op = dve.scalar_tensor_tensor(o, i, w, o, ALU.mult, ALU.add)
                    if k < CF_K - 1:
                        op.then_inc(dve_step, 1)
                        dve.wait_ge(dve_step, after(dve, dve_step))
                    else:
                        op.then_inc(head_in, 1)
                        dve.wait_ge(head_in, after(dve, head_in))
                next_tap[0] += n

            between = {0: centre, 1: variance, 2: normed, 6: gated_unit}
            tile = merged("a", by_hand=True)
            for st in range(C):
                tile(st)
                if st in between:
                    between[st]()
                else:
                    if st == 3:
                        padded()
                    some_taps(3)
            maxima, mix, store = dve_diff(dve, s)
            tile = merged("b", by_hand=True)
            maxima(0)
            for u in range(NU):
                mix(u)
                tile(u)
                if u:
                    store(u - 1)
                if u + 1 < NU:
                    maxima(u + 1)
                some_taps(3 if u < NU // 2 else 2)
            assert next_tap[0] >= CF_K
            centre, variance, divide = dve_layer_norm(dve, acc)
            centre()
            store(NU - 1)
            t = W[6][:, 0:4 * S]
            dve.tensor_tensor(t, DO, DO, ALU.mult).then_inc(head_in, 1)
            dve.wait_ge(head_in, after(dve, head_in))
            variance()
            dve_heads(dve, lambda c, ps: dve.tensor_scalar(t[:, c], ps, 1.0 / P, EPS, ALU.mult, ALU.add), 4, 5).then_inc(head_taken, 1)
            dve.wait_ge(head_taken, after(dve, head_taken))
            divide().then_inc(conf_ready, 1)
            dve.wait_ge(conf_ready, after(dve, conf_ready))
            dve.wait_ge(conf_act, after(dve, conf_act))
            split(dve, acc, branch_parts("d"))
            dve.wait_ge(root_ready, after(dve, root_ready))
            dve.reciprocal(t, t).then_inc(dve_step, 1)
            dve.wait_ge(dve_step, after(dve, dve_step))
            dve.tensor_scalar(t, t, 1.0 - lam_init[l], None, ALU.mult).then_inc(dve_step, 1)
            dve.wait_ge(dve_step, after(dve, dve_step))
            dve.scalar_tensor_tensor(DO, DO, VEC3[:, 10 + l:11 + l], t, ALU.mult, ALU.mult).then_inc(dve_step, 1)
            dve.wait_ge(dve_step, after(dve, dve_step))
            split(dve, DO, branch_parts("c"))
            merged("d")
            merged("c")
            split(dve, MERGED)
            dve_tiles(dve, f"{pre}.o", take_residual(dve, STREAM[s], mod_gate(s, 5)))

        CROWS = W[6]

        def sp_ctx(sp):
            sp.dma_start(CROWS[:, :].rearrange("p (a d) -> p a d", d=D),
                                       a["ctx_2"][0].rearrange("(a p) d -> p a d", p=P)).then_inc(ctx_landed, 16)

        def act_second(act):
            act_ada(act)
            act.wait_ge(x_ready, after(act, x_ready, 4))
            act_ffn(act, "f10x", X, mod("x", 0))
            act_ffn(act, "f10c", CTX, mod("c", 0))
            act.wait_ge(bank_free, tiles_of("f10c.down"))
            act_mix(act, 0, "c")
            act.wait_ge(bank_free, tiles_of("mix0c.o"))
            act_ffn(act, "f20c", CTX, mod("c", 6))
            act.wait_ge(bank_free, tiles_of("f20c.down"))
            act_mix(act, 0, "x")
            act.wait_ge(bank_free, tiles_of("mix0x.o"))
            act_ffn(act, "f20x", X, mod("x", 6))
            act_ada(act)
            act_ffn(act, "f11x", X, mod("x", 0))
            act.wait_ge(bank_free, tiles_of("f11x.down"))
            act_ffn(act, "f11c", CTX, mod("c", 0))
            act.wait_ge(bank_free, tiles_of("f11c.down"))
            act_mix(act, 1, "c")
            act_mix(act, 1, "x")
            act.wait_ge(bank_free, tiles_of("mix1x.o"))
            act_ffn(act, "f21x", X, mod("x", 6))
            act.wait_ge(bank_free, tiles_of("f21x.down"))
            act_norm(act, X)

        def pe_second(pe):
            pe.wait_ge(bank_free, tiles_of("ffn3.down"))
            pe.wait_ge(ctx_landed, after(pe, ctx_landed, 16))
            pe_turn_in(pe, CROWS)
            pe.wait_ge(x_ready, after(pe, x_ready, 4))
            pe_ada(pe)
            pe_ffn(pe, "f10x")
            pe_ffn(pe, "f10c")
            pe_mix(pe, 0, "c")
            pe_ffn(pe, "f20c")
            pe_mix(pe, 0, "x")
            pe_ffn(pe, "f20x")
            pe_ada(pe)
            pe_ffn(pe, "f11x")
            pe_ffn(pe, "f11c")
            pe_mix(pe, 1, "c")
            pe_mix(pe, 1, "x")
            pe_ffn(pe, "f21x")
            pe_norm(pe)
            pe.wait_ge(bank_free, tiles_of("f21x.down"))
            pe_turn_out(pe, W[7])

        def dve_second(dve):
            dve_turn_in(dve, CTX)
            dve_ada(dve, 0)
            dve_ffn2(dve, "f10x", "x", 0)
            dve_ffn2(dve, "f10c", "c", 0)
            dve_mix(dve, 0, "c")
            dve_ffn2(dve, "f20c", "c", 2)
            dve_mix(dve, 0, "x")
            dve_ffn2(dve, "f20x", "x", 2)
            dve_ada(dve, 1)
            dve_ffn2(dve, "f11x", "x", 0)
            dve_ffn2(dve, "f11c", "c", 0)
            dve_mix(dve, 1, "c")
            dve_mix(dve, 1, "x")
            dve_ffn2(dve, "f21x", "x", 2)
            dve_norm(dve, X, lambda c: vec("final_g_2", 0, c), W[7], to_operand=False)
            dve.memset(eps[:, 1:2], 0.0).then_inc(turn_in, 1)
            dve.wait_ge(turn_in, after(dve, turn_in))
            dve_turn_out(dve)

        block = ctx.enter_context(nc.Block())
        FIRST = [f"rw{0}", "sb", "ds", f"rw{3}"]

        @block.sync
        def _(sp):
            sp_setup(sp)
            sp_lora(sp, 0)
            for g in order:
                if g.name == "ds.q":
                    sp_ds_small(sp)
                if g.name == "rw3.r":
                    sp_lora(sp, 1)
                if g.name == "f10x.up":
                    sp_ctx(sp)
                if g.name.endswith(".q") and g.name[:5] in [f"mix{l}{s}" for l, s in FULL]:
                    sp_gated_unit(sp, int(g.name[3]))
                if g.direct:
                    sp_direct(sp, g.name)
                else:
                    sp_panels(sp, g.name)
            sp_out(sp)

        @block.gpsimd
        def _(pool):
            for g in order:
                if not g.direct:
                    pool_panels(pool, g.name)

        @block.scalar
        def _(act):
            for q in range(RING):
                act_round(act, order[0], q)
            act_input(act)
            act_cond(act)
            act_rwkv(act, 0)
            act.wait_ge(bank_free, tiles_of("rw0.out"))
            act_ffn(act, "ffn0", X)
            act.wait_ge(bank_free, tiles_of("ffn0.down"))
            act_sb(act)
            act.wait_ge(bank_free, tiles_of("sb.out"))
            act_ffn(act, "ffn1", X)
            act.wait_ge(bank_free, tiles_of("ffn1.down"))
            act_ds(act)
            act.wait_ge(bank_free, tiles_of("ds.out"))
            act_ffn(act, "ffn2", X)
            act.wait_ge(bank_free, tiles_of("ffn2.down"))
            act_rwkv(act, 3)
            act.wait_ge(bank_free, tiles_of("rw3.out"))
            act_ffn(act, "ffn3", X)
            act_second(act)

        @block.tensor
        def _(pe):
            pe_setup(pe)
            pe_rwkv(pe, 0)
            pe_ffn(pe, "ffn0")
            pe_sb(pe)
            pe_ffn(pe, "ffn1")
            pe_ds(pe)
            pe_ffn(pe, "ffn2")
            pe_rwkv(pe, 3)
            pe_ffn(pe, "ffn3")
            pe_second(pe)

        @block.vector
        def _(dve):
            dve_setup(dve)
            dve_rwkv(dve, 0)
            dve_ffn(dve, "ffn0", X, lambda c: vec("norm_ffn", 0, c))
            dve_sb(dve, 1)
            dve_ffn(dve, "ffn1", X, lambda c: vec("norm_ffn", 1, c))
            dve_ds(dve, 2)
            dve_ffn(dve, "ffn2", X, lambda c: vec("norm_ffn", 2, c))
            dve_rwkv(dve, 3)
            dve_ffn(dve, "ffn3", X, lambda c: vec("norm_ffn", 3, c))
            dve_second(dve)


def kernel(**inputs):
    import concourse.bacc as bacc
    from concourse.bass_utils import run_bass_kernel_spmd

    nc = bacc.Bacc("TRN2", target_bir_lowering=False, num_devices=1)
    table, at = constants()
    arrays, views = {}, {}
    for name, value in [*inputs.items(), ("const", table)]:
        array = np.ascontiguousarray(value)
        arrays[f"in_{name}"] = array
        views[name] = nc.dram_tensor(f"in_{name}", array.shape, F32, kind="ExternalInput").ap()
    out = nc.dram_tensor("out", (1, S, D), F32, kind="ExternalOutput").ap()
    build(nc, views, out, at)
    return run_bass_kernel_spmd(nc, [arrays], core_ids=[0]).results[0]["out"]
```
